# Optimizing a Trainium2 kernel written in Bass

```python
import math
import jax, jax.numpy as jnp
from jax import lax
import numpy as np

D_MODEL = 1024
BATCH = 1
SEQ = 512
DEPTH = 2
DEC_BATCH = 1
DEC_SEQ = 32
PAST_LEN = 512

CHUNK = 64
EPS = 1e-6
N_AB = (DEPTH + 1) // 2
N_C = DEPTH // 2
H_A = D_MODEL // 256
DK_A = 128
DV_A = 128
CONV_W = 4
A_QK = H_A * DK_A
A_V = H_A * DV_A
CONV_DIM = 2 * A_QK + A_V
H_B = D_MODEL // 256
HD_B = 128
B_W = H_B * HD_B
FOX_QBLK = 128
HQ_C = D_MODEL // 64
HKV_C = HQ_C // 4
G_C = HQ_C // HKV_C
HD_C = 64
WINDOW = 128
NB_C = WINDOW // CHUNK
H_X = 4
HD_X = 128
MEM_LEN = 256
D_FF = 4 * D_MODEL
AB_IN = CONV_DIM + A_V + 2 * H_A + 3 * B_W + H_B
AB_MIX = A_V + B_W
C_IN = (HQ_C + 2 * HKV_C) * HD_C
C_MIX = HQ_C * HD_C

kernel_name = 'hybrid_stream_gdn_fox_swa_step'

def rmsnorm(x, g):
    xf = x.astype(jnp.float32)
    y = xf * lax.rsqrt(jnp.mean(xf * xf, axis=-1, keepdims=True) + EPS)
    return (y * g.astype(jnp.float32)).astype(x.dtype)

def l2norm(x):
    return x * lax.rsqrt(jnp.sum(x * x, axis=-1, keepdims=True) + EPS)

def causal_conv_silu(u, prev, w):
    L = u.shape[1]
    full = jnp.concatenate([prev.astype(u.dtype), u], axis=1)
    out = full[:, 0:L] * w[0]
    for i in range(1, CONV_W):
        out = out + full[:, i:i + L] * w[i]
    return jax.nn.silu(out), full[:, L:]

def gated_delta_rule(q, k, v, g, beta, s0):
    B, L, H, DK = q.shape
    DV = v.shape[-1]
    C = min(CHUNK, L)
    N = L // C

    def chunks(a):
        return a.reshape(B, N, C, H, a.shape[-1]).transpose(1, 0, 3, 2, 4)

    q = chunks(q * DK ** -0.5)
    k = chunks(k)
    v = chunks(v)
    g = g.reshape(B, N, C, H).transpose(1, 0, 3, 2)
    beta = beta.reshape(B, N, C, H).transpose(1, 0, 3, 2)
    gc = jnp.cumsum(g, axis=-1)
    incl = jnp.tril(jnp.ones((C, C), bool))
    strict = jnp.tril(jnp.ones((C, C), bool), -1)
    decay = jnp.exp(jnp.where(incl, gc[..., :, None] - gc[..., None, :], -jnp.inf))
    kb = k * beta[..., None]
    lmat = jnp.where(strict, jnp.einsum('nbhik,nbhjk->nbhij', kb, k) * decay, 0.0)
    amat = lmat + jnp.eye(C, dtype=jnp.float32)
    rhs = jnp.concatenate([v * beta[..., None], kb * jnp.exp(gc)[..., None]], axis=-1)
    sol = lax.linalg.triangular_solve(amat, rhs, left_side=True, lower=True, unit_diagonal=True)
    u, w = sol[..., :DV], sol[..., DV:]
    attn = jnp.einsum('nbhik,nbhjk->nbhij', q, k) * decay

    def step(S, xs):
        qc, kc, uc, wc, gcc, ac = xs
        v_new = uc - jnp.einsum('bhck,bhkv->bhcv', wc, S)
        o = (jnp.einsum('bhck,bhkv->bhcv', qc * jnp.exp(gcc)[..., None], S)
             + jnp.einsum('bhij,bhjv->bhiv', ac, v_new))
        g_last = gcc[..., -1]
        S = (S * jnp.exp(g_last)[..., None, None]
             + jnp.einsum('bhck,bhcv->bhkv', kc * jnp.exp(g_last[..., None] - gcc)[..., None], v_new))
        return S, o

    S, o = lax.scan(step, s0, (q, k, u, w, gc, attn))
    o = o.transpose(1, 0, 3, 2, 4).reshape(B, L, H, DV)
    return o, S

def fox_attention(q, k, v, logf):
    B, Lq, H, D = q.shape
    Lk = k.shape[1]
    off = Lk - Lq
    F = jnp.cumsum(logf.astype(jnp.float32), axis=1).transpose(0, 2, 1)
    QB = min(FOX_QBLK, Lq)
    nb = Lq // QB
    kpos = jnp.arange(Lk)

    def block(i):
        start = i * QB
        qi = lax.dynamic_slice_in_dim(q, start, QB, axis=1)
        Fq = lax.dynamic_slice_in_dim(F, off + start, QB, axis=2)
        qpos = off + start + jnp.arange(QB)
        s = (jnp.einsum('bqhd,bkhd->bhqk', qi, k).astype(jnp.float32) * D ** -0.5
             + Fq[..., :, None] - F[..., None, :])
        s = jnp.where(kpos[None, :] <= qpos[:, None], s, -jnp.inf)
        p = jax.nn.softmax(s, axis=-1)
        return jnp.einsum('bhqk,bkhd->bqhd', p.astype(v.dtype), v)

    o = lax.map(block, jnp.arange(nb))
    return o.transpose(1, 0, 2, 3, 4).reshape(B, Lq, H, D)

def swa_attend(q, k, v, valid, sinks):
    Cq, KB = q.shape[2], k.shape[2]
    slopes = jnp.exp2(-8.0 * jnp.arange(1, HQ_C + 1, dtype=jnp.float32) / HQ_C).reshape(HKV_C, G_C)
    dist = jnp.abs(jnp.arange(Cq)[:, None] - jnp.arange(KB)[None, :] + WINDOW).astype(jnp.float32)
    s = jnp.einsum('bnqhgd,bnshd->bnhgqs', q, k).astype(jnp.float32) * HD_C ** -0.5
    s = s - slopes[:, :, None, None] * dist
    s = jnp.where(valid[:, None, None, None, :], s, -jnp.inf)
    sink = jnp.broadcast_to(sinks.astype(jnp.float32).reshape(HKV_C, G_C)[:, :, None, None], s.shape[:-1] + (1,))
    p = jax.nn.softmax(jnp.concatenate([s, sink], axis=-1), axis=-1)[..., :-1]
    return jnp.einsum('bnhgqs,bnshd->bnqhgd', p.astype(v.dtype), v)

def ab_mixer(h, conv_prev, s0, past_k, past_v, past_logf,
             w_in, conv_w, a_log, dt_bias, onorm_g, f_bias, w_out):
    B, L, _ = h.shape
    f32 = jnp.float32
    sizes = (CONV_DIM, A_V, H_A, H_A, B_W, B_W, B_W, H_B)
    idx = [sum(sizes[:j]) for j in range(1, len(sizes))]
    qkv_a, z_a, b_a, a_a, q_b, k_b, v_b, f_b = jnp.split(h @ w_in, idx, axis=-1)
    qkv_a, conv_new = causal_conv_silu(qkv_a, conv_prev, conv_w)
    qa, ka, va = jnp.split(qkv_a.astype(f32), [A_QK, 2 * A_QK], axis=-1)
    qa = l2norm(qa.reshape(B, L, H_A, DK_A))
    ka = l2norm(ka.reshape(B, L, H_A, DK_A))
    va = va.reshape(B, L, H_A, DV_A)
    beta = jax.nn.sigmoid(b_a.astype(f32))
    g = -jnp.exp(a_log.astype(f32)) * jax.nn.softplus(a_a.astype(f32) + dt_bias.astype(f32))
    oa, s_new = gated_delta_rule(qa, ka, va, g, beta, s0.astype(f32))
    oa = rmsnorm(oa, onorm_g) * jax.nn.silu(z_a.astype(f32).reshape(B, L, H_A, DV_A))
    oa = oa.reshape(B, L, A_V).astype(h.dtype)
    qb = q_b.reshape(B, L, H_B, HD_B)
    kb = k_b.reshape(B, L, H_B, HD_B)
    vb = v_b.reshape(B, L, H_B, HD_B)
    logf = jax.nn.log_sigmoid(f_b.astype(f32) + f_bias.astype(f32))
    if past_k is None:
        k_all, v_all, lf_all = kb, vb, logf
    else:
        k_all = jnp.concatenate([past_k.astype(kb.dtype), kb], axis=1)
        v_all = jnp.concatenate([past_v.astype(vb.dtype), vb], axis=1)
        lf_all = jnp.concatenate([past_logf.astype(f32), logf], axis=1)
    ob = fox_attention(qb, k_all, v_all, lf_all).reshape(B, L, B_W).astype(h.dtype)
    out = jnp.concatenate([oa, ob], axis=-1) @ w_out
    return out, s_new, conv_new, kb, vb, logf

def c_mixer(h, past_k, past_v, w_in, sinks, w_out):
    B, L, _ = h.shape
    q, k, v = jnp.split(h @ w_in, [HQ_C * HD_C, (HQ_C + HKV_C) * HD_C], axis=-1)
    q = q.reshape(B, L, HKV_C, G_C, HD_C)
    k = k.reshape(B, L, HKV_C, HD_C)
    v = v.reshape(B, L, HKV_C, HD_C)
    if past_k is None:
        N = L // CHUNK
        q_blk = q.reshape(B, N, CHUNK, HKV_C, G_C, HD_C)
        pad = ((0, 0), (WINDOW, 0), (0, 0), (0, 0))
        kc = jnp.pad(k, pad).reshape(B, N + NB_C, CHUNK, HKV_C, HD_C)
        vc = jnp.pad(v, pad).reshape(B, N + NB_C, CHUNK, HKV_C, HD_C)
        k_blk = jnp.concatenate([kc[:, j:j + N] for j in range(NB_C + 1)], axis=2)
        v_blk = jnp.concatenate([vc[:, j:j + N] for j in range(NB_C + 1)], axis=2)
        key_abs = jnp.arange(N)[:, None] * CHUNK - WINDOW + jnp.arange(WINDOW + CHUNK)[None, :]
        valid = key_abs >= 0
        new_k, new_v = k[:, -WINDOW:], v[:, -WINDOW:]
    else:
        q_blk = q[:, None]
        k_blk = jnp.concatenate([past_k.astype(k.dtype), k], axis=1)[:, None]
        v_blk = jnp.concatenate([past_v.astype(v.dtype), v], axis=1)[:, None]
        valid = jnp.ones((1, WINDOW + L), bool)
        new_k, new_v = k, v
    o = swa_attend(q_blk, k_blk, v_blk, valid, sinks).reshape(B, L, C_MIX)
    return o @ w_out, new_k, new_v

def mem_kv(mem, g, w_kv):
    B, M, _ = mem.shape
    mk, mv = jnp.split(rmsnorm(mem, g) @ w_kv, 2, axis=-1)
    return mk.reshape(B, M, H_X, HD_X), mv.reshape(B, M, H_X, HD_X)

def cross_attend(h, mk, mv, wq, wo):
    B, L, _ = h.shape
    q = (h @ wq).reshape(B, L, H_X, HD_X)
    s = jnp.einsum('blhd,bmhd->bhlm', q, mk.astype(q.dtype)).astype(jnp.float32) * HD_X ** -0.5
    p = jax.nn.softmax(s, axis=-1)
    o = jnp.einsum('bhlm,bmhd->blhd', p.astype(h.dtype), mv.astype(h.dtype))
    return o.reshape(B, L, H_X * HD_X) @ wo

def sq_relu_mlp(h, w_up, w_down):
    return jnp.square(jax.nn.relu(h @ w_up)) @ w_down

def setup_inputs(seed: int = 0) -> dict:
    key = jax.random.key(seed)
    ks = iter(jax.random.split(key, 48))
    f32 = jnp.float32

    def nrm(shape, scale=1.0):
        return scale * jax.random.normal(next(ks), shape, f32)

    def gain(shape):
        return 1.0 + 0.02 * jax.random.normal(next(ks), shape, f32)

    dt = jnp.exp(jax.random.uniform(next(ks), (N_AB, H_A), f32, math.log(1e-3), math.log(1e-1)))
    return {
        'x_prompt': nrm((BATCH, SEQ, D_MODEL)),
        'mem_prompt': nrm((BATCH, MEM_LEN, D_MODEL)),
        'x_sample': nrm((DEC_BATCH, DEC_SEQ, D_MODEL)),
        'state_gdn': nrm((N_AB, DEC_BATCH, H_A, DK_A, DV_A), 0.05),
        'state_gdn_conv': nrm((N_AB, DEC_BATCH, CONV_W - 1, CONV_DIM)),
        'cache_fox_k': nrm((N_AB, DEC_BATCH, PAST_LEN, H_B, HD_B)),
        'cache_fox_v': nrm((N_AB, DEC_BATCH, PAST_LEN, H_B, HD_B)),
        'cache_fox_logf': jax.nn.log_sigmoid(3.0 + nrm((N_AB, DEC_BATCH, PAST_LEN, H_B))),
        'cache_swa_k': nrm((N_C, DEC_BATCH, WINDOW, HKV_C, HD_C)),
        'cache_swa_v': nrm((N_C, DEC_BATCH, WINDOW, HKV_C, HD_C)),
        'cache_mem_k': nrm((DEPTH, DEC_BATCH, MEM_LEN, H_X, HD_X)),
        'cache_mem_v': nrm((DEPTH, DEC_BATCH, MEM_LEN, H_X, HD_X)),
        'g_mix': gain((DEPTH, D_MODEL)),
        'w_in_ab': nrm((N_AB, D_MODEL, AB_IN), D_MODEL ** -0.5),
        'conv_w_a': nrm((N_AB, CONV_W, CONV_DIM), CONV_W ** -0.5),
        'a_log_a': jnp.log(jax.random.uniform(next(ks), (N_AB, H_A), f32, 1.0, 16.0)),
        'dt_bias_a': dt + jnp.log(-jnp.expm1(-dt)),
        'onorm_g_a': gain((N_AB, DV_A)),
        'f_bias_b': 3.0 + nrm((N_AB, H_B), 0.5),
        'w_out_ab': nrm((N_AB, AB_MIX, D_MODEL), AB_MIX ** -0.5),
        'w_in_c': nrm((N_C, D_MODEL, C_IN), D_MODEL ** -0.5),
        'sinks_c': nrm((N_C, HQ_C), 0.5),
        'w_out_c': nrm((N_C, C_MIX, D_MODEL), C_MIX ** -0.5),
        'g_mem': gain((DEPTH, D_MODEL)),
        'w_xkv': nrm((DEPTH, D_MODEL, 2 * H_X * HD_X), D_MODEL ** -0.5),
        'g_cross': gain((DEPTH, D_MODEL)),
        'w_xq': nrm((DEPTH, D_MODEL, H_X * HD_X), D_MODEL ** -0.5),
        'w_xo': nrm((DEPTH, H_X * HD_X, D_MODEL), (H_X * HD_X) ** -0.5),
        'g_mlp': gain((DEPTH, D_MODEL)),
        'w_up': nrm((DEPTH, D_MODEL, D_FF), D_MODEL ** -0.5),
        'w_down': nrm((DEPTH, D_FF, D_MODEL), D_FF ** -0.5),
        'g_final': gain((D_MODEL,)),
    }

def reference(x_prompt, mem_prompt, x_sample, state_gdn, state_gdn_conv, cache_fox_k, cache_fox_v,
              cache_fox_logf, cache_swa_k, cache_swa_v, cache_mem_k, cache_mem_v,
              g_mix, w_in_ab, conv_w_a, a_log_a, dt_bias_a, onorm_g_a, f_bias_b, w_out_ab,
              w_in_c, sinks_c, w_out_c, g_mem, w_xkv, g_cross, w_xq, w_xo, g_mlp, w_up, w_down, g_final):
    xp, xs = x_prompt, x_sample
    Bp = xp.shape[0]
    p_s, p_c, p_fk, p_fv, p_fl, p_wk, p_wv, p_mk, p_mv = [], [], [], [], [], [], [], [], []
    s_s, s_c, s_fk, s_fv, s_fl, s_wk, s_wv = [], [], [], [], [], [], []
    for layer in range(DEPTH):
        i = layer // 2
        if layer % 2 == 0:
            wts = (w_in_ab[i], conv_w_a[i], a_log_a[i], dt_bias_a[i], onorm_g_a[i], f_bias_b[i], w_out_ab[i])
            conv0 = jnp.zeros((Bp, CONV_W - 1, CONV_DIM), xp.dtype)
            s0 = jnp.zeros((Bp, H_A, DK_A, DV_A), jnp.float32)
            o, st, cv, fk, fv, fl = ab_mixer(rmsnorm(xp, g_mix[layer]), conv0, s0, None, None, None, *wts)
            xp = xp + o
            p_s.append(st); p_c.append(cv); p_fk.append(fk); p_fv.append(fv); p_fl.append(fl)
            o, st, cv, fk, fv, fl = ab_mixer(rmsnorm(xs, g_mix[layer]), state_gdn_conv[i], state_gdn[i],
                                             cache_fox_k[i], cache_fox_v[i], cache_fox_logf[i], *wts)
            xs = xs + o
            s_s.append(st); s_c.append(cv); s_fk.append(fk); s_fv.append(fv); s_fl.append(fl)
        else:
            o, wk, wv = c_mixer(rmsnorm(xp, g_mix[layer]), None, None, w_in_c[i], sinks_c[i], w_out_c[i])
            xp = xp + o
            p_wk.append(wk); p_wv.append(wv)
            o, wk, wv = c_mixer(rmsnorm(xs, g_mix[layer]), cache_swa_k[i], cache_swa_v[i],
                                w_in_c[i], sinks_c[i], w_out_c[i])
            xs = xs + o
            s_wk.append(wk); s_wv.append(wv)
        mk, mv = mem_kv(mem_prompt, g_mem[layer], w_xkv[layer])
        p_mk.append(mk); p_mv.append(mv)
        xp = xp + cross_attend(rmsnorm(xp, g_cross[layer]), mk, mv, w_xq[layer], w_xo[layer])
        xs = xs + cross_attend(rmsnorm(xs, g_cross[layer]), cache_mem_k[layer], cache_mem_v[layer],
                               w_xq[layer], w_xo[layer])
        xp = xp + sq_relu_mlp(rmsnorm(xp, g_mlp[layer]), w_up[layer], w_down[layer])
        xs = xs + sq_relu_mlp(rmsnorm(xs, g_mlp[layer]), w_up[layer], w_down[layer])
    y_prompt = rmsnorm(xp, g_final)
    y_sample = rmsnorm(xs, g_final)
    return (y_prompt, y_sample,
            jnp.stack(p_s), jnp.stack(p_c), jnp.stack(p_fk), jnp.stack(p_fv), jnp.stack(p_fl),
            jnp.stack(p_wk), jnp.stack(p_wv), jnp.stack(p_mk), jnp.stack(p_mv),
            jnp.stack(s_s), jnp.stack(s_c), jnp.stack(s_fk), jnp.stack(s_fv), jnp.stack(s_fl),
            jnp.stack(s_wk), jnp.stack(s_wv))


_drawn_inputs = setup_inputs


def setup_inputs(seed=0):
    import zlib

    import numpy as np

    out = dict(_drawn_inputs(seed))
    spreads = {}
    factors = {'cache_fox_logf': 3.446,
     'onorm_g_a': 6.093,
     'sinks_c': 8.0,
     'g_mem': 2.886,
     'g_cross': 8.0,
     'g_final': 2.886}
    for name, (base, spread) in spreads.items():
        noise = np.random.default_rng([zlib.crc32(name.encode()), seed]).standard_normal(out[name].shape)
        drawn = base * np.exp(spread * noise) if base else spread * noise
        out[name] = __import__('jax').numpy.asarray(drawn.astype(out[name].dtype))
    for name, factor in factors.items():
        out[name] = (out[name] * factor).astype(out[name].dtype)
    return out
```

```python
import concourse.bass as bass
from concourse import mybir
from contextlib import ExitStack


def build_program(nc, t):
    f32, f32r = mybir.dt.float32, mybir.dt.float32r
    ALU, ACT, AX = mybir.AluOpType, mybir.ActivationFunctionType, mybir.AxisListType

    D = t["x_prompt"].shape[2]
    NPT = t["x_prompt"].shape[1]
    NS = t["x_sample"].shape[1]
    N = NPT + NS
    HALF = N // 2
    KT = D // 128
    H = t["state_gdn"].shape[2]
    HD = 128
    NCONV = t["state_gdn_conv"].shape[3] // 128
    CW = t["conv_w_a"].shape[1]
    PAD = CW - 1
    CH = 64
    PAST = t["cache_fox_k"].shape[2]
    WIN = t["cache_swa_k"].shape[2]
    HKV, HDC = t["cache_swa_k"].shape[3], t["cache_swa_k"].shape[4]
    HQ = t["sinks_c"].shape[1]
    MEM = t["mem_prompt"].shape[1]
    DFF = t["w_up"].shape[2]
    NB = DFF // D
    TT = NPT // 128
    NTOK = TT + 1
    EPS = 1e-6
    BIG = 1e30
    TOK = [(j, 128 * j, 128) for j in range(TT)] + [(TT, NPT, NS)]
    UPAD = PAD + NPT + PAD + NS
    GATES = 3 * H

    LIN = {}
    order = [("in_a", 8, 2), ("in_b", 6, 2)]
    for l in range(2):
        if l == 1:
            order += [("in_c", 6, 2)]
        order += [(f"out{l}", 4, 2), (f"mem{l}", 4, 2), (f"xq{l}", 2, 2), (f"xo{l}", 2, 4)]
        order += [(f"mlp{l}", 8 * NB, 2)]
    p = q = d = 0
    DRAINED = {}
    for name, panels, tpp in order:
        LIN[name] = (p, q, panels, tpp)
        DRAINED[name] = d
        p, q, d = p + panels, q + panels * tpp, d + panels * tpp // (2 if name[:3] == "mlp" else 1)
    PANELS = p

    def last_tile(name):
        return DRAINED[name] + LIN[name][2] * LIN[name][3]

    PER_LAYER = (2 + NB) * KT
    NORM_BASE = [0, KT, 2 * KT, PER_LAYER, PER_LAYER + KT, PER_LAYER + 2 * KT, 2 * PER_LAYER]
    RES = {"out0": 1, "xo0": 2, "out1": 4, "xo1": 5}
    MASKS = 15 + 6 + 3 + 6 + 6 + 2 + 6 + 2
    GATE_LOGF = 6
    STORES_TOTAL = 2 + 2 * NTOK + 2 + 2 + 4 + 4 + NTOK

    ctx = ExitStack()
    with ctx:
        def sem(name):
            return ctx.enter_context(nc.semaphore(name))

        cursor = [(nc.sbuf_base + 31) // 32 * 32]

        def place(name, shape, dt=f32, at=None):
            size = 4
            for n in shape[1:]:
                size *= n
            size = (size + 31) // 32 * 32
            if at is None:
                at = cursor[0]
                cursor[0] += size
            return nc.alloc_sbuf_tensor_at(name, shape, dt, offset=at)

        x = place("x", [128, KT, N])
        xh_at = cursor[0]
        xh = place("xh", [128, KT, N], f32r)
        xl_at = cursor[0]
        xl = place("xl", [128, KT, N], f32r)
        stage = [place(f"stage{s}", [128, 2048]) for s in range(2)]
        wh = [place(f"wh{s}", [128, 2048], f32r) for s in range(2)]
        wl = [place(f"wl{s}", [128, 2048], f32r) for s in range(2)]
        rstd = place("rstd", [128, N])
        acc_at = cursor[0]
        acc = place("acc", [128, N])
        sq_at = cursor[0]
        sq = place("sq", [128, 2, N])
        ident = place("ident", [128, 128])
        ones = place("ones", [128, 128])
        upper = place("upper", [128, NPT])
        chunk_upper = place("chunk_upper", [128, 128])
        chunk_later = place("chunk_later", [128, 128])
        chunk_strict = place("chunk_strict", [128, 128])
        chunk_rows = place("chunk_rows", [128, 2, 128])
        LEVELS = [1, 2, 4, 8, 16, 32]
        level = place("level", [128, len(LEVELS), 128])
        diag_mask = place("diag_mask", [128, 128])
        dist_p = place("dist_p", [128, 256])
        dist_s = place("dist_s", [NS, WIN + NS])
        NROW = 9 * KT + CW * NCONV + 1
        cols = place("cols", [128, NROW])
        gate_par = place("gate_par", [128, 3, H])
        sinks = place("sinks", [128, HQ])
        eps_col = place("eps_col", [128, 1])
        one_col = place("one_col", [128, 1])
        nm = place("nm", [128, 2])
        rs = place("rs", [128, 2])
        rr = place("rr", [128, 2])
        es = place("es", [128, 2])
        mem_ss = place("mem_ss", [128, 2])
        mem_rs = place("mem_rs", [128, 2])
        ARENA = cursor[0]
        peak = [ARENA]

        def arena(*parts):
            out, at = [], ARENA
            for part in parts:
                name, shape = part[0], part[1]
                dt = part[2] if len(part) > 2 else f32
                out.append(place(name, shape, dt, at=at))
                size = 4
                for n in shape[1:]:
                    size *= n
                at += (size + 31) // 32 * 32
            peak[0] = max(peak[0], at)
            return out

        x_rows, par_rows, conv_rows = arena(("x_rows", [128, NTOK, D]), ("par_rows", [NROW, 128]),
                                            ("conv_rows", [PAD * NCONV, 128]))
        (ua, z, vb_f, kb_f, qb_f, vb_n, Sb0, nF, PT0) = arena(
            ("ua", [128, NCONV, UPAD]), ("z", [128, H, N]),
            ("vb_f", [128, H, N]), ("kb_f", [128, H, N]), ("qb_f", [128, H, N]),
            ("vb_n", [128, NTOK, H * HD]), ("Sb0", [128, 2, N]), ("nF", [128, H, N]),
            ("PT0", [128, 2, 5 * 128]))
        gates_at = peak[0] - 4 * 2 * 5 * 128
        size = 4 * KT * GATES
        w_gate = place("w_gate", [128, KT, GATES], at=gates_at)
        wgh = place("wgh", [128, KT, GATES], f32r, at=gates_at + size)
        wgl = place("wgl", [128, KT, GATES], f32r, at=gates_at + 2 * size)
        k_out = place("k_out", [128, 2, H * HD], at=sq_at)
        gT = place("gT", [GATES, N], at=acc_at)
        at = ARENA + 4 * (NCONV * UPAD + H * N)
        at = (at + 31) // 32 * 32
        ka_at = at
        kpT = place("kpT", [128, H, PAST], at=xh_at)
        vp_n = place("vp_n", [128, PAST // 128, H * HD], at=xl_at)
        after_gates = [peak[0]]

        def more(name, shape, dt=f32):
            tt_ = place(name, shape, dt, at=after_gates[0])
            size = 4
            for n in shape[1:]:
                size *= n
            after_gates[0] += (size + 31) // 32 * 32
            return tt_

        G = more("G", [128, NTOK, GATES])
        Ga = more("Ga", [128, NTOK, GATES])
        Gb = more("Gb", [128, NTOK, GATES])
        lf_past = more("lf_past", [128, PAST // 128, H])
        peak[0] = max(peak[0], after_gates[0])
        gat = [ka_at]

        def gbuf(name, shape):
            b = place(name, shape, f32, at=gat[0])
            size = 4
            for n in shape[1:]:
                size *= n
            gat[0] += (size + 31) // 32 * 32
            return b

        o_a = gbuf("o_a", [128, H, N])
        dec, LT, AT, Tm, TmT, Xm, BT, kn, vbt, kbe, kd, um, wT, qe, vnew, S, brow = [
            gbuf(n, [128, H, 128]) for n in
            ("dec", "LT", "AT", "Tm", "TmT", "Xm", "BT", "kn", "vbt", "kbe", "kd", "um", "wT", "qe", "vnew", "S", "brow")]
        gsm = gbuf("gsm", [128, 16])
        eg = gbuf("eg", [128, 2, H])
        conv_new = gbuf("conv_new", [128, 2, PAD, NCONV])
        conv_newT = gbuf("conv_newT", [2 * NCONV * PAD, 128])
        assert gat[0] <= gates_at + 4 * 2 * 5 * 128
        (q_c, k_c, v_c, v_cn, kc_out, kc_rows, vc_rows, kcT, SbC, PTC) = arena(
            ("q_c", [128, 8, N]), ("k_c", [128, 2, N]), ("v_c", [128, 2, N]),
            ("v_cn", [128, NTOK, HKV * HDC]), ("kc_out", [128, 2, HKV * HDC]),
            ("kc_rows", [128, HKV * HDC]), ("vc_rows", [128, HKV * HDC]), ("kcT", [128, 2, WIN]),
            ("SbC", [128, 2, N]), ("PTC", [128, 2, 5 * 128]))
        (m_rows, mh, ml, kvT, kv_n, q_x, kx_rows, vx_rows, kxT, SbX, PTX) = arena(
            ("m_rows", [128, 2, D]), ("mh", [128, KT, MEM], f32r), ("ml", [128, KT, MEM], f32r),
            ("kvT", [128, KT, MEM]), ("kv_n", [128, 2, D]), ("q_x", [128, H, N]),
            ("kx_rows", [128, 2, H * HD]), ("vx_rows", [128, 2, H * HD]), ("kxT", [128, H, MEM]),
            ("SbX", [128, 2, N]), ("PTX", [128, 2, 5 * 128]))
        hh, hl, rel, hsq, dtmp, rstd2 = arena(
            ("hh", [128, KT, N], f32r), ("hl", [128, KT, N], f32r), ("rel", [128, 2, N]),
            ("hsq", [128, 2, N]), ("dtmp", [128, 2, N]), ("rstd2", [128, N]))
        y_rows, yT = arena(("y_rows", [128, NTOK, D]), ("yT", [128, KT, N]))
        assert peak[0] <= nc.sbuf_usable_end, (peak[0], nc.sbuf_usable_end)

        LP = ctx.enter_context(nc.psum_tensor("LP", [128, 4, 512], f32))
        MP = ctx.enter_context(nc.psum_tensor("MP", [128, 4, 512], f32))

        def column(row):
            return cols[:, row:row + 1]

        def gain(norm, k):
            return column(norm * KT + k)

        def conv_w(i, f):
            return column(9 * KT + i * NCONV + f)

        ONORM = 9 * KT + CW * NCONV

        w_loaded = [sem(f"w_loaded{s}") for s in range(2)]
        w_hi = sem("w_hi")
        w_lo = sem("w_lo")
        product_done = sem("product_done")
        drained = sem("drained")
        x_loaded, par_loaded, mask_done = sem("x_loaded"), sem("par_loaded"), sem("mask_done")
        param_turned, param_ready = sem("param_turned"), sem("param_ready")
        x_turned, x_done = sem("x_turned"), sem("x_done")
        sq_ready, sq_used, xh_ready, xs_ready = sem("sq_ready"), sem("sq_used"), sem("xh_ready"), sem("xs_ready")
        stat_done, rstd_ready = sem("stat_done"), sem("rstd_ready")
        act_step, dve_step, pe_step = sem("act_step"), sem("dve_step"), sem("pe_step")
        stored = sem("stored")
        relu_ready, hh_ready, hsq_ready, h_ready, down_mul = (sem("relu_ready"), sem("hh_ready"),
                                                              sem("hsq_ready"), sem("h_ready"), sem("down_mul"))
        gate_pe, gate_act, gate_dve = sem("gate_pe"), sem("gate_act"), sem("gate_dve")
        conv_act, conv_dve, conv_pe = sem("conv_act"), sem("conv_dve"), sem("conv_pe")
        turn_pe, turn_act = sem("turn_pe"), sem("turn_act")
        sc_ready, nm_ready, ex_ready, p_ready = sem("sc_ready"), sem("nm_ready"), sem("ex_ready"), sem("p_ready")
        tr_ready, pt_ready, o_ready, oh_ready, ol_ready = (sem("tr_ready"), sem("pt_ready"), sem("o_ready"),
                                                           sem("oh_ready"), sem("ol_ready"))
        gd_pe, gd_act, gd_dve = sem("gd_pe"), sem("gd_act"), sem("gd_dve")
        s_loaded = sem("s_loaded")
        mem_loaded, mem_act, mem_dve, mem_pe = sem("mem_loaded"), sem("mem_act"), sem("mem_dve"), sem("mem_pe")
        cx_loaded, cx_pe, cx_act = sem("cx_loaded"), sem("cx_pe"), sem("cx_act")
        cc_loaded, cc_pe, cc_act = sem("cc_loaded"), sem("cc_pe"), sem("cc_act")
        y_pe, y_act, y_dve = sem("y_pe"), sem("y_act"), sem("y_dve")
        arena_free = sem("arena_free")
        rows_pe, rows_act = sem("rows_pe"), sem("rows_act")
        head_sq, head_sum, head_ln, head_exp, head_mul = (sem("head_sq"), sem("head_sum"), sem("head_ln"),
                                                          sem("head_exp"), sem("head_mul"))
        head_y, head_hi = sem("head_y"), sem("head_hi")
        gate_in, vpast_in = sem("gate_in"), sem("vpast_in")
        kpast_in = [sem(f"kpast_in{s}") for s in range(2)]
        s_zero, low_done = sem("s_zero"), sem("low_done")

        UNITS, GROUP = [], {}

        def group(name, units):
            GROUP[name] = (len(UNITS), len(units))
            UNITS.extend(units)

        def unit(**kw):
            return kw

        def fox_units(sample):
            out = []
            for h in range(H):
                if sample:
                    out.append(unit(P=NS, q=qb_f[:, h, NPT:N],
                                    keys=[(kpT[:, h, :], PAST), (kb_f[:, h, NPT:N], NS)],
                                    scale=HD ** -0.5, bias=("fox", h), diag=NS, S=Sb0, PT=PT0,
                                    v=[(128, vp_n[:, c, h * HD:(h + 1) * HD]) for c in range(PAST // 128)]
                                    + [(NS, vb_n[0:NS, TT, h * HD:(h + 1) * HD])],
                                    D=HD, hi=xh[:, H + h, NPT:N], lo=xl[:, H + h, NPT:N]))
                    continue
                for j in range(TT):
                    nk = 128 * (j + 1)
                    out.append(unit(P=128, q=qb_f[:, h, 128 * j:nk], keys=[(kb_f[:, h, 0:nk], nk)],
                                    scale=HD ** -0.5, bias=("fox", h), diag=128, S=Sb0, PT=PT0,
                                    v=[(128, vb_n[:, c, h * HD:(h + 1) * HD]) for c in range(j + 1)],
                                    D=HD, hi=xh[:, H + h, 128 * j:nk], lo=xl[:, H + h, 128 * j:nk]))
            return out

        def cross_units():
            out = []
            for h in range(H):
                for j, a, P in TOK:
                    kT = kvT[:, h, :] if j < TT else kxT[:, h, :]
                    vv = [(128, kv_n[:, c, H * HD + h * HD:H * HD + (h + 1) * HD]) if j < TT else
                          (128, vx_rows[:, c, h * HD:(h + 1) * HD]) for c in range(MEM // 128)]
                    out.append(unit(P=P, q=q_x[:, h, a:a + P], keys=[(kT, MEM)], scale=HD ** -0.5, bias=None,
                                    diag=0, S=SbX, PT=PTX, v=vv, D=HD,
                                    hi=xh[:, h, a:a + P], lo=xl[:, h, a:a + P]))
            return out

        def swa_units():
            out = []
            for h in range(HQ):
                kv = h // (HQ // HKV)
                o, slot, kt_ = (kv % 2) * 64, (h // 8) * 4 + h % 4, kv // 2
                ho = (h % 2) * 64
                slope = 2.0 ** (-8.0 * (h + 1) / HQ)
                for j, a, P in TOK:
                    if j == TT:
                        keys = [(kcT[o:o + 64, kt_, :], WIN), (k_c[o:o + 64, kt_, a:a + P], P)]
                        vv = [(WIN, vc_rows[:, kv * HDC:(kv + 1) * HDC]), (P, v_cn[0:P, j, kv * HDC:(kv + 1) * HDC])]
                        dist = dist_s[:, :]
                    else:
                        first = max(j - 1, 0)
                        n = a + 128 - 128 * first
                        keys = [(k_c[o:o + 64, kt_, 128 * first:a + 128], n)]
                        vv = [(128, v_cn[:, c, kv * HDC:(kv + 1) * HDC]) for c in range(first, j + 1)]
                        dist = dist_p[:, 256 - n:256]
                    out.append(unit(P=P, q=q_c[o:o + 64, slot, a:a + P], keys=keys, scale=1.0,
                                    bias=("swa", h, dist, slope), diag=0, S=SbC, PT=PTC, v=vv, D=HDC,
                                    hi=xh[ho:ho + 64, h // 2, a:a + P], lo=xl[ho:ho + 64, h // 2, a:a + P]))
            return out

        group("fox_p", fox_units(False))
        group("fox_s", fox_units(True))
        group("cross0", cross_units())
        group("swa", swa_units())
        group("cross1", cross_units())

        PE_GD = ["gram", "turns"] + [f"{w}{s}" for s in LEVELS[1:] for w in ("bx", "delta")] \
            + ["uw", "ws0", "o0", "ws1", "o1"]
        ACT_GD = ["exps", "dec", "kn", "t_copy"] + [f"x{s}" for s in LEVELS[1:]] + ["wT", "ov"]
        DVE_GD = ["rows", "lt", "tt1", "mul"] + [f"{w}{s}" for s in LEVELS[1:] for w in ("b", "t")] \
            + ["u", "vn0", "s0", "vn1", "s1"]

        def at_step(steps, name, j):
            return j * len(steps) + steps.index(name) + 1

        STORES = [0]

        block = ctx.enter_context(nc.Block())

        def loads_of(name):
            l = int(name[-1]) if name[-1].isdigit() else 0
            if name in ("in_a", "in_b", "in_c", "mem0", "mem1", "xq0", "xq1", "out0", "out1"):
                w, c0 = {"in_a": (t["w_in_ab"][0], 0), "in_b": (t["w_in_ab"][0], 16 * 128 + 2 * H),
                         "in_c": (t["w_in_c"][0], 0), "mem": (t["w_xkv"][l], 0), "xq": (t["w_xq"][l], 0),
                         "out": (t["w_out_ab"][0] if l == 0 else t["w_out_c"][0], 0)}[
                             name if name in ("in_a", "in_b", "in_c") else name[:-1]]
                v = w.rearrange("(k p) n -> p k n", p=128)
                return lambda i: v[:, :, bass.ds(c0 + 256 * i, 256)]
            v = t["w_xo"][l].rearrange("(k p) n -> p k n", p=128)
            return lambda i: v[:, :, bass.ds(512 * i, 512)]

        @block.sync
        def _(sp):
            for j, a, P in TOK[:TT]:
                sp.dma_start(x_rows[:, j, :], t["x_prompt"][0, a:a + P, :]).then_inc(x_loaded, 16)
            sp.dma_start(x_rows[0:NS, TT, :], t["x_sample"][0]).then_inc(x_loaded, 16)
            row = 0
            for name, l in (("g_mix", 0), ("g_cross", 0), ("g_mlp", 0), ("g_mix", 1), ("g_cross", 1), ("g_mlp", 1),
                            ("g_final", None), ("g_mem", 0), ("g_mem", 1)):
                g = t[name] if l is None else t[name][l]
                sp.dma_start(par_rows[row:row + KT, :], g.rearrange("(k p) -> k p", p=128)).then_inc(par_loaded, 16)
                row += KT
            sp.dma_start(par_rows[row:row + CW * NCONV, :],
                         t["conv_w_a"][0].rearrange("i (f p) -> (i f) p", p=128)).then_inc(par_loaded, 16)
            row += CW * NCONV
            sp.dma_start(par_rows[row:row + 1, :], t["onorm_g_a"]).then_inc(par_loaded, 16)
            sp.dma_start(conv_rows[:, :], t["state_gdn_conv"][0, 0].rearrange("i (f p) -> (i f) p", p=128)
                         ).then_inc(par_loaded, 16)
            for i, name in enumerate(("a_log_a", "dt_bias_a", "f_bias_b")):
                sp.dma_start(gate_par[:, i, :], t[name][0].partition_broadcast(128)).then_inc(par_loaded, 16)
            sp.dma_start(sinks[:, :], t["sinks_c"][0].partition_broadcast(128)).then_inc(par_loaded, 16)

            def load(slot, source, kt, panel):
                if not (isinstance(panel, int) and panel < 2):
                    sp.wait_ge(w_lo, panel - 1)
                sp.dma_start(stage[slot][:, :].rearrange("p (k n) -> p k n", k=kt), source
                             ).then_inc(w_loaded[slot], 16)

            def first_pair(name, kt=KT):
                src = loads_of(name)
                load(0, src(0), kt, LIN[name][0])
                load(1, src(1), kt, LIN[name][0] + 1)

            def rest(name, kt=KT):
                p0, _, panels, _ = LIN[name]
                src = loads_of(name)
                if panels > 2:
                    with sp.Fori(1, panels // 2) as i:
                        load(0, src(2 * i), kt, p0 + 2 * i)
                        load(1, src(2 * i + 1), kt, p0 + 2 * i + 1)

            def product(name, kt=KT):
                first_pair(name, kt)
                rest(name, kt)

            def mlp(l):
                p0 = LIN[f"mlp{l}"][0]
                up_v = t["w_up"][l].rearrange("(k p) n -> p k n", p=128)
                dn_v = t["w_down"][l].rearrange("(k p) n -> p k n", p=128)
                with sp.Fori(0, NB) as b:
                    for i in range(4):
                        load(i % 2, up_v[:, :, bass.ds(b * D + 256 * i, 256)], KT, p0 + 8 * b + i)
                    for i in range(4):
                        load(i % 2, dn_v[:, bass.ds(b * KT, KT), 256 * i:256 * i + 256], KT, p0 + 8 * b + 4 + i)

            def layer_end(l):
                rest(f"out{l}")
                first_pair(f"mem{l}")
                sp.wait_ge(arena_free, 1 + l)
                sp.dma_start(m_rows[:, :, :], t["mem_prompt"][0].rearrange("(c p) d -> p c d", p=128)
                             ).then_inc(mem_loaded, 16)
                sp.dma_start(kx_rows[:, :, :], t["cache_mem_k"][l, 0].rearrange("(c p) h d -> p c (h d)", p=128)
                             ).then_inc(cx_loaded, 16)
                sp.dma_start(vx_rows[:, :, :], t["cache_mem_v"][l, 0].rearrange("(c p) h d -> p c (h d)", p=128)
                             ).then_inc(cx_loaded, 16)
                rest(f"mem{l}")
                product(f"xq{l}")
                product(f"xo{l}", 4)
                mlp(l)

            first_pair("in_a")
            sp.wait_ge(x_done, KT)
            w = t["w_in_ab"][0].rearrange("(k p) n -> p k n", p=128)
            sp.dma_start(w_gate[:, :, 0:2 * H], w[:, :, 16 * 128:16 * 128 + 2 * H]).then_inc(gate_in, 16)
            sp.dma_start(w_gate[:, :, 2 * H:3 * H], w[:, :, w.shape[2] - H:w.shape[2]]).then_inc(gate_in, 16)
            sp.dma_start(lf_past[:, :, :], t["cache_fox_logf"][0, 0].rearrange("(c p) h -> p c h", p=128)
                         ).then_inc(gate_in, 16)
            rest("in_a")
            product("in_b")
            first_pair("out0")
            sp.wait_ge(gate_pe, 1)
            sp.dma_start(vp_n[:, :, :],
                         t["cache_fox_v"][0, 0].rearrange("(c p) h d -> p c (h d)", p=128)).then_inc(vpast_in, 16)
            for c in range(PAST // 128):
                if c >= 2:
                    sp.wait_ge(turn_pe, NTOK + c - 1)
                else:
                    sp.wait_ge(turn_act, NTOK + 1)
                sp.dma_start(k_out[:, c % 2, :],
                             t["cache_fox_k"][0, 0, 128 * c:128 * c + 128].rearrange("p h d -> p (h d)")
                             ).then_inc(kpast_in[c % 2], 16)
            layer_end(0)
            product("in_c")
            first_pair("out1")
            sp.wait_ge(drained, DRAINED["in_c"] + 4)
            sp.dma_start(kc_rows[:, :], t["cache_swa_k"][0, 0].rearrange("p h d -> p (h d)")).then_inc(cc_loaded, 16)
            sp.dma_start(vc_rows[:, :], t["cache_swa_v"][0, 0].rearrange("p h d -> p (h d)")).then_inc(cc_loaded, 16)
            layer_end(1)
            sp.wait_ge(stored, 16 * STORES_TOTAL)

        @block.gpsimd
        def _(pool):
            n = [0]

            def step(inst):
                inst.then_inc(mask_done, 1)
                n[0] += 1
                pool.wait_ge(mask_done, n[0])

            for m, v in ((ident, 0.0), (ones, 1.0), (upper, 1.0), (chunk_upper, 1.0), (chunk_later, 1.0),
                         (chunk_strict, 1.0), (diag_mask, 0.0), (eps_col, EPS), (dist_p, 0.0), (dist_s, 0.0)):
                step(pool.memset(m[:, :], v))
            step(pool.memset(level[:, :, :], 0.0))
            step(pool.memset(G[:, :, :], 0.0))
            step(pool.memset(chunk_rows[:, :, :], 0.0))
            for c in range(2):
                step(pool.memset(chunk_rows[64 * c:64 * c + 64, c, :], 1.0))

            def select(m, pattern, base, mult, op, fill):
                step(pool.affine_select(out=m, in_=m, pattern=pattern, base=base, channel_multiplier=mult,
                                        compare_op=op, fill=fill))

            select(ident[:, :], [[-1, 128]], 0, 1, ALU.not_equal, 1.0)
            select(upper[:, :], [[1, NPT]], 0, -1, ALU.is_ge, 0.0)
            select(chunk_upper[:, :], [[1, 128]], 0, -1, ALU.is_ge, 0.0)
            select(chunk_strict[:, :], [[1, 128]], -1, -1, ALU.is_ge, 0.0)
            select(chunk_later[:, :], [[-1, 128]], -1, 1, ALU.is_ge, 0.0)
            select(diag_mask[:, :], [[-1, 128]], 0, 1, ALU.is_ge, -BIG)
            for m in (chunk_upper, chunk_strict):
                select(m[0:64, 64:128], [[0, 64]], -1, 0, ALU.is_ge, 0.0)
            select(chunk_later[64:128, 0:64], [[0, 64]], -1, 0, ALU.is_ge, 0.0)
            for n_, s in enumerate(LEVELS):
                part = level[:, n_, :].rearrange("p (b r c) -> p b r c", r=2, c=s)[:, :, 1, :]
                step(pool.memset(part, 1.0))
            for n_, s in enumerate(LEVELS):
                part = level[:, n_, :].rearrange("p (b r c) -> p b r c", r=2, c=s)[:, :, 1, :]
                select(part, [[-2 * s, 64 // s], [0, s]], 0, 1, ALU.is_ge, 0.0)
            step(pool.iota(dist_p[:, :], [[-1, 256]], base=128, channel_multiplier=1,
                           allow_small_or_imprecise_dtypes=True))
            step(pool.iota(dist_s[:, :], [[-1, WIN + NS]], base=WIN, channel_multiplier=1,
                           allow_small_or_imprecise_dtypes=True))
            for n_, s in enumerate(LEVELS):
                part = level[:, n_, :].rearrange("p (b r c) -> p b r c", r=2, c=s)[:, :, 1, :]
                select(part, [[2 * s, 64 // s], [0, s]], s - 1, -1, ALU.is_ge, 0.0)
            step(pool.memset(dist_p[0:64, 192:256], BIG))
            step(pool.memset(dist_p[64:128, 0:64], BIG))
            assert n[0] == MASKS, n[0]

            with pool.Fori(0, PANELS // 2) as i:
                for s in range(2):
                    pool.wait_ge(w_hi, 2 * i + s + 1)
                    pool.tensor_tensor(wl[s][:, :], stage[s][:, :], wh[s][:, :].bitcast(f32), ALU.subtract
                                       ).then_inc(w_lo, 1)

        @block.tensor
        def _(pe):
            def tile(slot, s, col, W, kt, halves, X, ready=None):
                w_view = [w[s][:, :].rearrange("p (k n) -> p k n", k=kt) for w in (wh, wl)]
                mm = None
                for k in range(kt):
                    if ready is not None:
                        pe.wait_ge(ready[0], ready[1] + k + 1)
                    for n_, (w, part) in enumerate(((0, 0), (0, 1), (1, 0))):
                        for half, (a, b) in enumerate(halves):
                            mm = pe.matmul(LP[:, 2 * slot + half, 0:b - a], w_view[w][:, k, col:col + 128],
                                           X[part][:, k, a:b], start=(k == 0 and n_ == 0),
                                           stop=(k == kt - 1 and n_ == 2))
                return mm

            TOKENS = ((0, HALF), (HALF, N))

            def pair(free, Pn, tpp, kt, halves, X, ready, after_first=None):
                for s in range(2):
                    pe.wait_ge(w_lo, Pn + s + 1)
                    for i in range(tpp):
                        tt_ = s * tpp + i
                        if free(tt_) is not None:
                            pe.wait_ge(*free(tt_))
                        tile(tt_ % 2, s, 128 * i, None, kt, halves, X, ready if tt_ == 0 else None
                             ).then_inc(product_done, 1)
                        if tt_ == 0 and after_first is not None:
                            after_first()

            def product(name, X, ready, kt=KT, halves=TOKENS, after_first=None):
                p0, _, panels, tpp = LIN[name]
                d0 = DRAINED[name]
                pair(lambda n_: (drained, d0 + n_ - 1) if d0 + n_ >= 2 else None, p0, tpp, kt, halves, X, ready,
                     after_first)
                if panels > 2:
                    with pe.Fori(1, panels // 2) as i:
                        pair(lambda n_: (drained, d0 + 2 * tpp * i + n_ - 1), p0 + 2 * i, tpp, kt, halves, X, None)

            def stat(n):
                def go():
                    pe.wait_ge(sq_used, KT * (n + 1))
                    if n:
                        pe.wait_ge(rstd_ready, n)
                    for half, (a, b) in enumerate(TOKENS):
                        mm = pe.matmul(MP[:, half, 0:HALF], ones[:, :], acc[:, a:b], start=True, stop=True)
                    mm.then_inc(stat_done, 1)
                return go

            XS = (xh, xl)

            def attention(name):
                u0, count = GROUP[name]

                def scores(u):
                    U = UNITS[u]
                    if u >= 2:
                        pe.wait_ge(ex_ready, u - 1)
                    at = 0
                    for kT, n in U["keys"]:
                        slot = 2 * (u % 2) + at // 512
                        mm = pe.matmul(LP[0:U["P"], slot, at % 512:at % 512 + n], U["q"], kT, start=True, stop=True)
                        at += n
                    mm.then_inc(sc_ready, 1)

                def turn(u):
                    U = UNITS[u]
                    P = U["P"]
                    pe.wait_ge(p_ready, u + 1)
                    if u >= 2:
                        pe.wait_ge(pt_ready, u - 1)
                    at = 0
                    for c, (n, _) in enumerate(U["v"]):
                        mm = pe.transpose(MP[0:n, u % 2, c * P:c * P + P], U["S"][0:P, u % 2, at:at + n],
                                          ident[0:P, 0:P])
                        at += n
                    mm.then_inc(tr_ready, 1)

                def values(u):
                    U = UNITS[u]
                    P = U["P"]
                    pe.wait_ge(pt_ready, u + 1)
                    if u >= 2:
                        pe.wait_ge(ol_ready, u - 1)
                    for c, (n, v) in enumerate(U["v"]):
                        mm = pe.matmul(MP[0:U["D"], 2 + u % 2, 0:P], v, U["PT"][0:n, u % 2, c * P:c * P + P],
                                       start=(c == 0), stop=(c == len(U["v"]) - 1))
                    mm.then_inc(o_ready, 1)

                for i in range(count + 2):
                    if i < count:
                        scores(u0 + i)
                    if 1 <= i <= count:
                        turn(u0 + i - 1)
                    if i >= 2:
                        values(u0 + i - 2)

            pe.wait_ge(mask_done, MASKS)
            pe.wait_ge(par_loaded, 16 * 16)
            pe.transpose(MP[:, 0, 0:NROW], par_rows[:, :], ident[0:NROW, 0:NROW])
            pe.transpose(MP[:, 1, 0:PAD * NCONV], conv_rows[:, :], ident[0:PAD * NCONV, 0:PAD * NCONV]
                         ).then_inc(param_turned, 1)
            pe.wait_ge(x_loaded, 16 * NTOK)
            for k in range(KT):
                if k >= 2:
                    pe.wait_ge(x_done, k - 1)
                for j, a, P in TOK:
                    mm = pe.transpose(LP[:, 2 * (k % 2) + j // TT, (a % NPT):(a % NPT) + P],
                                      x_rows[0:P, j, 128 * k:128 * k + 128], ident[0:P, 0:P])
                mm.then_inc(x_turned, 1)
            pe.wait_ge(x_done, KT)
            pe.wait_ge(param_ready, 2)

            product("in_a", XS, (xs_ready, 0), after_first=stat(0))
            product("in_b", XS, None)
            pe.wait_ge(gate_act, 1)
            pe.wait_ge(gate_dve, 1)
            pe.wait_ge(drained, last_tile("in_b"))
            for k in range(KT):
                for n_, (w, X) in enumerate(((wgh, xh), (wgh, xl), (wgl, xh))):
                    for half, (a, b) in enumerate(TOKENS):
                        mm = pe.matmul(MP[0:GATES, half, 0:HALF], w[:, k, :], X[:, k, a:b],
                                       start=(k == 0 and n_ == 0), stop=(k == KT - 1 and n_ == 2))
            mm.then_inc(gate_pe, 1)
            pe.wait_ge(gate_dve, 2)
            for j, a, P in TOK:
                mm = pe.transpose(MP[0:P, 2, GATES * j:GATES * j + GATES], gT[:, a:a + P], ident[0:GATES, 0:GATES])
            mm.then_inc(gate_pe, 1)
            for j, a, P in TOK:
                if j >= 2:
                    pe.wait_ge(turn_act, j - 1)
                for h in range(H):
                    pe.transpose(LP[0:P, 2 * (j % 2), 128 * h:128 * h + 128], kb_f[:, h, a:a + P], ident[:, :])
                for h in range(H):
                    mm = pe.transpose(LP[0:P, 2 * (j % 2) + 1, 128 * h:128 * h + 128], vb_f[:, h, a:a + P],
                                      ident[:, :])
                mm.then_inc(turn_pe, 1)
            pe.wait_ge(turn_act, NTOK + 1)
            for c in range(PAST // 128):
                pe.wait_ge(kpast_in[c % 2], 16 * (c // 2 + 1))
                if c >= 2:
                    pe.wait_ge(turn_act, NTOK + 1 + c - 1)
                for h in range(H):
                    mm = pe.transpose(LP[:, c % 2, 128 * h:128 * h + 128], k_out[:, c % 2, 128 * h:128 * h + 128],
                                      ident[:, :])
                mm.then_inc(turn_pe, 1)
            pe.wait_ge(turn_act, NTOK + 1 + PAST // 128)

            def forget_rows(sample):
                pe.wait_ge(gate_dve, GATE_LOGF)
                if sample:
                    pe.wait_ge(ol_ready, GROUP["fox_p"][0] + GROUP["fox_p"][1])
                    pe.wait_ge(gate_in, 16 * 3)
                    pe.wait_ge(vpast_in, 16)
                for h in range(H):
                    if h >= 2:
                        pe.wait_ge(rows_act, (H if sample else 0) + h - 1)
                    b = 2 * (h % 2)
                    nt = NTOK if sample else TT
                    for j in range(nt):
                        if not sample:
                            lf, P = G[:, j, 2 * H + h:2 * H + h + 1], 128
                        elif j < TT:
                            lf, P = lf_past[:, j, h:h + 1], 128
                        else:
                            lf, P = G[0:NS, TT, 2 * H + h:2 * H + h + 1], NS
                        if j < TT:
                            mm = pe.matmul(LP[:, b, 128 * j:512], lf.to_broadcast([P, 128]),
                                           upper[0:P, 0:512 - 128 * j], start=(j == 0),
                                           stop=(j == TT - 1), skip_group_check=True)
                        if sample:
                            m = (ones[:, 0:NS] if j < TT else upper[0:NS, 0:NS])
                            mm = pe.matmul(LP[:, b + 1, 0:NS], lf.to_broadcast([P, 128]), m,
                                           start=(j == 0), stop=(j == TT), skip_group_check=True)
                    mm.then_inc(rows_pe, 1)

            forget_rows(False)
            pe.wait_ge(rows_act, H)
            attention("fox_p")
            forget_rows(True)
            pe.wait_ge(rows_act, 2 * H)
            attention("fox_s")
            pe.wait_ge(ol_ready, GROUP["fox_s"][0] + GROUP["fox_s"][1])

            def head_sums(first, count):
                for f in range(first, first + count):
                    pe.wait_ge(head_sq, f + 1)
                    if f >= 2:
                        pe.wait_ge(head_mul, f - 1)
                    for half, (a, b) in enumerate(TOKENS):
                        mm = pe.matmul(LP[:, 2 * (f % 2) + half, 0:HALF], ones[:, :], sq[:, f % 2, a:b],
                                       start=True, stop=True)
                    mm.then_inc(head_sum, 1)

            head_sums(0, 2 * H)
            pe.wait_ge(conv_dve, 1)
            pe.transpose(MP[0:2 * NCONV * PAD, 0, 0:128], conv_new[:, :, :, :].rearrange("p a i f -> p (a i f)"),
                         ident[:, :]).then_inc(conv_pe, 1)
            pe.wait_ge(head_mul, 2 * H)
            pe.wait_ge(conv_act, 2 + NCONV + 1)
            pe.wait_ge(gate_act, 7)

            def delta(j, a, P):
                nch = 2 if P == 128 else 1

                def done(mm, name):
                    mm.then_inc(gd_pe, 1)

                def dv(name, jj=j):
                    pe.wait_ge(gd_dve, at_step(DVE_GD, name, jj))

                def ac(name, jj=j):
                    pe.wait_ge(gd_act, at_step(ACT_GD, name, jj))

                if j:
                    dv("s1", j - 1)
                    ac("ov", j - 1)
                for h in range(H):
                    g = Gb[0:P, j, H + h:H + h + 1].to_broadcast([P, 128])
                    be = Gb[0:P, j, h:h + 1].to_broadcast([P, 128])
                    kT, qT = ua[:, H + h, a:a + P], ua[:, h, a:a + P]
                    pe.matmul(LP[:, 0, h * P:h * P + P], g, chunk_upper[0:P, 0:P], start=True, stop=True,
                              skip_group_check=True)
                    pe.matmul(LP[:, 1, h * P:h * P + P], be, ident[0:P, 0:P], start=True, stop=True,
                              skip_group_check=True)
                    pe.matmul(LP[0:P, 2, h * P:h * P + P], kT, kT, start=True, stop=True, skip_group_check=True)
                    pe.matmul(LP[0:P, 3, h * P:h * P + P], kT, qT, start=True, stop=True, skip_group_check=True)
                g4 = Gb[0:P, j, H:2 * H]
                pe.matmul(MP[0:P, 0, 0:4], chunk_upper[0:P, 0:P], g4, start=True, stop=True, skip_group_check=True)
                mm = pe.matmul(MP[0:P, 0, 4:8], chunk_later[0:P, 0:P], g4, start=True, stop=True,
                               skip_group_check=True)
                C = P // nch
                for c in range(nch):
                    mm = pe.matmul(MP[:, 0, 8 + 4 * c:12 + 4 * c], chunk_rows[0:P, c, :], g4,
                                   start=True, stop=True, skip_group_check=True)
                done(mm, "gram")
                dv("tt1")
                for h in range(H):
                    pe.transpose(MP[0:P, 1, 128 * h:128 * h + 128], ua[:, H + h, a:a + P], ident[:, :])
                    pe.transpose(MP[0:P, 2, 128 * h:128 * h + 128], ua[:, 2 * H + h, a:a + P], ident[:, :])
                    mm = pe.transpose(MP[0:P, 3, P * h:P * h + P], TmT[0:P, h, 0:P], ident[0:P, 0:P])
                done(mm, "turns")
                for s in LEVELS[1:]:
                    dv(f"b{s}")
                    if s == 2:
                        ac("t_copy")
                    else:
                        dv(f"t{s // 2}")
                    for h in range(H):
                        mm = pe.matmul(LP[0:P, 2, h * P:h * P + P], BT[0:P, h, 0:P], Tm[0:P, h, 0:P],
                                       start=True, stop=True, skip_group_check=True)
                    done(mm, f"bx{s}")
                    ac(f"x{s}")
                    for h in range(H):
                        mm = pe.matmul(LP[0:P, 3, h * P:h * P + P], TmT[0:P, h, 0:P], Xm[0:P, h, 0:P],
                                       start=True, stop=True, skip_group_check=True)
                        mm = pe.matmul(LP[0:P, 1, h * P:h * P + P], Xm[0:P, h, 0:P], TmT[0:P, h, 0:P],
                                       start=True, stop=True, skip_group_check=True)
                    done(mm, f"delta{s}")
                dv("t32")
                dv("mul")
                for h in range(H):
                    pe.matmul(MP[0:P, 2, 128 * h:128 * h + 128], TmT[0:P, h, 0:P], vbt[0:P, h, :],
                              start=True, stop=True, skip_group_check=True)
                    mm = pe.matmul(MP[:, 3, P * h:P * h + P], kbe[0:P, h, :], TmT[0:P, h, 0:P],
                                   start=True, stop=True, skip_group_check=True)
                done(mm, "uw")
                ac("wT")
                dv("u")
                for c in range(2):
                    r = slice(c * C, c * C + C)
                    if c < nch:
                        if c == 1:
                            dv("s0")
                        elif j:
                            dv("s1", j - 1)
                        for h in range(H):
                            mm = pe.matmul(LP[0:P, 0, 128 * h:128 * h + 128], wT[:, h, 0:P], S[:, h, :],
                                           start=True, stop=True, skip_group_check=True)
                        done(mm, f"ws{c}")
                        dv(f"vn{c}")
                        for h in range(H):
                            pe.matmul(MP[:, 0, P * h + c * C:P * h + c * C + C], S[:, h, :], qe[:, h, r],
                                      start=True, stop=False, skip_group_check=True)
                            pe.matmul(MP[:, 0, P * h + c * C:P * h + c * C + C], vnew[r, h, :], AT[r, h, r],
                                      start=False, stop=True, skip_group_check=True)
                            mm = pe.matmul(MP[:, 1, 128 * h:128 * h + 128], kd[r, h, :], vnew[r, h, :],
                                           start=True, stop=True, skip_group_check=True)
                        done(mm, f"o{c}")
                    else:
                        pe.wait_ge(gd_pe, at_step(PE_GD, "o0", j))
                        pe.nop().then_inc(gd_pe, 2)

            for j, a, P in TOK:
                if j == TT:
                    pe.wait_ge(s_loaded, 16)
                elif j == 0:
                    pe.wait_ge(s_zero, 1)
                delta(j, a, P)
            head_sums(2 * H, H)
            pe.wait_ge(low_done, H)

            def layer_end(l):
                product(f"out{l}", XS, None)
                for k in range(KT):
                    pe.wait_ge(mem_dve, (KT + 1) * l + 1)
                    if k >= 2:
                        pe.wait_ge(mem_dve, (KT + 1) * l + k)
                    for c in range(MEM // 128):
                        mm = pe.transpose(MP[:, k % 2, 128 * c:128 * c + 128], m_rows[:, c, 128 * k:128 * k + 128],
                                          ident[:, :])
                    mm.then_inc(mem_pe, 1)
                product(f"mem{l}", (mh, ml), (mem_dve, (KT + 1) * l + 1), halves=((0, MEM),))
                pe.wait_ge(drained, last_tile(f"mem{l}"))
                for c in range(MEM // 128):
                    for k in range(KT):
                        mm = pe.transpose(MP[:, 2 * c + k // 4, 128 * (k % 4):128 * (k % 4) + 128],
                                          kvT[:, k, 128 * c:128 * c + 128], ident[:, :])
                mm.then_inc(cx_pe, 1)
                pe.wait_ge(cx_loaded, 32 * (l + 1))
                for h in range(H):
                    for c in range(MEM // 128):
                        mm = pe.transpose(LP[:, h // 2, 256 * (h % 2) + 128 * c:256 * (h % 2) + 128 * c + 128],
                                          kx_rows[:, c, 128 * h:128 * h + 128], ident[:, :])
                mm.then_inc(cx_pe, 1)
                pe.wait_ge(cx_act, 2 * (l + 1))
                product(f"xq{l}", XS, (xs_ready, KT * (3 * l + 1)), after_first=stat(3 * l + 1))
                pe.wait_ge(drained, last_tile(f"xq{l}"))
                attention(f"cross{l}")
                pe.wait_ge(ol_ready, sum(GROUP[f"cross{l}"]))
                product(f"xo{l}", XS, None, kt=4)
                mlp(l)

            def mlp_block(l, b, after_first):
                P_ = LIN[f"mlp{l}"][0] + 8 * b
                relus, downs = KT * NB * l + KT * b, DRAINED[f"mlp{l}"] + KT * b

                def free(k):
                    if k < 2:
                        return drained, downs - 1 + k
                    if k < KT + 2:
                        return relu_ready, relus + k - 1
                    return drained, downs + k - KT - 1

                pair(free, P_, 2, KT, TOKENS, XS, (xs_ready, KT * (3 * l + 2)) if after_first else None, after_first)
                pair(lambda n_: free(4 + n_), P_ + 2, 2, KT, TOKENS, XS, None)
                pair(lambda n_: free(8 + n_), P_ + 4, 2, KT, TOKENS, (hh, hl), (h_ready, relus))
                pair(lambda n_: free(12 + n_), P_ + 6, 2, KT, TOKENS, (hh, hl), None)

            def mlp(l):
                mlp_block(l, 0, stat(3 * l + 2))
                with pe.Fori(1, NB) as b:
                    mlp_block(l, b, None)

            layer_end(0)
            product("in_c", XS, (xs_ready, KT * 3), after_first=stat(3))
            pe.wait_ge(drained, last_tile("in_c"))
            pe.wait_ge(cc_loaded, 32)
            for c in range(2):
                mm = pe.transpose(LP[:, 0, 128 * c:128 * c + 128], kc_rows[:, 128 * c:128 * c + 128], ident[:, :])
            mm.then_inc(cc_pe, 1)
            for j, a, P in TOK:
                if j >= 2:
                    pe.wait_ge(cc_act, 1 + j - 1)
                for c in range(2):
                    pe.transpose(MP[0:P, 2 * (j % 2), 128 * c:128 * c + 128], k_c[:, c, a:a + P], ident[:, :])
                    mm = pe.transpose(MP[0:P, 2 * (j % 2) + 1, 128 * c:128 * c + 128], v_c[:, c, a:a + P],
                                      ident[:, :])
                mm.then_inc(cc_pe, 1)
            pe.wait_ge(cc_act, 1 + NTOK)
            attention("swa")
            pe.wait_ge(ol_ready, sum(GROUP["swa"]))
            layer_end(1)
            stat(6)()
            for j, a, P in TOK:
                if j == 0:
                    pe.wait_ge(y_dve, KT)
                if j >= 2:
                    pe.wait_ge(y_act, j - 1)
                for k in range(KT):
                    mm = pe.transpose(LP[0:P, 2 * (j % 2) + k // 4, 128 * (k % 4):128 * (k % 4) + 128],
                                      yT[:, k, a:a + P], ident[:, :])
                mm.then_inc(y_pe, 1)

        @block.scalar
        def _(act):
            n = [0]

            def step(inst):
                inst.then_inc(act_step, 1)
                n[0] += 1

            def settled():
                act.wait_ge(act_step, n[0])

            def store(dst, src):
                act.dma_start(dst, src).then_inc(stored, 16)
                STORES[0] += 1

            def split(s, need):
                act.wait_ge(w_loaded[s], need)
                act.copy(wh[s][:, :], stage[s][:, :]).then_inc(w_hi, 1)

            def splits(p0, t0, tpp, i):
                for s in range(2):
                    act.wait_ge(product_done, t0 + 2 * tpp * i + tpp * (s + 1))
                    split(s, 16 * (p0 // 2 + 2) + 16 * i)

            def product(name):
                p0, t0, panels, tpp = LIN[name]
                with act.Fori(0, panels // 2) as i:
                    splits(p0, t0, tpp, i)

            def norm(n_, last=False):
                g = n_
                for k in range(KT):
                    act.wait_ge(x_done, NORM_BASE[n_] + k + 1)
                    if k >= 2:
                        act.wait_ge(sq_used, KT * n_ + k - 1)
                    act.activation(sq[:, k % 2, :], x[:, k, :], ACT.Square).then_inc(sq_ready, 1)
                    if not last:
                        act.activation(xh[:, k, :], x[:, k, :], ACT.Copy, scale=gain(g, k)).then_inc(xh_ready, 1)

            def make_rstd(n_, squared=False):
                act.wait_ge(stat_done, n_ + 1)
                src = MP[:, 0:2, 0:HALF]
                dst = rstd[:, :].rearrange("p (a n) -> p a n", a=2)
                step(act.activation(dst, src, ACT.Ln, bias=eps_col[:, :], scale=1.0 / D))
                settled()
                if squared:
                    act.activation(rstd[:, :], rstd[:, :], ACT.Exp, scale=-1.0).then_inc(rstd_ready, 1)
                else:
                    act.activation(rstd[:, :], rstd[:, :], ACT.Exp, scale=-0.5).then_inc(rstd_ready, 1)

            def attention(name):
                u0, count = GROUP[name]

                def exps(u):
                    U = UNITS[u]
                    P, nk, s = U["P"], sum(n_ for _, n_ in U["keys"]), u % 2
                    act.wait_ge(nm_ready, u + 1)
                    src = U["S"][0:P, s, 0:nk] if U["bias"] else LP[0:P, 2 * s, 0:nk]
                    sc = 1.0 if U["bias"] else U["scale"]
                    inst = act.activation(U["S"][0:P, s, 0:nk], src, ACT.Exp, bias=nm[0:P, s:s + 1], scale=sc,
                                          accum_out=rs[0:P, s:s + 1])
                    if U["bias"] and U["bias"][0] == "swa":
                        h = U["bias"][1]
                        inst = act.activation(es[0:P, s:s + 1], sinks[0:P, h:h + 1], ACT.Exp, bias=nm[0:P, s:s + 1])
                    inst.then_inc(ex_ready, 1)

                def pt(u):
                    U = UNITS[u]
                    P, s = U["P"], u % 2
                    act.wait_ge(tr_ready, u + 1)
                    if u >= 2:
                        act.wait_ge(o_ready, u - 1)
                    full = sum(n_ == 128 for n_, _ in U["v"])
                    inst = act.copy(U["PT"][:, s, 0:full * P], MP[:, s, 0:full * P])
                    if full < len(U["v"]):
                        rows = U["v"][-1][0]
                        inst = act.copy(U["PT"][0:rows, s, full * P:full * P + P], MP[0:rows, s, full * P:full * P + P])
                    inst.then_inc(pt_ready, 1)

                def high(u):
                    U = UNITS[u]
                    act.wait_ge(o_ready, u + 1)
                    act.copy(U["hi"], MP[0:U["D"], 2 + u % 2, 0:U["P"]]).then_inc(oh_ready, 1)

                for i in range(count + 2):
                    if i < count:
                        exps(u0 + i)
                    if 1 <= i <= count:
                        pt(u0 + i - 1)
                    if i >= 2:
                        high(u0 + i - 2)

            act.preload_act_table_set("natural_log_exp_and_others")
            act.wait_ge(param_turned, 1)
            act.copy(cols[:, :], MP[:, 0, 0:NROW]).then_inc(param_ready, 1)
            act.wait_ge(param_ready, 1)
            norm(0)
            split(0, 16)
            split(1, 16)
            make_rstd(0)
            act.wait_ge(gate_in, 16 * 3)
            act.copy(wgh[:, :, :], w_gate[:, :, :]).then_inc(gate_act, 1)
            product("in_a")
            product("in_b")
            act.wait_ge(gate_pe, 2)
            act.copy(G[:, 0:TT, :].rearrange("p j c -> p (j c)"), MP[:, 2, 0:GATES * TT]).then_inc(gate_act, 1)
            act.copy(G[0:NS, TT, :], MP[0:NS, 2, GATES * TT:GATES * NTOK]).then_inc(gate_act, 1)
            act.wait_ge(gate_dve, 4)
            act.activation(Gb[:, :, :], Gb[:, :, :], ACT.Exp).then_inc(gate_act, 1)
            act.activation(gate_par[:, 0, :], gate_par[:, 0, :], ACT.Exp).then_inc(gate_act, 1)
            act.wait_ge(gate_act, 5)
            act.activation(Gb[:, :, :], Gb[:, :, :], ACT.Ln, bias=one_col[:, :]).then_inc(gate_act, 1)
            act.wait_ge(gate_dve, GATE_LOGF)
            act.activation(Gb[:, :, 0:H], Gb[:, :, 0:H], ACT.Exp, scale=-1.0).then_inc(gate_act, 1)
            act.wait_ge(gate_dve, GATE_LOGF)
            store(t["o_p_fox_logf"][0, 0].rearrange("(j p) h -> p j h", p=128), G[:, 0:TT, 2 * H:3 * H])
            store(t["o_s_fox_logf"][0, 0], G[0:NS, TT, 2 * H:3 * H])
            for j, a, P in TOK:
                act.wait_ge(turn_pe, j + 1)
                if j >= 2:
                    act.wait_ge(stored, 16 * STORES[0])
                step(act.copy(k_out[0:P, j % 2, :], LP[0:P, 2 * (j % 2), :]))
                act.copy(vb_n[0:P, j, :], LP[0:P, 2 * (j % 2) + 1, :]).then_inc(turn_act, 1)
                act.wait_ge(turn_act, j + 1)
                for nm_, src in (("k", k_out[0:P, j % 2, :]), ("v", vb_n[0:P, j, :])):
                    dst = t[f"o_p_fox_{nm_}"][0, 0, a:a + P] if j < TT else t[f"o_s_fox_{nm_}"][0, 0]
                    store(dst.rearrange("p h d -> p (h d)"), src)
            act.wait_ge(stored, 16 * STORES[0])
            act.nop().then_inc(turn_act, 1)
            for c in range(PAST // 128):
                act.wait_ge(turn_pe, NTOK + c + 1)
                act.copy(kpT[:, :, 128 * c:128 * c + 128].rearrange("p h n -> p h n"),
                         LP[:, c % 2, :].rearrange("p (h n) -> p h n", h=H)).then_inc(turn_act, 1)

            def forget_rows(sample):
                for h in range(H):
                    act.wait_ge(rows_pe, (H if sample else 0) + h + 1)
                    b = 2 * (h % 2)
                    inst = act.activation(nF[:, h, 0:512], LP[:, b, 0:512], ACT.Copy, scale=-1.0)
                    if sample:
                        inst = act.activation(nF[:, h, 512:N], LP[:, b + 1, 0:NS], ACT.Copy, scale=-1.0)
                    inst.then_inc(rows_act, 1)

            forget_rows(False)
            attention("fox_p")
            act.wait_ge(ol_ready, sum(GROUP["fox_p"]))
            forget_rows(True)
            attention("fox_s")

            act.wait_ge(conv_dve, 2)
            act.preload_act_table_set("silu_and_others")
            act.activation(z[:, :, :], z[:, :, :], ACT.Silu).then_inc(conv_act, 2)
            for f in range(NCONV):
                act.wait_ge(conv_dve, 2 + CW * (f + 1))
                act.activation(ua[:, f, 0:N], sq[:, f % 2, :], ACT.Silu).then_inc(conv_act, 1)
            act.wait_ge(conv_act, 2 + NCONV)
            act.preload_act_table_set("natural_log_exp_and_others")

            def head_square(f, src):
                if f >= 2:
                    act.wait_ge(head_sum, f - 1)
                act.activation(sq[:, f % 2, :], src, ACT.Square).then_inc(head_sq, 1)

            def head_rstd(f, scale):
                act.wait_ge(head_sum, f + 1)
                if f >= 2:
                    act.wait_ge(head_mul, f - 1)
                buf = (rstd, acc)[f % 2]
                act.activation(buf[:, :].rearrange("p (a n) -> p a n", a=2),
                               LP[:, 2 * (f % 2):2 * (f % 2) + 2, 0:HALF], ACT.Ln, bias=eps_col[:, :], scale=scale
                               ).then_inc(head_ln, 1)
                act.wait_ge(head_ln, f + 1)
                act.activation(buf[:, :], buf[:, :], ACT.Exp, scale=-0.5).then_inc(head_exp, 1)

            for f in range(2 * H + 1):
                if f < 2 * H:
                    head_square(f, ua[:, f, 0:N])
                if f:
                    head_rstd(f - 1, 1.0)
            act.wait_ge(conv_pe, 1)
            act.copy(conv_newT[:, :], MP[0:2 * NCONV * PAD, 0, 0:128]).then_inc(conv_act, 1)
            act.wait_ge(conv_act, 2 + NCONV + 1)
            R = NCONV * PAD
            for s, o in ((0, "o_p_gdn_conv"), (1, "o_s_gdn_conv")):
                store(t[o][0, 0].rearrange("i (f p) -> (i f) p", p=128), conv_newT[R * s:R * s + R, :])

            def delta(j, a, P):
                nch = 2 if P == 128 else 1

                def pw(name, jj=j):
                    act.wait_ge(gd_pe, at_step(PE_GD, name, jj))

                def dv(name, jj=j):
                    act.wait_ge(gd_dve, at_step(DVE_GD, name, jj))

                def done(inst):
                    inst.then_inc(gd_act, 1)

                pw("gram")
                act.activation(qe[:, :, 0:P].rearrange("p h n -> p h n"),
                               LP[:, 0, 0:H * P].rearrange("p (h n) -> p h n", h=H), ACT.Exp)
                act.activation(gsm[0:P, 4:12], MP[0:P, 0, 0:8], ACT.Exp)
                done(act.activation(eg[:, 0:nch, :].rearrange("p c h -> p (c h)"), MP[:, 0, 8:8 + 4 * nch], ACT.Exp))
                dv("rows")
                done(act.activation(dec[0:P, :, 0:P], dec[0:P, :, 0:P], ACT.Exp))
                pw("turns")
                done(act.copy(kn[0:P, :, :], MP[0:P, 1, :].rearrange("p (h n) -> p h n", h=H)))
                done(act.copy(Tm[0:P, :, 0:P], MP[0:P, 3, 0:H * P].rearrange("p (h n) -> p h n", h=H)))
                for s in LEVELS[1:]:
                    pw(f"bx{s}")
                    done(act.copy(Xm[0:P, :, 0:P], LP[0:P, 2, 0:H * P].rearrange("p (h n) -> p h n", h=H)))
                pw("uw")
                done(act.copy(wT[:, :, 0:P], MP[:, 3, 0:H * P].rearrange("p (h n) -> p h n", h=H)))
                pw("o1")
                done(act.copy(o_a[:, :, a:a + P], MP[:, 0, 0:H * P].rearrange("p (h n) -> p h n", h=H)))

            for j, a, P in TOK:
                delta(j, a, P)
                if j == TT - 1:
                    act.wait_ge(gd_dve, at_step(DVE_GD, "s1", j))
                    act.wait_ge(gd_pe, at_step(PE_GD, "o1", j))
                    store(t["o_p_gdn_state"][0, 0].rearrange("h k v -> k h v"), S[:, :, :])
                    act.wait_ge(stored, 16 * STORES[0])
                    act.dma_start(S[:, :, :], t["state_gdn"][0, 0].rearrange("h k v -> k h v")).then_inc(s_loaded, 16)
            act.wait_ge(gd_dve, at_step(DVE_GD, "s1", TT))
            store(t["o_s_gdn_state"][0, 0].rearrange("h k v -> k h v"), S[:, :, :])
            act.wait_ge(gd_act, NTOK * len(ACT_GD))
            for h in range(H + 2):
                if h < H:
                    head_square(2 * H + h, o_a[:, h, :])
                if 1 <= h <= H:
                    head_rstd(2 * H + h - 1, 1.0 / HD)
                if h >= 2:
                    act.wait_ge(head_y, h - 1)
                    act.copy(xh[:, h - 2, :], o_a[:, h - 2, :]).then_inc(head_hi, 1)

            def layer_end(l):
                product(f"out{l}")
                act.wait_ge(stored, 16 * STORES[0])
                act.nop().then_inc(arena_free, 1)
                act.wait_ge(mem_loaded, 16 * (l + 1))
                for c in range(MEM // 128):
                    step(act.activation(kv_n[:, c, :], m_rows[:, c, :], ACT.Square, accum_out=mem_ss[:, c:c + 1]))
                settled()
                step(act.activation(mem_rs[:, :], mem_ss[:, :], ACT.Ln, bias=eps_col[:, :], scale=1.0 / D))
                settled()
                act.activation(mem_rs[:, :], mem_rs[:, :], ACT.Exp, scale=-0.5).then_inc(mem_act, 1)
                for k in range(KT):
                    act.wait_ge(mem_pe, KT * l + k + 1)
                    act.activation(mh[:, k, :], MP[:, k % 2, 0:MEM], ACT.Copy, scale=gain(7 + l, k)
                                   ).then_inc(mem_act, 1)
                norm(3 * l + 1)
                product(f"mem{l}")
                act.wait_ge(cx_pe, 2 * l + 1)
                for c in range(MEM // 128):
                    step(act.copy(kv_n[:, c, :].rearrange("p (b n) -> p b n", b=2), MP[:, 2 * c:2 * c + 2, :]))
                settled()
                for i, o in ((0, "o_p_mem_k"), (1, "o_p_mem_v")):
                    store(t[o][l, 0].rearrange("(c p) h d -> p c (h d)", p=128), kv_n[:, :, 512 * i:512 * i + 512])
                act.nop().then_inc(cx_act, 1)
                act.wait_ge(cx_pe, 2 * l + 2)
                act.copy(kxT[:, :, :].rearrange("p (b h) n -> p b (h n)", b=2), LP[:, 0:2, :]).then_inc(cx_act, 1)
                rstd_then_product(3 * l + 1, f"xq{l}")
                attention(f"cross{l}")
                product(f"xo{l}")
                norm(3 * l + 2)
                mlp(l)

            def rstd_then_product(n_, name):
                make_rstd(n_)
                product(name)

            def mlp_block(l, b, last):
                p0, t0, _, _ = LIN[f"mlp{l}"]
                for i in range(4):
                    for m in range(2):
                        k = 2 * i + m
                        T = t0 + 16 * b + k
                        hcount = KT * NB * l + KT * b + k
                        act.wait_ge(product_done, T + 1)
                        if not (isinstance(hcount, int) and hcount < 2):
                            act.wait_ge(hsq_ready, hcount - 1)
                            act.wait_ge(hh_ready, hcount - 1)
                        act.activation(rel[:, k % 2, :].rearrange("p (a n) -> p a n", a=2),
                                       LP[:, 2 * (k % 2):2 * (k % 2) + 2, 0:HALF], ACT.Relu).then_inc(relu_ready, 1)
                        act.wait_ge(relu_ready, hcount + 1)
                        act.activation(hh[:, k, :], rel[:, k % 2, :], ACT.Square).then_inc(hh_ready, 1)
                    split(i % 2, 16 * ((p0 + i) // 2 + 2) + 64 * b)
                for i in range(4):
                    act.wait_ge(product_done, t0 + 16 * b + 8 + 2 * (i + 1))
                    if not (last and i >= 2):
                        split(i % 2, 16 * ((p0 + 4 + i) // 2 + 2) + 64 * b)

            def mlp(l):
                act.wait_ge(stored, 16 * STORES[0])
                p0, t0, _, _ = LIN[f"mlp{l}"]
                make_rstd(3 * l + 2, squared=True)
                mlp_block(l, 0, False)
                end = NB if l == 0 else NB - 1
                with act.Fori(1, end) as b:
                    mlp_block(l, b, False)
                if l == 1:
                    mlp_block(l, NB - 1, True)

            layer_end(0)
            norm(3)
            make_rstd(3)
            product("in_c")
            act.wait_ge(cc_pe, 1)
            act.copy(kcT[:, :, :].rearrange("p c n -> p (c n)"), LP[:, 0, 0:256]).then_inc(cc_act, 1)
            for j, a, P in TOK:
                act.wait_ge(cc_pe, 1 + j + 1)
                if j >= TT - 1:
                    step(act.copy(kc_out[0:P, j % 2, :], MP[0:P, 2 * (j % 2), 0:256]))
                act.copy(v_cn[0:P, j, :], MP[0:P, 2 * (j % 2) + 1, 0:256]).then_inc(cc_act, 1)
                if j >= TT - 1:
                    act.wait_ge(cc_act, 1 + j + 1)
                    for nm_, src in (("k", kc_out[0:P, j % 2, :]), ("v", v_cn[0:P, j, :])):
                        dst = t[f"o_{'p' if j < TT else 's'}_swa_{nm_}"][0, 0]
                        store(dst.rearrange("p h d -> p (h d)"), src)
            attention("swa")
            layer_end(1)
            norm(6, last=True)
            make_rstd(6)
            for j, a, P in TOK:
                act.wait_ge(y_pe, j + 1)
                act.copy(y_rows[0:P, j, :].rearrange("p (b n) -> p b n", b=2), LP[0:P, 2 * (j % 2):2 * (j % 2) + 2, :]
                         ).then_inc(y_act, 1)
                act.wait_ge(y_act, j + 1)
                store(t["o_y_prompt"][0, a:a + P, :] if j < TT else t["o_y_sample"][0], y_rows[0:P, j, :])
            assert STORES[0] == STORES_TOTAL, STORES[0]

        @block.vector
        def _(dve):
            n = [0]

            def step(inst):
                inst.then_inc(dve_step, 1)
                n[0] += 1

            def settled():
                dve.wait_ge(dve_step, n[0])

            def norm(n_, last=False):
                g = n_
                for k in range(KT):
                    if not last:
                        dve.wait_ge(xh_ready, KT * n_ + k + 1)
                        dve.wait_ge(x_done, NORM_BASE[n_] + k + 1)
                        dve.scalar_tensor_tensor(out=xl[:, k, :], in0=x[:, k, :], scalar=gain(g, k),
                                                 in1=xh[:, k, :].bitcast(f32), op0=ALU.mult, op1=ALU.subtract
                                                 ).then_inc(xs_ready, 1)
                    dve.wait_ge(sq_ready, KT * n_ + k + 1)
                    if k:
                        dve.wait_ge(sq_used, KT * n_ + k)
                        dve.tensor_tensor(acc[:, :], acc[:, :], sq[:, k % 2, :], ALU.add).then_inc(sq_used, 1)
                    else:
                        dve.tensor_copy(acc[:, :], sq[:, 0, :]).then_inc(sq_used, 1)

            def banks(T):
                s = T % 2
                return LP[:, 2 * s:2 * s + 2, 0:HALF]

            def two(v):
                return v.rearrange("p (a n) -> p a n", a=2)

            def residual_product(name):
                _, t0, panels, tpp = LIN[name]
                with dve.Fori(0, KT // 4) as i:
                    for m in range(4):
                        dve.wait_ge(product_done, t0 + 4 * i + m + 1)
                        dst = x[:, bass.ds(4 * i + m, 1), :].rearrange("p o (a n) -> p (o a) n", a=2)
                        dve.tensor_tensor(dst, banks(m), dst, ALU.add).then_inc(x_done, 1)
                        dve.wait_ge(x_done, NORM_BASE[RES[name]] + 4 * i + m + 1)
                        dve.nop().then_inc(drained, 1)

            def attention(name):
                u0, count = GROUP[name]

                def first(u):
                    U = UNITS[u]
                    P, nk, s = U["P"], sum(n_ for _, n_ in U["keys"]), u % 2
                    dve.wait_ge(sc_ready, u + 1)
                    if u >= 2:
                        dve.wait_ge(tr_ready, u - 1)
                    buf = U["S"][0:P, s, 0:nk]
                    parts = [(0, min(nk, 512), 2 * s)] + ([(512, nk, 2 * s + 1)] if nk > 512 else [])
                    kind = U["bias"]
                    if kind is None:
                        step(dve.tensor_reduce(rr[0:P, s:s + 1], LP[0:P, 2 * s, 0:nk], AX.X, ALU.max))
                        settled()
                        dve.tensor_scalar(nm[0:P, s:s + 1], rr[0:P, s:s + 1], -U["scale"], None, ALU.mult
                                          ).then_inc(nm_ready, 1)
                        return
                    for lo_, hi_, b in parts:
                        if kind[0] == "fox":
                            inst = dve.scalar_tensor_tensor(
                                out=buf[:, lo_:hi_], in0=LP[0:P, b, 0:hi_ - lo_], scalar=U["scale"],
                                in1=nF[0:P, kind[1], lo_:hi_], op0=ALU.mult, op1=ALU.add)
                        else:
                            inst = dve.scalar_tensor_tensor(
                                out=buf[:, lo_:hi_], in0=kind[2], scalar=-kind[3],
                                in1=LP[0:P, b, 0:hi_ - lo_], op0=ALU.mult, op1=ALU.add)
                        step(inst)
                    settled()
                    if U["diag"]:
                        w = U["diag"]
                        step(dve.tensor_tensor(buf[:, nk - w:nk], buf[:, nk - w:nk], diag_mask[0:P, 0:w], ALU.add))
                        settled()
                    if kind[0] == "fox":
                        dve.tensor_reduce(nm[0:P, s:s + 1], buf, AX.X, ALU.max, negate=True).then_inc(nm_ready, 1)
                    else:
                        step(dve.tensor_reduce(rr[0:P, s:s + 1], buf, AX.X, ALU.max))
                        settled()
                        dve.tensor_scalar(nm[0:P, s:s + 1], rr[0:P, s:s + 1], sinks[0:P, kind[1]:kind[1] + 1], -1.0,
                                          ALU.max, ALU.mult).then_inc(nm_ready, 1)

                def second(u):
                    U = UNITS[u]
                    P, nk, s = U["P"], sum(n_ for _, n_ in U["keys"]), u % 2
                    dve.wait_ge(ex_ready, u + 1)
                    if U["bias"] and U["bias"][0] == "swa":
                        step(dve.tensor_tensor(rs[0:P, s:s + 1], rs[0:P, s:s + 1], es[0:P, s:s + 1], ALU.add))
                        settled()
                    step(dve.reciprocal(rr[0:P, s:s + 1], rs[0:P, s:s + 1]))
                    settled()
                    buf = U["S"][0:P, s, 0:nk]
                    dve.tensor_scalar(buf, buf, rr[0:P, s:s + 1], None, ALU.mult).then_inc(p_ready, 1)

                def low(u):
                    U = UNITS[u]
                    dve.wait_ge(oh_ready, u + 1)
                    dve.tensor_tensor(U["lo"], MP[0:U["D"], 2 + u % 2, 0:U["P"]], U["hi"].bitcast(f32), ALU.subtract
                                      ).then_inc(ol_ready, 1)

                for i in range(count + 2):
                    if i < count:
                        first(u0 + i)
                    if 1 <= i <= count:
                        second(u0 + i - 1)
                    if i >= 2:
                        low(u0 + i - 2)

            step(dve.memset(one_col[:, :], 1.0))
            dve.wait_ge(mask_done, MASKS)
            for m, w in ((dist_p, 256), (dist_s, WIN + NS)):
                P = m.shape[0]
                step(dve.tensor_scalar(sq[0:P, 0, 0:w], m[:, :], -1.0, None, ALU.mult))
                settled()
                step(dve.tensor_tensor(m[:, :], m[:, :], sq[0:P, 0, 0:w], ALU.max))
                settled()
            for k in range(KT):
                dve.wait_ge(x_turned, k + 1)
                dve.tensor_copy(x[:, k, 0:NPT], LP[:, 2 * (k % 2), 0:NPT])
                dve.tensor_copy(x[:, k, NPT:N], LP[:, 2 * (k % 2) + 1, 0:NS]).then_inc(x_done, 1)
            dve.wait_ge(param_turned, 1)
            dve.wait_ge(param_ready, 1)
            dve.wait_ge(x_turned, KT)
            step(dve.memset(ua[:, :, 0:PAD], 0.0))
            dve.tensor_copy(ua[:, :, PAD + NPT:PAD + NPT + PAD].rearrange("p f i -> p i f"),
                            MP[:, 1, 0:PAD * NCONV].rearrange("p (i f) -> p i f", i=PAD)).then_inc(param_ready, 1)
            norm(0)
            dve.wait_ge(gate_act, 1)
            dve.tensor_tensor(wgl[:, :, :], w_gate[:, :, :], wgh[:, :, :].bitcast(f32), ALU.subtract
                              ).then_inc(gate_dve, 1)
            dve.wait_ge(rstd_ready, 1)
            ta = LIN["in_a"][1]
            with dve.Fori(0, NCONV // 4) as i:
                for m in range(4):
                    dve.wait_ge(product_done, ta + 4 * i + m + 1)
                    b = 2 * (m % 2)
                    row = ua[:, bass.ds(4 * i + m, 1), :].rearrange("p o n -> p (o n)")
                    dve.tensor_tensor(row[:, PAD:PAD + HALF], LP[:, b, 0:HALF], rstd[:, 0:HALF], ALU.mult)
                    dve.tensor_tensor(row[:, PAD + HALF:PAD + NPT], LP[:, b + 1, 0:NPT - HALF], rstd[:, HALF:NPT],
                                      ALU.mult)
                    dve.tensor_tensor(row[:, 2 * PAD + NPT:UPAD], LP[:, b + 1, NPT - HALF:HALF], rstd[:, NPT:N],
                                      ALU.mult).then_inc(drained, 1)
            for m in range(H):
                dve.wait_ge(product_done, ta + NCONV + m + 1)
                dve.tensor_tensor(two(z[:, m, :]), banks(m), two(rstd[:, :]), ALU.mult).then_inc(drained, 1)
            tb = LIN["in_b"][1]
            for n_, dst in enumerate((qb_f, kb_f, vb_f)):
                for m in range(H):
                    dve.wait_ge(product_done, tb + H * n_ + m + 1)
                    dve.tensor_tensor(two(dst[:, m, :]), banks(m), two(rstd[:, :]), ALU.mult).then_inc(drained, 1)
            dve.wait_ge(gate_pe, 1)
            dve.tensor_tensor(two(gT[:, :]), MP[0:GATES, 0:2, 0:HALF], two(rstd[0:GATES, :]), ALU.mult
                              ).then_inc(gate_dve, 1)
            dve.wait_ge(gate_act, 3)
            dve.wait_ge(par_loaded, 16 * 16)

            def bc(i):
                return gate_par[:, i:i + 1, :].to_broadcast([128, NTOK, H])

            step(dve.tensor_tensor(G[:, :, H:2 * H], G[:, :, H:2 * H], bc(1), ALU.add))
            step(dve.tensor_tensor(G[:, :, 2 * H:3 * H], G[:, :, 2 * H:3 * H], bc(2), ALU.add))
            settled()
            step(dve.tensor_scalar(G[:, :, 0:H], G[:, :, 0:H], -1.0, None, ALU.mult))
            step(dve.tensor_scalar(G[:, :, 2 * H:3 * H], G[:, :, 2 * H:3 * H], -1.0, None, ALU.mult))
            settled()
            dve.tensor_scalar(Ga[:, :, :], G[:, :, :], -1.0, None, ALU.mult).then_inc(gate_dve, 1)
            dve.wait_ge(gate_dve, 3)
            dve.tensor_tensor(Gb[:, :, :], G[:, :, :], Ga[:, :, :], ALU.min).then_inc(gate_dve, 1)
            step(dve.tensor_scalar(G[:, :, :], G[:, :, :], 0.0, None, ALU.max))
            settled()
            dve.wait_ge(gate_act, 6)
            step(dve.tensor_tensor(Ga[:, :, :], G[:, :, :], Gb[:, :, :], ALU.add))
            settled()
            step(dve.tensor_scalar(G[:, :, 2 * H:3 * H], Ga[:, :, 2 * H:3 * H], -1.0, None, ALU.mult))
            step(dve.tensor_tensor(Gb[:, :, H:2 * H], Ga[:, :, H:2 * H], bc(0), ALU.mult))
            settled()
            step(dve.tensor_scalar(Gb[:, :, H:2 * H], Gb[:, :, H:2 * H], -1.0, None, ALU.mult))
            dve.tensor_copy(Gb[:, :, 0:H], Ga[:, :, 0:H]).then_inc(gate_dve, 2)
            attention("fox_p")
            attention("fox_s")
            dve.tensor_copy(conv_new[:, 0, :, :], ua[:, :, NPT:NPT + PAD].rearrange("p f i -> p i f"))
            dve.tensor_copy(conv_new[:, 1, :, :], ua[:, :, UPAD - PAD:UPAD].rearrange("p f i -> p i f")
                            ).then_inc(conv_dve, 2)
            for f in range(NCONV):
                if f >= 2:
                    dve.wait_ge(conv_act, 2 + f - 1)
                b, e = sq[:, f % 2, 0:NPT], sq[:, f % 2, NPT:N]
                for i in range(CW):
                    if i == 0:
                        dve.tensor_scalar(b, ua[:, f, 0:NPT], conv_w(0, f), None, ALU.mult)
                        inst = dve.tensor_scalar(e, ua[:, f, PAD + NPT:PAD + NPT + NS], conv_w(0, f), None, ALU.mult)
                    else:
                        dve.wait_ge(conv_dve, 2 + CW * f + i)
                        dve.scalar_tensor_tensor(out=b, in0=ua[:, f, i:i + NPT], scalar=conv_w(i, f), in1=b,
                                                 op0=ALU.mult, op1=ALU.add)
                        inst = dve.scalar_tensor_tensor(out=e, in0=ua[:, f, PAD + NPT + i:PAD + NPT + i + NS],
                                                        scalar=conv_w(i, f), in1=e, op0=ALU.mult, op1=ALU.add)
                    inst.then_inc(conv_dve, 1)
            for f in range(2 * H):
                dve.wait_ge(head_exp, f + 1)
                dve.scalar_tensor_tensor(out=ua[:, f, 0:N], in0=ua[:, f, 0:N], scalar=HD ** -0.5 if f < H else 1.0,
                                         in1=(rstd, acc)[f % 2][:, :], op0=ALU.mult, op1=ALU.mult
                                         ).then_inc(head_mul, 1)
            dve.wait_ge(gate_act, 7)
            dve.memset(S[:, :, :], 0.0).then_inc(s_zero, 1)

            def delta(j, a, P):
                nch = 2 if P == 128 else 1
                C = P // nch

                def pw(name, jj=j):
                    dve.wait_ge(gd_pe, at_step(PE_GD, name, jj))

                def aw(name, jj=j):
                    dve.wait_ge(gd_act, at_step(ACT_GD, name, jj))

                def done(inst):
                    inst.then_inc(gd_dve, 1)

                def own(name):
                    dve.wait_ge(gd_dve, at_step(DVE_GD, name, j))

                def heads(v):
                    return v.rearrange("p (h n) -> p h n", h=H)

                def over(m):
                    return m.rearrange("p (o n) -> p o n", o=1).to_broadcast([P, H, P])

                pw("gram")
                aw("exps")
                step(dve.tensor_copy(gsm[0:P, 0:4], MP[0:P, 0, 0:4]))
                settled()
                for h in range(H):
                    inst = dve.tensor_scalar(dec[0:P, h, 0:P], LP[0:P, 0, h * P:h * P + P], gsm[0:P, h:h + 1], 0.0,
                                             ALU.subtract, ALU.min)
                done(inst)
                aw("dec")
                step(dve.tensor_tensor(LT[0:P, :, 0:P], heads(LP[0:P, 2, 0:H * P]), dec[0:P, :, 0:P], ALU.mult))
                step(dve.tensor_tensor(AT[0:P, :, 0:P], heads(LP[0:P, 3, 0:H * P]), dec[0:P, :, 0:P], ALU.mult))
                settled()
                step(dve.tensor_tensor(LT[0:P, :, 0:P], LT[0:P, :, 0:P], heads(LP[0:P, 1, 0:H * P]), ALU.mult))
                step(dve.tensor_tensor(AT[0:P, :, 0:P], AT[0:P, :, 0:P], over(chunk_upper[0:P, 0:P]), ALU.mult))
                settled()
                done(dve.tensor_tensor(LT[0:P, :, 0:P], LT[0:P, :, 0:P], over(chunk_strict[0:P, 0:P]), ALU.mult))
                own("lt")
                step(dve.tensor_tensor(BT[0:P, :, 0:P], LT[0:P, :, 0:P], over(level[0:P, 0, 0:P]), ALU.mult))
                settled()
                done(dve.tensor_tensor(TmT[0:P, :, 0:P], over(ident[0:P, 0:P]), BT[0:P, :, 0:P], ALU.subtract))
                aw("kn")
                pw("turns")
                step(dve.tensor_tensor(gsm[0:P, 12:16], Gb[0:P, j, 0:H], gsm[0:P, 4:8], ALU.mult))
                settled()
                for h in range(H):
                    dve.tensor_scalar(kbe[0:P, h, :], kn[0:P, h, :], gsm[0:P, 12 + h:13 + h], None, ALU.mult)
                    dve.tensor_scalar(kd[0:P, h, :], kn[0:P, h, :], gsm[0:P, 8 + h:9 + h], None, ALU.mult)
                    dve.tensor_scalar(vbt[0:P, h, :], MP[0:P, 2, 128 * h:128 * h + 128], Gb[0:P, j, h:h + 1], None,
                                      ALU.mult)
                done(dve.tensor_tensor(qe[:, :, 0:P], qe[:, :, 0:P], ua[:, 0:H, a:a + P], ALU.mult))
                own("tt1")
                for n_, s in enumerate(LEVELS):
                    if s == 1:
                        continue
                    if s > 2:
                        pw(f"bx{s // 2}")
                    done(dve.tensor_tensor(BT[0:P, :, 0:P], LT[0:P, :, 0:P], over(level[0:P, n_, 0:P]), ALU.mult))
                    pw(f"delta{s}")
                    if s == 2:
                        aw("t_copy")
                    dve.tensor_tensor(Tm[0:P, :, 0:P], Tm[0:P, :, 0:P], heads(LP[0:P, 3, 0:H * P]), ALU.subtract)
                    done(dve.tensor_tensor(TmT[0:P, :, 0:P], TmT[0:P, :, 0:P], heads(LP[0:P, 1, 0:H * P]),
                                           ALU.subtract))
                    own(f"t{s}")
                pw("uw")
                done(dve.tensor_copy(um[0:P, :, :], heads(MP[0:P, 2, :])))
                own("u")
                for c in range(2):
                    if c >= nch:
                        dve.nop().then_inc(gd_dve, 2)
                        continue
                    r = slice(c * C, c * C + C)
                    pw(f"ws{c}")
                    done(dve.tensor_tensor(vnew[r, :, :], um[r, :, :], heads(LP[r, 0, :]), ALU.subtract))
                    pw(f"o{c}")
                    for h in range(H):
                        inst = dve.scalar_tensor_tensor(out=S[:, h, :], in0=S[:, h, :], scalar=eg[:, c, h:h + 1],
                                                        in1=MP[:, 1, 128 * h:128 * h + 128], op0=ALU.mult, op1=ALU.add)
                    done(inst)
                    own(f"s{c}")

            for j, a, P in TOK:
                if j == TT:
                    dve.wait_ge(s_loaded, 16)
                delta(j, a, P)
            for h in range(H + 1):
                if h < H:
                    f = 2 * H + h
                    dve.wait_ge(head_exp, f + 1)
                    dve.scalar_tensor_tensor(out=o_a[:, h, :], in0=o_a[:, h, :], scalar=column(ONORM),
                                             in1=(rstd, acc)[f % 2][:, :], op0=ALU.mult, op1=ALU.mult
                                             ).then_inc(head_mul, 1)
                    dve.wait_ge(head_mul, f + 1)
                    dve.tensor_tensor(o_a[:, h, :], o_a[:, h, :], z[:, h, :], ALU.mult).then_inc(head_y, 1)
                if h:
                    dve.wait_ge(head_hi, h)
                    dve.tensor_tensor(xl[:, h - 1, :], o_a[:, h - 1, :], xh[:, h - 1, :].bitcast(f32), ALU.subtract
                                      ).then_inc(low_done, 1)

            def layer_end(l):
                residual_product(f"out{l}")
                dve.wait_ge(mem_act, (KT + 1) * l + 1)
                for c in range(MEM // 128):
                    inst = dve.tensor_scalar(m_rows[:, c, :], m_rows[:, c, :], mem_rs[:, c:c + 1], None, ALU.mult)
                inst.then_inc(mem_dve, 1)
                for k in range(KT):
                    dve.wait_ge(mem_act, (KT + 1) * l + k + 2)
                    dve.scalar_tensor_tensor(out=ml[:, k, :], in0=MP[:, k % 2, 0:MEM], scalar=gain(7 + l, k),
                                             in1=mh[:, k, :].bitcast(f32), op0=ALU.mult, op1=ALU.subtract
                                             ).then_inc(mem_dve, 1)
                norm(3 * l + 1)
                _, t0, panels, tpp = LIN[f"mem{l}"]
                with dve.Fori(0, KT // 4) as i:
                    for m in range(4):
                        dve.wait_ge(product_done, t0 + 4 * i + m + 1)
                        dve.tensor_copy(kvT[:, bass.ds(4 * i + m, 1), :].rearrange("p o n -> p (o n)"),
                                        LP[:, 2 * (m % 2), 0:MEM]).then_inc(drained, 1)
                dve.wait_ge(rstd_ready, 3 * l + 2)
                t0 = LIN[f"xq{l}"][1]
                for m in range(H):
                    dve.wait_ge(product_done, t0 + m + 1)
                    dve.tensor_tensor(two(q_x[:, m, :]), banks(m), two(rstd[:, :]), ALU.mult).then_inc(drained, 1)
                attention(f"cross{l}")
                residual_product(f"xo{l}")
                norm(3 * l + 2)
                mlp(l)

            def mlp_block(l, b):
                t0, d0 = LIN[f"mlp{l}"][1], DRAINED[f"mlp{l}"]
                for k in range(KT):
                    hcount = KT * NB * l + KT * b + k
                    dve.wait_ge(relu_ready, hcount + 1)
                    if not (isinstance(hcount, int) and hcount < 2):
                        dve.wait_ge(h_ready, hcount - 1)
                    dve.tensor_tensor(hsq[:, k % 2, :], rel[:, k % 2, :], rel[:, k % 2, :], ALU.mult
                                      ).then_inc(hsq_ready, 1)
                    dve.wait_ge(hsq_ready, hcount + 1)
                    dve.wait_ge(hh_ready, hcount + 1)
                    dve.tensor_tensor(hl[:, k, :], hsq[:, k % 2, :], hh[:, k, :].bitcast(f32), ALU.subtract
                                      ).then_inc(h_ready, 1)
                base = NORM_BASE[3 * l + 2]
                for k in range(KT):
                    dve.wait_ge(product_done, t0 + 16 * b + KT + k + 1)
                    count = KT * NB * l + KT * b + k
                    if not (isinstance(count, int) and count < 2):
                        dve.wait_ge(x_done, base + KT + KT * b + k - 1)
                    dve.tensor_tensor(two(dtmp[:, k % 2, :]), banks(k), two(rstd[:, :]), ALU.mult
                                      ).then_inc(drained, 1)
                    dve.wait_ge(drained, d0 + KT * b + k + 1)
                    dve.tensor_tensor(x[:, k, :], x[:, k, :], dtmp[:, k % 2, :], ALU.add).then_inc(x_done, 1)

            def mlp(l):
                dve.wait_ge(rstd_ready, 3 * l + 3)
                mlp_block(l, 0)
                with dve.Fori(1, NB) as b:
                    mlp_block(l, b)

            layer_end(0)
            norm(3)
            dve.wait_ge(rstd_ready, 4)
            tc = LIN["in_c"][1]
            for m in range(12):
                dve.wait_ge(product_done, tc + m + 1)
                if m >= 8:
                    dst = (k_c, v_c)[(m - 8) // 2][:, m % 2, :]
                    dve.tensor_tensor(two(dst), banks(m), two(rstd[:, :]), ALU.mult).then_inc(drained, 1)
                    continue
                kv = m // 2
                o = (kv % 2) * 64
                for h in (2 * m, 2 * m + 1):
                    slot, ho = (h // 8) * 4 + h % 4, (h % 2) * 64
                    inst = dve.scalar_tensor_tensor(
                        out=two(q_c[o:o + 64, slot, :]), in0=LP[ho:ho + 64, 2 * (m % 2):2 * (m % 2) + 2, 0:HALF],
                        scalar=HDC ** -0.5, in1=two(rstd[ho:ho + 64, :]), op0=ALU.mult, op1=ALU.mult)
                inst.then_inc(drained, 1)
            attention("swa")
            layer_end(1)
            norm(6, last=True)
            dve.wait_ge(rstd_ready, 7)
            for k in range(KT):
                dve.scalar_tensor_tensor(out=yT[:, k, :], in0=x[:, k, :], scalar=gain(6, k), in1=rstd[:, :],
                                         op0=ALU.mult, op1=ALU.mult).then_inc(y_dve, 1)



def kernel(**inputs):
    import numpy as _np
    import concourse.bacc as _bacc
    from concourse import mybir as _mybir
    from concourse.bass_utils import run_bass_kernel_spmd as _run

    nc = _bacc.Bacc("TRN2", target_bir_lowering=False, num_devices=1)
    arrays, t = {}, {}
    for name, value in inputs.items():
        a = _np.ascontiguousarray(value)
        arrays[f"in_{name}"] = a
        t[name] = nc.dram_tensor(f"in_{name}", a.shape, _mybir.dt.from_np(a.dtype), kind="ExternalInput").ap()
    s = {k: tuple(v.shape) for k, v in inputs.items()}
    _, np_, d = s["x_prompt"]
    ns = s["x_sample"][1]
    _, _, h, dk, dv = s["state_gdn"]
    cw, cdim = s["state_gdn_conv"][2:]
    win, hkv, hdc = s["cache_swa_k"][2:]
    depth, _, mem, hx, hdx = s["cache_mem_k"]
    outs = [("y_prompt", (1, np_, d)), ("y_sample", (1, ns, d)),
            ("p_gdn_state", (1, 1, h, dk, dv)), ("p_gdn_conv", (1, 1, cw, cdim)),
            ("p_fox_k", (1, 1, np_, h, dk)), ("p_fox_v", (1, 1, np_, h, dk)), ("p_fox_logf", (1, 1, np_, h)),
            ("p_swa_k", (1, 1, win, hkv, hdc)), ("p_swa_v", (1, 1, win, hkv, hdc)),
            ("p_mem_k", (depth, 1, mem, hx, hdx)), ("p_mem_v", (depth, 1, mem, hx, hdx)),
            ("s_gdn_state", (1, 1, h, dk, dv)), ("s_gdn_conv", (1, 1, cw, cdim)),
            ("s_fox_k", (1, 1, ns, h, dk)), ("s_fox_v", (1, 1, ns, h, dk)), ("s_fox_logf", (1, 1, ns, h)),
            ("s_swa_k", (1, 1, ns, hkv, hdc)), ("s_swa_v", (1, 1, ns, hkv, hdc))]
    for name, shape in outs:
        t[f"o_{name}"] = nc.dram_tensor(f"o_{name}", shape, _mybir.dt.float32, kind="ExternalOutput").ap()
    build_program(nc, t)
    r = _run(nc, [arrays], core_ids=[0])
    return tuple(r.results[0][f"o_{name}"] for name, _ in outs)
```

```python
import concourse.bass as bass
from concourse import mybir
from contextlib import ExitStack


def build_program(nc, t):
    f32, f32r = mybir.dt.float32, mybir.dt.float32r
    ALU, ACT, AX = mybir.AluOpType, mybir.ActivationFunctionType, mybir.AxisListType

    D = t["x_prompt"].shape[2]
    NPT = t["x_prompt"].shape[1]
    NS = t["x_sample"].shape[1]
    N = NPT + NS
    HALF = N // 2
    KT = D // 128
    H = t["state_gdn"].shape[2]
    HD = 128
    NCONV = t["state_gdn_conv"].shape[3] // 128
    CW = t["conv_w_a"].shape[1]
    PAD = CW - 1
    CH = 64
    PAST = t["cache_fox_k"].shape[2]
    WIN = t["cache_swa_k"].shape[2]
    HKV, HDC = t["cache_swa_k"].shape[3], t["cache_swa_k"].shape[4]
    HQ = t["sinks_c"].shape[1]
    MEM = t["mem_prompt"].shape[1]
    DFF = t["w_up"].shape[2]
    NB = DFF // D
    TT = NPT // 128
    NTOK = TT + 1
    EPS = 1e-6
    BIG = 1e30
    TOK = [(j, 128 * j, 128) for j in range(TT)] + [(TT, NPT, NS)]
    UPAD = PAD + NPT + PAD + NS
    GATES = 3 * H

    LIN = {}
    order = [("in_a", 8, 2), ("in_b", 6, 2)]
    for l in range(2):
        if l == 1:
            order += [("in_c", 6, 2)]
        order += [(f"out{l}", 4, 2), (f"mem{l}", 4, 2), (f"xq{l}", 2, 2), (f"xo{l}", 2, 4)]
        order += [(f"mlp{l}", 8 * NB, 2)]
    p = q = d = 0
    DRAINED = {}
    for name, panels, tpp in order:
        LIN[name] = (p, q, panels, tpp)
        DRAINED[name] = d
        p, q, d = p + panels, q + panels * tpp, d + panels * tpp // (2 if name[:3] == "mlp" else 1)
    PANELS = p

    def last_tile(name):
        return DRAINED[name] + LIN[name][2] * LIN[name][3]

    PER_LAYER = (2 + NB) * KT
    NORM_BASE = [0, KT, 2 * KT, PER_LAYER, PER_LAYER + KT, PER_LAYER + 2 * KT, 2 * PER_LAYER]
    RES = {"out0": 1, "xo0": 2, "out1": 4, "xo1": 5}
    MASKS = 15 + 6 + 3 + 6 + 6 + 2 + 6 + 2
    GATE_LOGF = 6
    STORES_TOTAL = 2 + 2 * NTOK + 2 + 2 + 4 + 4 + NTOK

    ctx = ExitStack()
    with ctx:
        def sem(name):
            return ctx.enter_context(nc.semaphore(name))

        cursor = [(nc.sbuf_base + 31) // 32 * 32]

        def place(name, shape, dt=f32, at=None):
            size = 4
            for n in shape[1:]:
                size *= n
            size = (size + 31) // 32 * 32
            if at is None:
                at = cursor[0]
                cursor[0] += size
            return nc.alloc_sbuf_tensor_at(name, shape, dt, offset=at)

        x = place("x", [128, KT, N])
        xh_at = cursor[0]
        xh = place("xh", [128, KT, N], f32r)
        xl_at = cursor[0]
        xl = place("xl", [128, KT, N], f32r)
        stage = [place(f"stage{s}", [128, 2048]) for s in range(2)]
        wh = [place(f"wh{s}", [128, 2048], f32r) for s in range(2)]
        wl = [place(f"wl{s}", [128, 2048], f32r) for s in range(2)]
        rstd = place("rstd", [128, N])
        acc_at = cursor[0]
        acc = place("acc", [128, N])
        sq_at = cursor[0]
        sq = place("sq", [128, 2, N])
        probs = place("probs", [128, 3, N], at=acc_at)
        ident = place("ident", [128, 128])
        ones = place("ones", [128, 128])
        upper = place("upper", [128, NPT])
        chunk_upper = place("chunk_upper", [128, 128])
        chunk_later = place("chunk_later", [128, 128])
        chunk_mask = place("chunk_mask", [128, 128])
        chunk_rows = place("chunk_rows", [128, 2, 128])
        LEVELS = [1, 2, 4, 8, 16, 32]
        level = place("level", [128, len(LEVELS), 128])
        diag_mask = place("diag_mask", [128, 128])
        dist_p = place("dist_p", [128, 256])
        dist_s = place("dist_s", [NS, WIN + NS])
        NROW = 9 * KT + CW * NCONV + 1
        cols = place("cols", [128, NROW])
        gate_par = place("gate_par", [128, 3, H])
        sinks = place("sinks", [128, HQ])
        eps_col = place("eps_col", [128, 1])
        one_col = place("one_col", [128, 1])
        nm = place("nm", [128, 2, 2])
        rs = place("rs", [128, 2, 2])
        rr = place("rr", [128, 2, 2])
        es = place("es", [128, 2, 2])
        neg_sinks = place("neg_sinks", [128, HQ])
        mem_ss = place("mem_ss", [128, 2])
        mem_rs = place("mem_rs", [128, 2])
        ARENA = cursor[0]
        peak = [ARENA]

        def arena(*parts):
            out, at = [], ARENA
            for part in parts:
                name, shape = part[0], part[1]
                dt = part[2] if len(part) > 2 else f32
                out.append(place(name, shape, dt, at=at))
                size = 4
                for n in shape[1:]:
                    size *= n
                at += (size + 31) // 32 * 32
            peak[0] = max(peak[0], at)
            return out

        x_rows, par_rows, conv_rows = arena(("x_rows", [128, NTOK, D]), ("par_rows", [NROW, 128]),
                                            ("conv_rows", [PAD * NCONV, 128]))
        (ua, z, vb_f, kb_f, qb_f, vb_n, nF, PT0) = arena(
            ("ua", [128, NCONV, UPAD]), ("z", [128, H, N]),
            ("vb_f", [128, H, N]), ("kb_f", [128, H, N]), ("qb_f", [128, H, N]),
            ("vb_n", [128, NTOK, H * HD]), ("nF", [128, H, N]),
            ("PT0", [128, 2, 5 * 128]))
        gates_at = peak[0] - 4 * 2 * 5 * 128
        size = 4 * KT * GATES
        w_gate = place("w_gate", [128, KT, GATES], at=gates_at)
        wgh = place("wgh", [128, KT, GATES], f32r, at=gates_at + size)
        wgl = place("wgl", [128, KT, GATES], f32r, at=gates_at + 2 * size)
        k_out = place("k_out", [128, TT, H * HD], at=peak[0] - 4 * (2 * 5 * 128 + H * N))
        conv_new = place("conv_new", [128, 2, PAD, NCONV], at=gates_at + 3 * size)
        conv_newT = place("conv_newT", [2 * NCONV * PAD, 128], at=gates_at + 3 * size + 512)
        gT = place("gT", [GATES, N], at=acc_at)
        at = ARENA + 4 * (NCONV * UPAD + H * N)
        at = (at + 31) // 32 * 32
        ka_at = at
        kpT = place("kpT", [128, H, PAST], at=xh_at)
        kp_rows = place("kp_rows", [128, PAST // 128, H * HD], at=xh_at + 4 * H * PAST)
        vp_n = place("vp_n", [128, PAST // 128, H * HD], at=xl_at)
        k_out_s = place("k_out_s", [NS, H * HD], at=peak[0])
        head_squares = place("head_squares", [128, N], at=peak[0] + 4 * H * HD)
        gates_start = peak[0] + 4 * 2 * N
        after_gates = [gates_start]

        def more(name, shape, dt=f32):
            tt_ = place(name, shape, dt, at=after_gates[0])
            size = 4
            for n in shape[1:]:
                size *= n
            after_gates[0] += (size + 31) // 32 * 32
            return tt_

        G = more("G", [128, NTOK, GATES])
        Ga = more("Ga", [128, NTOK, GATES])
        Gb = more("Gb", [128, NTOK, GATES])
        lf_past = more("lf_past", [128, PAST // 128, H])
        peak[0] = max(peak[0], after_gates[0])
        gat = [ka_at]

        def gbuf(name, shape):
            b = place(name, shape, f32, at=gat[0])
            size = 4
            for n in shape[1:]:
                size *= n
            gat[0] += (size + 31) // 32 * 32
            return b

        o_a = gbuf("o_a", [128, H, N])
        LT, Tm, TmT, Xm, BT, kn, vbt, kbe, vnew = [
            gbuf(n, [128, H, 128]) for n in ("LT", "Tm", "TmT", "Xm", "BT", "kn", "vbt", "kbe", "vnew")]
        dec = Xm
        AT, um, wT, qe, kd = [gbuf(n, [128, 2, H, 128]) for n in ("AT", "um", "wT", "qe", "kd")]
        S = gbuf("S", [128, 3, H, 128])
        gsm = gbuf("gsm", [128, 2, 16])
        eg = gbuf("eg", [128, 2, 2, H])
        assert gat[0] <= gates_start
        (q_c, k_c, v_c, v_cn, kc_out, kc_rows, vc_rows, kcT, PTC) = arena(
            ("q_c", [128, 8, N]), ("k_c", [128, 2, N]), ("v_c", [128, 2, N]),
            ("v_cn", [128, NTOK, HKV * HDC]), ("kc_out", [128, 2, HKV * HDC]),
            ("kc_rows", [128, HKV * HDC]), ("vc_rows", [128, HKV * HDC]), ("kcT", [128, 2, WIN]),
            ("PTC", [128, 2, 5 * 128]))
        (m_rows, mh, ml, kvT, kv_n, q_x, kx_rows, vx_rows, kxT, PTX) = arena(
            ("m_rows", [128, 2, D]), ("mh", [128, KT, MEM], f32r), ("ml", [128, KT, MEM], f32r),
            ("kvT", [128, KT, MEM]), ("kv_n", [128, 2, D]), ("q_x", [128, H, N]),
            ("kx_rows", [128, 2, H * HD]), ("vx_rows", [128, 2, H * HD]), ("kxT", [128, H, MEM]),
            ("PTX", [128, 2, 5 * 128]))
        hh, hl, rel, hsq, dtmp, rstd2 = arena(
            ("hh", [128, KT, N], f32r), ("hl", [128, KT, N], f32r), ("rel", [128, 2, N]),
            ("hsq", [128, 2, N]), ("dtmp", [128, 2, N]), ("rstd2", [128, N]))
        y_rows, yT = arena(("y_rows", [128, NTOK, D]), ("yT", [128, KT, N]))
        assert peak[0] <= nc.sbuf_usable_end, (peak[0], nc.sbuf_usable_end)

        LP = ctx.enter_context(nc.psum_tensor("LP", [128, 4, 512], f32))
        MP = ctx.enter_context(nc.psum_tensor("MP", [128, 4, 512], f32))

        def column(row):
            return cols[:, row:row + 1]

        def gain(norm, k):
            return column(norm * KT + k)

        def conv_w(i, f):
            return column(9 * KT + i * NCONV + f)

        ONORM = 9 * KT + CW * NCONV

        w_loaded = [sem(f"w_loaded{s}") for s in range(2)]
        w_hi = sem("w_hi")
        w_lo = sem("w_lo")
        product_done = sem("product_done")
        drained = sem("drained")
        x_loaded, par_loaded, mask_done = sem("x_loaded"), sem("par_loaded"), sem("mask_done")
        param_turned, param_ready = sem("param_turned"), sem("param_ready")
        x_turned, x_done = sem("x_turned"), sem("x_done")
        sq_ready, sq_used, xh_ready, xs_ready = sem("sq_ready"), sem("sq_used"), sem("xh_ready"), sem("xs_ready")
        stat_done, rstd_ready = sem("stat_done"), sem("rstd_ready")
        act_step, dve_step, pe_step = sem("act_step"), sem("dve_step"), sem("pe_step")
        stored = sem("stored")
        relu_ready, hh_ready, hsq_ready, h_ready, down_mul = (sem("relu_ready"), sem("hh_ready"),
                                                              sem("hsq_ready"), sem("h_ready"), sem("down_mul"))
        gate_pe, gate_act, gate_dve = sem("gate_pe"), sem("gate_act"), sem("gate_dve")
        conv_act, conv_dve = sem("conv_act"), sem("conv_dve")
        turn_pe, turn_act = sem("turn_pe"), sem("turn_act")
        sc_ready, nm_ready, ex_ready, p_ready = sem("sc_ready"), sem("nm_ready"), sem("ex_ready"), sem("p_ready")
        tr_ready, pt_ready, o_ready, oh_ready, ol_ready = (sem("tr_ready"), sem("pt_ready"), sem("o_ready"),
                                                           sem("oh_ready"), sem("ol_ready"))
        inv_pe, inv_act, inv_dve = [[sem(f"inv_{e}{half}") for half in range(2)] for e in ("pe", "act", "dve")]
        rec_pe, rec_act, rec_dve = sem("rec_pe"), sem("rec_act"), sem("rec_dve")
        row_pe, row_act, row_dve = sem("row_pe"), sem("row_act"), sem("row_dve")
        s_loaded = sem("s_loaded")
        mem_loaded, mem_act, mem_dve, mem_pe = sem("mem_loaded"), sem("mem_act"), sem("mem_dve"), sem("mem_pe")
        cx_loaded, cx_pe, cx_act = sem("cx_loaded"), sem("cx_pe"), sem("cx_act")
        cc_loaded, cc_pe, cc_act = sem("cc_loaded"), sem("cc_pe"), sem("cc_act")
        y_pe, y_act, y_dve = sem("y_pe"), sem("y_act"), sem("y_dve")
        arena_free = sem("arena_free")
        rows_pe, rows_act = sem("rows_pe"), sem("rows_act")
        head_sq, head_sum, head_ln, head_exp, head_mul = (sem("head_sq"), sem("head_sum"), sem("head_ln"),
                                                          sem("head_exp"), sem("head_mul"))
        head_y, head_hi = sem("head_y"), sem("head_hi")
        gate_in, vpast_in = sem("gate_in"), sem("vpast_in")
        kpast_in, conv_turned, conv_out = sem("kpast_in"), sem("conv_turned"), sem("conv_out")
        s_zero, low_done = sem("s_zero"), sem("low_done")

        UNITS, GROUP = [], {}

        def group(name, units):
            GROUP[name] = (len(UNITS), len(units))
            UNITS.extend(units)

        def unit(**kw):
            kw["G"], kw["nk"] = len(kw["q"]), sum(n for _, n in kw["keys"][0])
            return kw

        def fox_units(sample):
            out = []
            for h in range(H):
                hd = slice(h * HD, (h + 1) * HD)
                for j, a, P in (TOK[TT:] if sample else TOK[:TT]):
                    o = (slice(None), H + h, slice(a, a + P))
                    if sample:
                        keys = [(kpT[:, h, :], PAST), (kb_f[:, h, a:a + P], P)]
                        v = [(128, [vp_n[:, c, hd]]) for c in range(PAST // 128)] + [(P, [vb_n[0:P, j, hd]])]
                    else:
                        keys = [(kb_f[:, h, 0:a + P], a + P)]
                        v = [(128, [vb_n[:, c, hd]]) for c in range(j + 1)]
                    out.append(unit(kind="fox", h=h, P=P, q=[qb_f[:, h, a:a + P]], keys=[keys], scale=HD ** -0.5,
                                    PT=PT0, v=v, D=HD, hi=xh[o], lo=xl[o]))
            return out

        def cross_units():
            out = []
            for h in range(0, H, 2):
                for j, a, P in TOK:
                    kT = kvT if j < TT else kxT
                    vv = [(128, [(kv_n[:, c, (H + g) * HD:(H + g + 1) * HD] if j < TT else
                                  vx_rows[:, c, g * HD:(g + 1) * HD]) for g in (h, h + 1)])
                          for c in range(MEM // 128)]
                    o = (slice(None), slice(h, h + 2), slice(a, a + P))
                    out.append(unit(kind="cross", h=h, P=P, q=[q_x[:, g, a:a + P] for g in (h, h + 1)],
                                    keys=[[(kT[:, g, :], MEM)] for g in (h, h + 1)], scale=HD ** -0.5,
                                    PT=PTX, v=vv, D=HD, hi=xh[o], lo=xl[o]))
            return out

        def swa_units():
            out = []
            for h in [4 * g + e for g in range(HQ // 4) for e in range(2)]:
                kv = h // (HQ // HKV)
                o, kt_ = (kv % 2) * 64, kv // 2
                ho = (h % 2) * 64
                kd_ = slice(kv * HDC, (kv + 1) * HDC)
                for j, a, P in TOK:
                    first = max(j - 1, 0)
                    if j == TT:
                        keys = [(kcT[o:o + 64, kt_, :], WIN), (k_c[o:o + 64, kt_, a:a + P], P)]
                        vv = [(WIN, [vc_rows[:, kd_]]), (P, [v_cn[0:P, j, kd_]])]
                        dist = dist_s[:, :]
                    else:
                        n = a + 128 - 128 * first
                        keys = [(k_c[o:o + 64, kt_, 128 * first:a + 128], n)]
                        vv = [(128, [v_cn[:, c, kd_]]) for c in range(first, j + 1)]
                        dist = dist_p[:, 256 - n:256]
                    oo = (slice(ho, ho + 64), slice(h // 2, h // 2 + 2), slice(a, a + P))
                    out.append(unit(kind="swa", h=h, P=P, dist=dist,
                                    q=[q_c[o:o + 64, (g // 8) * 4 + g % 4, a:a + P] for g in (h, h + 2)],
                                    keys=[keys, keys], scale=1.0, PT=PTC, v=vv, D=HDC, hi=xh[oo], lo=xl[oo]))
            return out

        group("fox_p", fox_units(False))
        group("fox_s", fox_units(True))
        group("cross0", cross_units())
        group("swa", swa_units())
        group("cross1", cross_units())

        def out_bank(U, u):
            bank = MP[0:U["D"], 2 + u % 2, 0:U["P"] * U["G"]]
            return bank.rearrange("p (g n) -> p g n", g=U["G"]) if U["G"] > 1 else bank

        SIZES = LEVELS[1:]
        INV = {"pe": ["gram", "turns"] + [f"{w}{s}" for s in SIZES for w in ("x", "delta")] + ["uw"],
               "act": ["gram", "turns"] + [f"x{s}" for s in SIZES] + ["uw"],
               "dve": ["gram", "turns"] + [f"delta{s}" for s in SIZES]}
        REC = {"pe": ["ws0", "ds0", "o0", "ws1", "ds1", "o1"], "dve": ["ws0", "ds0", "ws1", "ds1"]}

        def count_of(steps, name, j):
            return j * len(steps) + steps.index(name) + 1

        def delta_order(j):
            main = []
            if j < NTOK:
                main = [("rows",), (0, "gram"), (1, "gram"), (0, "turns"), (1, "turns"), (0, "x2"), (0, "delta2"),
                        (1, "x2")]
                for s in SIZES[1:]:
                    main += [(0, f"x{s}"), (1, f"delta{s // 2}"), (0, f"delta{s}"), (1, f"x{s}")]
                main += [(1, f"delta{SIZES[-1]}"), (0, "uw"), (1, "uw")]
            rec = []
            if j:
                nch = 2 if TOK[j - 1][2] == 128 else 1
                rec = [("rec", f"{w}{c}") for c in range(nch) for w in ("ws", "ds", "o")]
            out = []
            for i in range(max(len(main), 1)):
                out += main[i:i + 1]
                if i >= 2 and (i - 2) % 4 == 0 or not main:
                    out, rec = out + rec[:1], rec[1:]
            return out + rec

        STORES = [0]

        block = ctx.enter_context(nc.Block())

        IN_B = (2, 3, 4, 5, 0, 1)

        def loads_of(name):
            l = int(name[-1]) if name[-1].isdigit() else 0
            if name in ("in_a", "in_b", "in_c", "mem0", "mem1", "xq0", "xq1", "out0", "out1"):
                w, c0 = {"in_a": (t["w_in_ab"][0], 0), "in_b": (t["w_in_ab"][0], 16 * 128 + 2 * H),
                         "in_c": (t["w_in_c"][0], 0), "mem": (t["w_xkv"][l], 0), "xq": (t["w_xq"][l], 0),
                         "out": (t["w_out_ab"][0] if l == 0 else t["w_out_c"][0], 0)}[
                             name if name in ("in_a", "in_b", "in_c") else name[:-1]]
                v = w.rearrange("(k p) n -> p k n", p=128)
                return lambda i: v[:, :, bass.ds(c0 + 256 * i, 256)]
            v = t["w_xo"][l].rearrange("(k p) n -> p k n", p=128)
            return lambda i: v[:, :, bass.ds(512 * i, 512)]

        @block.sync
        def _(sp):
            for j, a, P in TOK[:TT]:
                sp.dma_start(x_rows[:, j, :], t["x_prompt"][0, a:a + P, :]).then_inc(x_loaded, 16)
            sp.dma_start(x_rows[0:NS, TT, :], t["x_sample"][0]).then_inc(x_loaded, 16)
            row = 0
            for name, l in (("g_mix", 0), ("g_cross", 0), ("g_mlp", 0), ("g_mix", 1), ("g_cross", 1), ("g_mlp", 1),
                            ("g_final", None), ("g_mem", 0), ("g_mem", 1)):
                g = t[name] if l is None else t[name][l]
                sp.dma_start(par_rows[row:row + KT, :], g.rearrange("(k p) -> k p", p=128)).then_inc(par_loaded, 16)
                row += KT
            sp.dma_start(par_rows[row:row + CW * NCONV, :],
                         t["conv_w_a"][0].rearrange("i (f p) -> (i f) p", p=128)).then_inc(par_loaded, 16)
            row += CW * NCONV
            sp.dma_start(par_rows[row:row + 1, :], t["onorm_g_a"]).then_inc(par_loaded, 16)
            sp.dma_start(conv_rows[:, :], t["state_gdn_conv"][0, 0].rearrange("i (f p) -> (i f) p", p=128)
                         ).then_inc(par_loaded, 16)
            for i, name in enumerate(("a_log_a", "dt_bias_a", "f_bias_b")):
                sp.dma_start(gate_par[:, i, :], t[name][0].partition_broadcast(128)).then_inc(par_loaded, 16)
            sp.dma_start(sinks[:, :], t["sinks_c"][0].partition_broadcast(128)).then_inc(par_loaded, 16)

            def load(slot, source, kt, panel):
                if not (isinstance(panel, int) and panel < 2):
                    sp.wait_ge(w_lo, panel - 1)
                sp.dma_start(stage[slot][:, :].rearrange("p (k n) -> p k n", k=kt), source
                             ).then_inc(w_loaded[slot], 16)

            def first_pair(name, kt=KT):
                src = loads_of(name)
                load(0, src(0), kt, LIN[name][0])
                load(1, src(1), kt, LIN[name][0] + 1)

            def rest(name, kt=KT):
                p0, _, panels, _ = LIN[name]
                src = loads_of(name)
                if panels > 2:
                    with sp.Fori(1, panels // 2) as i:
                        load(0, src(2 * i), kt, p0 + 2 * i)
                        load(1, src(2 * i + 1), kt, p0 + 2 * i + 1)

            def product(name, kt=KT):
                first_pair(name, kt)
                rest(name, kt)

            def mlp(l):
                p0 = LIN[f"mlp{l}"][0]
                up_v = t["w_up"][l].rearrange("(k p) n -> p k n", p=128)
                dn_v = t["w_down"][l].rearrange("(k p) n -> p k n", p=128)
                with sp.Fori(0, NB) as b:
                    for i in range(4):
                        load(i % 2, up_v[:, :, bass.ds(b * D + 256 * i, 256)], KT, p0 + 8 * b + i)
                    for i in range(4):
                        load(i % 2, dn_v[:, bass.ds(b * KT, KT), 256 * i:256 * i + 256], KT, p0 + 8 * b + 4 + i)

            def layer_end(l):
                rest(f"out{l}")
                first_pair(f"mem{l}")
                sp.wait_ge(arena_free, 1 + l)
                sp.dma_start(m_rows[:, :, :], t["mem_prompt"][0].rearrange("(c p) d -> p c d", p=128)
                             ).then_inc(mem_loaded, 16)
                sp.dma_start(kx_rows[:, :, :], t["cache_mem_k"][l, 0].rearrange("(c p) h d -> p c (h d)", p=128)
                             ).then_inc(cx_loaded, 16)
                sp.dma_start(vx_rows[:, :, :], t["cache_mem_v"][l, 0].rearrange("(c p) h d -> p c (h d)", p=128)
                             ).then_inc(cx_loaded, 16)
                rest(f"mem{l}")
                product(f"xq{l}")
                product(f"xo{l}", 4)
                mlp(l)

            first_pair("in_a")
            sp.wait_ge(x_done, KT)
            w = t["w_in_ab"][0].rearrange("(k p) n -> p k n", p=128)
            sp.dma_start(w_gate[:, :, 0:2 * H], w[:, :, 16 * 128:16 * 128 + 2 * H]).then_inc(gate_in, 16)
            sp.dma_start(w_gate[:, :, 2 * H:3 * H], w[:, :, w.shape[2] - H:w.shape[2]]).then_inc(gate_in, 16)
            sp.dma_start(lf_past[:, :, :], t["cache_fox_logf"][0, 0].rearrange("(c p) h -> p c h", p=128)
                         ).then_inc(gate_in, 16)
            rest("in_a")
            p0 = LIN["in_b"][0]
            src = loads_of("in_b")
            for i, panel in enumerate(IN_B):
                load(i % 2, src(panel), KT, p0 + i)
            first_pair("out0")
            sp.wait_ge(product_done, LIN["out0"][1])
            for dst, src_, signal in ((kp_rows, "cache_fox_k", kpast_in), (vp_n, "cache_fox_v", vpast_in)):
                sp.dma_start(dst[:, :, :], t[src_][0, 0].rearrange("(c p) h d -> p c (h d)", p=128)
                             ).then_inc(signal, 16)
            layer_end(0)
            product("in_c")
            first_pair("out1")
            sp.wait_ge(drained, DRAINED["in_c"] + 4)
            sp.dma_start(kc_rows[:, :], t["cache_swa_k"][0, 0].rearrange("p h d -> p (h d)")).then_inc(cc_loaded, 16)
            sp.dma_start(vc_rows[:, :], t["cache_swa_v"][0, 0].rearrange("p h d -> p (h d)")).then_inc(cc_loaded, 16)
            layer_end(1)
            sp.wait_ge(stored, 16 * STORES_TOTAL)

        @block.gpsimd
        def _(pool):
            n = [0]

            def step(inst):
                inst.then_inc(mask_done, 1)
                n[0] += 1
                pool.wait_ge(mask_done, n[0])

            for m, v in ((ident, 0.0), (ones, 1.0), (upper, 1.0), (chunk_upper, 1.0), (chunk_later, 1.0),
                         (chunk_mask, 0.0), (diag_mask, 0.0), (eps_col, EPS), (dist_p, 0.0), (dist_s, 0.0)):
                step(pool.memset(m[:, :], v))
            step(pool.memset(level[:, :, :], 0.0))
            step(pool.memset(G[:, :, :], 0.0))
            step(pool.memset(chunk_rows[:, :, :], 0.0))
            for c in range(2):
                step(pool.memset(chunk_rows[64 * c:64 * c + 64, c, :], 1.0))

            def select(m, pattern, base, mult, op, fill):
                step(pool.affine_select(out=m, in_=m, pattern=pattern, base=base, channel_multiplier=mult,
                                        compare_op=op, fill=fill))

            select(ident[:, :], [[-1, 128]], 0, 1, ALU.not_equal, 1.0)
            select(upper[:, :], [[1, NPT]], 0, -1, ALU.is_ge, 0.0)
            select(chunk_upper[:, :], [[1, 128]], 0, -1, ALU.is_ge, 0.0)
            select(chunk_mask[:, :], [[1, 128]], 0, -1, ALU.is_ge, -BIG)
            select(chunk_later[:, :], [[-1, 128]], -1, 1, ALU.is_ge, 0.0)
            select(diag_mask[:, :], [[-1, 128]], 0, 1, ALU.is_ge, -BIG)
            for m, v in ((chunk_upper, 0.0), (chunk_mask, -BIG)):
                select(m[0:64, 64:128], [[0, 64]], -1, 0, ALU.is_ge, v)
            select(chunk_later[64:128, 0:64], [[0, 64]], -1, 0, ALU.is_ge, 0.0)
            for n_, s in enumerate(LEVELS):
                part = level[:, n_, :].rearrange("p (b r c) -> p b r c", r=2, c=s)[:, :, 1, :]
                step(pool.memset(part, 1.0))
            for n_, s in enumerate(LEVELS):
                part = level[:, n_, :].rearrange("p (b r c) -> p b r c", r=2, c=s)[:, :, 1, :]
                select(part, [[-2 * s, 64 // s], [0, s]], 0, 1, ALU.is_ge, 0.0)
            step(pool.iota(dist_p[:, :], [[-1, 256]], base=128, channel_multiplier=1,
                           allow_small_or_imprecise_dtypes=True))
            step(pool.iota(dist_s[:, :], [[-1, WIN + NS]], base=WIN, channel_multiplier=1,
                           allow_small_or_imprecise_dtypes=True))
            for n_, s in enumerate(LEVELS):
                part = level[:, n_, :].rearrange("p (b r c) -> p b r c", r=2, c=s)[:, :, 1, :]
                select(part, [[2 * s, 64 // s], [0, s]], s - 1, -1, ALU.is_ge, 0.0)
            step(pool.memset(dist_p[0:64, 192:256], BIG))
            step(pool.memset(dist_p[64:128, 0:64], BIG))
            assert n[0] == MASKS, n[0]

            with pool.Fori(0, PANELS // 2) as i:
                for s in range(2):
                    pool.wait_ge(w_hi, 2 * i + s + 1)
                    pool.tensor_tensor(wl[s][:, :], stage[s][:, :], wh[s][:, :].bitcast(f32), ALU.subtract
                                       ).then_inc(w_lo, 1)

        @block.tensor
        def _(pe):
            def tile(slot, s, col, W, kt, halves, X, ready=None):
                w_view = [w[s][:, :].rearrange("p (k n) -> p k n", k=kt) for w in (wh, wl)]
                mm = None
                for k in range(kt):
                    if ready is not None:
                        pe.wait_ge(ready[0], ready[1] + k + 1)
                    for n_, (w, part) in enumerate(((0, 0), (0, 1), (1, 0))):
                        for half, (a, b) in enumerate(halves):
                            mm = pe.matmul(LP[:, 2 * slot + half, 0:b - a], w_view[w][:, k, col:col + 128],
                                           X[part][:, k, a:b], start=(k == 0 and n_ == 0),
                                           stop=(k == kt - 1 and n_ == 2))
                return mm

            TOKENS = ((0, HALF), (HALF, N))

            def pair(free, Pn, tpp, kt, halves, X, ready, after_first=None):
                for s in range(2):
                    pe.wait_ge(w_lo, Pn + s + 1)
                    for i in range(tpp):
                        tt_ = s * tpp + i
                        if free(tt_) is not None:
                            pe.wait_ge(*free(tt_))
                        tile(tt_ % 2, s, 128 * i, None, kt, halves, X, ready if tt_ == 0 else None
                             ).then_inc(product_done, 1)
                        if tt_ == 0 and after_first is not None:
                            after_first()

            def one_pair(name, i, X, ready=None, kt=KT, halves=TOKENS, after_first=None):
                p0, _, _, tpp = LIN[name]
                d0 = DRAINED[name] + 2 * tpp * i
                pair(lambda n_: (drained, d0 + n_ - 1) if not isinstance(d0, int) or d0 + n_ >= 2 else None,
                     p0 + 2 * i, tpp, kt, halves, X, ready, after_first)

            def rest(name, X, kt=KT, halves=TOKENS):
                panels = LIN[name][2]
                if panels > 2:
                    with pe.Fori(1, panels // 2) as i:
                        one_pair(name, i, X, None, kt, halves)

            def product(name, X, ready, kt=KT, halves=TOKENS, after_first=None):
                one_pair(name, 0, X, ready, kt, halves, after_first)
                rest(name, X, kt, halves)

            def stat(n):
                def go():
                    pe.wait_ge(sq_used, KT * (n + 1))
                    if n:
                        pe.wait_ge(rstd_ready, n)
                    for half, (a, b) in enumerate(TOKENS):
                        mm = pe.matmul(MP[:, half, 0:HALF], ones[:, :], acc[:, a:b], start=True, stop=True)
                    mm.then_inc(stat_done, 1)
                return go

            XS = (xh, xl)

            def attention(name, also=lambda i: None):
                u0, count = GROUP[name]

                def scores(u):
                    U = UNITS[u]
                    if u >= 2:
                        pe.wait_ge(ex_ready if UNITS[u - 2]["kind"] == "cross" else nm_ready, u - 1)
                    for g in range(U["G"]):
                        at = g * U["nk"]
                        for kT, n in U["keys"][g]:
                            mm = pe.matmul(LP[0:U["P"], 2 * (u % 2) + at // 512, at % 512:at % 512 + n], U["q"][g],
                                           kT, start=True, stop=True, skip_group_check=True)
                            at += n
                    mm.then_inc(sc_ready, 1)

                def turn(u):
                    U = UNITS[u]
                    P, G_ = U["P"], U["G"]
                    pe.wait_ge(p_ready, u + 1)
                    if u >= 2:
                        pe.wait_ge(pt_ready, u - 1)
                    for g in range(G_):
                        at = g * U["nk"]
                        for c, (n, _) in enumerate(U["v"]):
                            to = (c * G_ + g) * P
                            mm = pe.transpose(MP[0:n, u % 2, to:to + P], probs[0:P, u % 3, at:at + n],
                                              ident[0:P, 0:P])
                            at += n
                    mm.then_inc(tr_ready, 1)

                def values(u):
                    U = UNITS[u]
                    P, G_, last = U["P"], U["G"], len(U["v"]) - 1
                    pe.wait_ge(pt_ready, u + 1)
                    if u >= 2:
                        pe.wait_ge(ol_ready, u - 1)
                    shared = len(U["v"][0][1]) < G_
                    for g in range(1 if shared else G_):
                        w = (G_ if shared else 1) * P
                        for c, (n, v) in enumerate(U["v"]):
                            at = (c * G_ + g) * P
                            mm = pe.matmul(MP[0:U["D"], 2 + u % 2, g * P:g * P + w], v[g],
                                           U["PT"][0:n, u % 2, at:at + w], start=(c == 0), stop=(c == last),
                                           skip_group_check=True)
                    mm.then_inc(o_ready, 1)

                for i in range(-1, count + 3):
                    if 2 <= i < count + 2:
                        turn(u0 + i - 2)
                    if i >= 3:
                        values(u0 + i - 3)
                    if i + 1 < count:
                        scores(u0 + i + 1)
                    also(i)

            pe.wait_ge(mask_done, MASKS)
            pe.wait_ge(par_loaded, 16 * 16)
            pe.transpose(MP[:, 0, 0:NROW], par_rows[:, :], ident[0:NROW, 0:NROW])
            pe.transpose(MP[:, 1, 0:PAD * NCONV], conv_rows[:, :], ident[0:PAD * NCONV, 0:PAD * NCONV]
                         ).then_inc(param_turned, 1)
            pe.wait_ge(x_loaded, 16 * NTOK)
            for k in range(KT):
                if k >= 2:
                    pe.wait_ge(x_done, k - 1)
                for j, a, P in TOK:
                    mm = pe.transpose(LP[:, 2 * (k % 2) + j // TT, (a % NPT):(a % NPT) + P],
                                      x_rows[0:P, j, 128 * k:128 * k + 128], ident[0:P, 0:P])
                mm.then_inc(x_turned, 1)
            pe.wait_ge(x_done, KT)
            pe.wait_ge(param_ready, 2)

            one_pair("in_a", 0, XS, (xs_ready, 0), after_first=stat(0))
            pe.wait_ge(gate_act, 1)
            pe.wait_ge(gate_dve, 1)
            pe.wait_ge(rstd_ready, 1)
            for k in range(KT):
                for n_, (w, X) in enumerate(((wgh, xh), (wgh, xl), (wgl, xh))):
                    for half, (a, b) in enumerate(TOKENS):
                        mm = pe.matmul(MP[0:GATES, half, 0:HALF], w[:, k, :], X[:, k, a:b],
                                       start=(k == 0 and n_ == 0), stop=(k == KT - 1 and n_ == 2))
            mm.then_inc(gate_pe, 1)
            rest("in_a", XS)
            pe.wait_ge(gate_dve, 2)
            for j, a, P in TOK:
                mm = pe.transpose(MP[0:P, 2, GATES * j:GATES * j + GATES], gT[:, a:a + P], ident[0:GATES, 0:GATES])
            mm.then_inc(gate_pe, 1)

            def turned(n_, P, source):
                if n_ >= 4:
                    pe.wait_ge(turn_act, n_ - 3)
                for h in range(H):
                    mm = pe.transpose(MP[0:P, n_ % 4, 128 * h:128 * h + 128], source(h), ident[:, :])
                mm.then_inc(turn_pe, 1)

            one_pair("in_b", 0, XS)
            pe.wait_ge(conv_dve, 1)
            pe.transpose(MP[0:2 * NCONV * PAD, 3, 0:128], conv_new[:, :, :, :].rearrange("p a i f -> p (a i f)"),
                         ident[:, :]).then_inc(conv_turned, 1)
            one_pair("in_b", 1, XS)
            pe.wait_ge(gate_act, 3)
            pe.wait_ge(conv_out, 1)
            for j, a, P in TOK:
                turned(j, P, lambda h: kb_f[:, h, a:a + P])
            one_pair("in_b", 2, XS)
            for j, a, P in TOK:
                turned(NTOK + j, P, lambda h: vb_f[:, h, a:a + P])

            def forget_rows(sample):
                pe.wait_ge(gate_dve, GATE_LOGF)
                if sample:
                    pe.wait_ge(ol_ready, GROUP["fox_p"][0] + GROUP["fox_p"][1])
                    pe.wait_ge(gate_in, 16 * 3)
                    pe.wait_ge(vpast_in, 16)
                for h in range(H):
                    if h >= 2:
                        pe.wait_ge(rows_act, (H if sample else 0) + h - 1)
                    b = 2 * (h % 2)
                    nt = NTOK if sample else TT
                    for j in range(nt):
                        if not sample:
                            lf, P = G[:, j, 2 * H + h:2 * H + h + 1], 128
                        elif j < TT:
                            lf, P = lf_past[:, j, h:h + 1], 128
                        else:
                            lf, P = G[0:NS, TT, 2 * H + h:2 * H + h + 1], NS
                        if j < TT:
                            mm = pe.matmul(LP[:, b, 128 * j:512], lf.to_broadcast([P, 128]),
                                           upper[0:P, 0:512 - 128 * j], start=(j == 0),
                                           stop=(j == TT - 1), skip_group_check=True)
                        if sample:
                            m = (ones[:, 0:NS] if j < TT else upper[0:NS, 0:NS])
                            mm = pe.matmul(LP[:, b + 1, 0:NS], lf.to_broadcast([P, 128]), m,
                                           start=(j == 0), stop=(j == TT), skip_group_check=True)
                    mm.then_inc(rows_pe, 1)

            pe.wait_ge(drained, last_tile("in_b"))
            forget_rows(False)
            pe.wait_ge(kpast_in, 16)
            for c in range(PAST // 128):
                turned(2 * NTOK + c, 128, lambda h: kp_rows[:, c, 128 * h:128 * h + 128])
            pe.wait_ge(turn_act, 2 * NTOK + PAST // 128)
            pe.wait_ge(rows_act, H)

            def delta_sums(i):
                if i < 0 or i % 2 == 0 or i // 2 >= 2 * H:
                    return
                f = i // 2
                pe.wait_ge(head_sq, f + 1)
                if f:
                    pe.wait_ge(head_ln, f)
                for half, (a, b) in enumerate(TOKENS):
                    mm = pe.matmul(LP[:, 1 + 2 * half, 0:HALF], ones[:, :], head_squares[:, a:b],
                                   start=True, stop=True)
                mm.then_inc(head_sum, 1)

            attention("fox_p", delta_sums)
            pe.wait_ge(head_ln, 2 * H)
            forget_rows(True)
            pe.wait_ge(rows_act, 2 * H)
            attention("fox_s")
            pe.wait_ge(ol_ready, GROUP["fox_s"][0] + GROUP["fox_s"][1])
            pe.wait_ge(head_mul, 2 * H)
            pe.wait_ge(conv_act, 2 + NCONV)
            pe.wait_ge(gate_act, 7)

            def rows(j):
                _, a, P = TOK[j]
                nch = 2 if P == 128 else 1
                if j:
                    pe.wait_ge(row_act, j)
                if j >= 2:
                    pe.wait_ge(rec_dve, count_of(REC["dve"], "ds1", j - 2))
                    pe.wait_ge(rec_act, j - 1)
                for h in range(H):
                    pe.matmul(MP[:, 0, h * P:h * P + P], Gb[0:P, j, H + h:H + h + 1].to_broadcast([P, 128]),
                              chunk_upper[0:P, 0:P], start=True, stop=True, skip_group_check=True)
                g4 = Gb[0:P, j, H:2 * H]
                pe.matmul(MP[0:P, 3, 0:4], chunk_upper[0:P, 0:P], g4, start=True, stop=True, skip_group_check=True)
                pe.matmul(MP[0:P, 3, 4:8], chunk_later[0:P, 0:P], g4, start=True, stop=True, skip_group_check=True)
                for c in range(nch):
                    mm = pe.matmul(MP[:, 3, 8 + 4 * c:12 + 4 * c], chunk_rows[0:P, c, :], g4,
                                   start=True, stop=True, skip_group_check=True)
                mm.then_inc(row_pe, 1)

            def inverse(half, name, j):
                _, a, P = TOK[j]
                b0, b1 = 2 * half, 2 * half + 1
                heads = (2 * half, 2 * half + 1)

                def dve_at(step_, jj=j):
                    pe.wait_ge(inv_dve[half], count_of(INV["dve"], step_, jj))

                def act_at(step_, jj=j):
                    pe.wait_ge(inv_act[half], count_of(INV["act"], step_, jj))

                def mm_(out, lhsT, rhs, start=True, stop=True):
                    return pe.matmul(out, lhsT, rhs, start=start, stop=stop, skip_group_check=True)

                if name == "gram":
                    if j:
                        act_at("uw", j - 1)
                        dve_at("delta32", j - 1)
                    for i, h in enumerate(heads):
                        g = Gb[0:P, j, H + h:H + h + 1].to_broadcast([P, P])
                        kT, qT = ua[:, H + h, a:a + P], ua[:, h, a:a + P]
                        mm_(LP[0:P, b0, i * P:i * P + P], g, chunk_upper[0:P, 0:P], stop=False)
                        mm_(LP[0:P, b0, i * P:i * P + P], ident[0:P, 0:P], chunk_mask[0:P, 0:P], start=False)
                        mm_(LP[0:P, b0, (2 + i) * P:(3 + i) * P], Gb[0:P, j, h:h + 1].to_broadcast([P, P]),
                            ident[0:P, 0:P])
                        mm_(LP[0:P, b1, i * P:i * P + P], kT, kT)
                        mm = mm_(LP[0:P, b1, (2 + i) * P:(3 + i) * P], kT, qT)
                elif name == "turns":
                    dve_at("gram")
                    for i, h in enumerate(heads):
                        pe.transpose(LP[0:P, b0, 128 * i:128 * i + 128], ua[:, H + h, a:a + P], ident[:, :])
                        pe.transpose(LP[0:P, b0, 256 + 128 * i:384 + 128 * i], ua[:, 2 * H + h, a:a + P], ident[:, :])
                        mm = pe.transpose(LP[0:P, b1, P * i:P * i + P], TmT[0:P, h, 0:P], ident[0:P, 0:P])
                elif name[0] == "x":
                    s = int(name[1:])
                    if s == 2:
                        act_at("turns")
                        dve_at("turns")
                    else:
                        dve_at(f"delta{s // 2}")
                    for i, h in enumerate(heads):
                        mm = mm_(LP[0:P, b0, i * P:i * P + P], BT[0:P, h, 0:P], Tm[0:P, h, 0:P])
                elif name[:5] == "delta":
                    act_at("x" + name[5:])
                    for i, h in enumerate(heads):
                        if name != "delta32":
                            mm_(LP[0:P, b1, i * P:i * P + P], TmT[0:P, h, 0:P], Xm[0:P, h, 0:P])
                        mm = mm_(LP[0:P, b1, (2 + i) * P:(3 + i) * P], Xm[0:P, h, 0:P], TmT[0:P, h, 0:P])
                else:
                    dve_at("delta32")
                    for i, h in enumerate(heads):
                        mm_(LP[0:P, b0, 128 * i:128 * i + 128], TmT[0:P, h, 0:P], vbt[0:P, h, :])
                        mm = mm_(LP[:, b0, 256 + P * i:256 + P * i + P], kbe[0:P, h, :], TmT[0:P, h, 0:P])
                mm.then_inc(inv_pe[half], 1)

            def recurrence(name, j):
                _, a, P = TOK[j]
                c, par = int(name[-1]), j % 2
                C = 64 if P == 128 else P
                r = slice(c * C, c * C + C)
                old = 2 if j == TT else c
                if name[:2] == "ws":
                    if c == 0:
                        for half in range(2):
                            pe.wait_ge(inv_act[half], count_of(INV["act"], "uw", j))
                        pe.wait_ge(row_dve, j + 1)
                        if j:
                            pe.wait_ge(rec_dve, count_of(REC["dve"], "ds1", j - 1))
                        else:
                            pe.wait_ge(s_zero, 1)
                        if j == TT:
                            pe.wait_ge(s_loaded, 16)
                    else:
                        pe.wait_ge(rec_dve, count_of(REC["dve"], "ds0", j))
                    for h in range(H):
                        mm = pe.matmul(MP[0:P, 1, 128 * h:128 * h + 128], wT[:, par, h, 0:P], S[:, old, h, :],
                                       start=True, stop=True, skip_group_check=True)
                elif name[:2] == "ds":
                    pe.wait_ge(rec_dve, count_of(REC["dve"], f"ws{c}", j))
                    for h in range(H):
                        mm = pe.matmul(MP[:, 1, 128 * h:128 * h + 128], kd[r, par, h, :], vnew[r, h, :],
                                       start=True, stop=True, skip_group_check=True)
                else:
                    if j and c == 0:
                        pe.wait_ge(rec_act, j)
                    for h in range(H):
                        o = MP[:, 2, P * h + c * C:P * h + c * C + C]
                        pe.matmul(o, S[:, old, h, :], qe[:, par, h, r], start=True, stop=False, skip_group_check=True)
                        mm = pe.matmul(o, vnew[r, h, :], AT[r, par, h, r], start=False, stop=True,
                                       skip_group_check=True)
                mm.then_inc(rec_pe, 1)

            for j in range(NTOK + 1):
                for what in delta_order(j):
                    if what[0] == "rows":
                        rows(j)
                    elif what[0] == "rec":
                        recurrence(what[1], j - 1)
                    else:
                        inverse(*what, j)
            pe.wait_ge(rec_act, NTOK)
            for f in range(2 * H, 3 * H):
                pe.wait_ge(head_sq, f + 1)
                if f >= 2 * H + 2:
                    pe.wait_ge(head_mul, f - 1)
                for half, (a, b) in enumerate(TOKENS):
                    mm = pe.matmul(MP[:, 2 * (f % 2) + half, 0:HALF], ones[:, :], sq[:, f % 2, a:b],
                                   start=True, stop=True)
                mm.then_inc(head_sum, 1)
            pe.wait_ge(low_done, H)

            def layer_end(l):
                product(f"out{l}", XS, None)
                for k in range(KT):
                    pe.wait_ge(mem_dve, (KT + 1) * l + 1)
                    if k >= 2:
                        pe.wait_ge(mem_dve, (KT + 1) * l + k)
                    for c in range(MEM // 128):
                        mm = pe.transpose(MP[:, k % 2, 128 * c:128 * c + 128], m_rows[:, c, 128 * k:128 * k + 128],
                                          ident[:, :])
                    mm.then_inc(mem_pe, 1)
                product(f"mem{l}", (mh, ml), (mem_dve, (KT + 1) * l + 1), halves=((0, MEM),))
                pe.wait_ge(drained, last_tile(f"mem{l}"))
                for c in range(MEM // 128):
                    for k in range(KT):
                        mm = pe.transpose(MP[:, 2 * c + k // 4, 128 * (k % 4):128 * (k % 4) + 128],
                                          kvT[:, k, 128 * c:128 * c + 128], ident[:, :])
                mm.then_inc(cx_pe, 1)
                pe.wait_ge(cx_loaded, 32 * (l + 1))
                for h in range(H):
                    for c in range(MEM // 128):
                        mm = pe.transpose(LP[:, h // 2, 256 * (h % 2) + 128 * c:256 * (h % 2) + 128 * c + 128],
                                          kx_rows[:, c, 128 * h:128 * h + 128], ident[:, :])
                mm.then_inc(cx_pe, 1)
                pe.wait_ge(cx_act, 2 * (l + 1))
                product(f"xq{l}", XS, (xs_ready, KT * (3 * l + 1)), after_first=stat(3 * l + 1))
                pe.wait_ge(drained, last_tile(f"xq{l}"))
                attention(f"cross{l}")
                pe.wait_ge(ol_ready, sum(GROUP[f"cross{l}"]))
                product(f"xo{l}", XS, None, kt=4)
                mlp(l)

            def mlp_block(l, b, after_first):
                P_ = LIN[f"mlp{l}"][0] + 8 * b
                relus, downs = KT * NB * l + KT * b, DRAINED[f"mlp{l}"] + KT * b

                def free(k):
                    if k < 2:
                        return drained, downs - 1 + k
                    if k < KT + 2:
                        return relu_ready, relus + k - 1
                    return drained, downs + k - KT - 1

                pair(free, P_, 2, KT, TOKENS, XS, (xs_ready, KT * (3 * l + 2)) if after_first else None, after_first)
                pair(lambda n_: free(4 + n_), P_ + 2, 2, KT, TOKENS, XS, None)
                pair(lambda n_: free(8 + n_), P_ + 4, 2, KT, TOKENS, (hh, hl), (h_ready, relus))
                pair(lambda n_: free(12 + n_), P_ + 6, 2, KT, TOKENS, (hh, hl), None)

            def mlp(l):
                mlp_block(l, 0, stat(3 * l + 2))
                with pe.Fori(1, NB) as b:
                    mlp_block(l, b, None)

            layer_end(0)
            product("in_c", XS, (xs_ready, KT * 3), after_first=stat(3))
            pe.wait_ge(drained, last_tile("in_c"))
            pe.wait_ge(cc_loaded, 32)
            for c in range(2):
                mm = pe.transpose(LP[:, 0, 128 * c:128 * c + 128], kc_rows[:, 128 * c:128 * c + 128], ident[:, :])
            mm.then_inc(cc_pe, 1)
            for j, a, P in TOK:
                if j >= 2:
                    pe.wait_ge(cc_act, 1 + j - 1)
                for c in range(2):
                    pe.transpose(MP[0:P, 2 * (j % 2), 128 * c:128 * c + 128], k_c[:, c, a:a + P], ident[:, :])
                    mm = pe.transpose(MP[0:P, 2 * (j % 2) + 1, 128 * c:128 * c + 128], v_c[:, c, a:a + P],
                                      ident[:, :])
                mm.then_inc(cc_pe, 1)
            pe.wait_ge(cc_act, 1 + NTOK)
            attention("swa")
            pe.wait_ge(ol_ready, sum(GROUP["swa"]))
            layer_end(1)
            stat(6)()
            for j, a, P in TOK:
                if j == 0:
                    pe.wait_ge(y_dve, KT)
                if j >= 2:
                    pe.wait_ge(y_act, j - 1)
                for k in range(KT):
                    mm = pe.transpose(LP[0:P, 2 * (j % 2) + k // 4, 128 * (k % 4):128 * (k % 4) + 128],
                                      yT[:, k, a:a + P], ident[:, :])
                mm.then_inc(y_pe, 1)

        @block.scalar
        def _(act):
            n = [0]

            def step(inst):
                inst.then_inc(act_step, 1)
                n[0] += 1

            def settled():
                act.wait_ge(act_step, n[0])

            def store(dst, src):
                act.dma_start(dst, src).then_inc(stored, 16)
                STORES[0] += 1

            def split(s, need):
                act.wait_ge(w_loaded[s], need)
                act.copy(wh[s][:, :], stage[s][:, :]).then_inc(w_hi, 1)

            def splits(p0, t0, tpp, i):
                for s in range(2):
                    act.wait_ge(product_done, t0 + 2 * tpp * i + tpp * (s + 1))
                    split(s, 16 * (p0 // 2 + 2) + 16 * i)

            def product(name):
                p0, t0, panels, tpp = LIN[name]
                with act.Fori(0, panels // 2) as i:
                    splits(p0, t0, tpp, i)

            def norm(n_, last=False):
                g = n_
                for k in range(KT):
                    act.wait_ge(x_done, NORM_BASE[n_] + k + 1)
                    if k >= 2:
                        act.wait_ge(sq_used, KT * n_ + k - 1)
                    act.activation(sq[:, k % 2, :], x[:, k, :], ACT.Square).then_inc(sq_ready, 1)
                    if not last:
                        act.activation(xh[:, k, :], x[:, k, :], ACT.Copy, scale=gain(g, k)).then_inc(xh_ready, 1)

            def make_rstd(n_, squared=False):
                act.wait_ge(stat_done, n_ + 1)
                src = MP[:, 0:2, 0:HALF]
                dst = rstd[:, :].rearrange("p (a n) -> p a n", a=2)
                step(act.activation(dst, src, ACT.Ln, bias=eps_col[:, :], scale=1.0 / D))
                settled()
                if squared:
                    act.activation(rstd[:, :], rstd[:, :], ACT.Exp, scale=-1.0).then_inc(rstd_ready, 1)
                else:
                    act.activation(rstd[:, :], rstd[:, :], ACT.Exp, scale=-0.5).then_inc(rstd_ready, 1)

            def attention(name, also=lambda i: None):
                u0, count = GROUP[name]

                def exps(u):
                    U = UNITS[u]
                    P, nk, s = U["P"], U["nk"], u % 2
                    act.wait_ge(nm_ready, u + 1)
                    for g in range(U["G"]):
                        at = slice(g * nk, (g + 1) * nk)
                        cross = U["kind"] == "cross"
                        inst = act.activation(probs[0:P, u % 3, at], LP[0:P, 2 * s, at] if cross else probs[0:P, u % 3, at],
                                              ACT.Exp, bias=nm[0:P, s, g:g + 1], scale=U["scale"] if cross else 1.0,
                                              accum_out=rs[0:P, s, g:g + 1])
                    if U["kind"] == "swa":
                        inst = act.activation(es[0:P, s, :], es[0:P, s, :], ACT.Exp)
                    inst.then_inc(ex_ready, 1)

                def pt(u):
                    U = UNITS[u]
                    s, w = u % 2, U["P"] * U["G"]
                    act.wait_ge(tr_ready, u + 1)
                    if u >= 2:
                        act.wait_ge(o_ready, u - 1)
                    full = sum(n_ == 128 for n_, _ in U["v"])
                    inst = act.copy(U["PT"][:, s, 0:full * w], MP[:, s, 0:full * w])
                    if full < len(U["v"]):
                        rows = U["v"][-1][0]
                        inst = act.copy(U["PT"][0:rows, s, full * w:full * w + w], MP[0:rows, s, full * w:full * w + w])
                    inst.then_inc(pt_ready, 1)

                def high(u):
                    U = UNITS[u]
                    act.wait_ge(o_ready, u + 1)
                    act.copy(U["hi"], out_bank(U, u)).then_inc(oh_ready, 1)

                for i in range(count + 3):
                    if 2 <= i < count + 2:
                        pt(u0 + i - 2)
                    if i < count:
                        exps(u0 + i)
                    if i >= 3:
                        high(u0 + i - 3)
                    also(i)

            act.preload_act_table_set("natural_log_exp_and_others")
            act.wait_ge(param_turned, 1)
            act.copy(cols[:, :], MP[:, 0, 0:NROW]).then_inc(param_ready, 1)
            act.wait_ge(param_ready, 1)
            norm(0)
            split(0, 16)
            split(1, 16)
            make_rstd(0)
            act.wait_ge(gate_in, 16 * 3)
            act.copy(wgh[:, :, :], w_gate[:, :, :]).then_inc(gate_act, 1)
            product("in_a")
            act.wait_ge(gate_pe, 2)
            act.copy(G[:, 0:TT, :].rearrange("p j c -> p (j c)"), MP[:, 2, 0:GATES * TT]).then_inc(gate_act, 1)
            act.copy(G[0:NS, TT, :], MP[0:NS, 2, GATES * TT:GATES * NTOK]).then_inc(gate_act, 1)
            act.wait_ge(gate_dve, 4)
            act.activation(Gb[:, :, :], Gb[:, :, :], ACT.Exp).then_inc(gate_act, 1)
            act.activation(gate_par[:, 0, :], gate_par[:, 0, :], ACT.Exp).then_inc(gate_act, 1)
            act.wait_ge(gate_act, 5)
            act.activation(Gb[:, :, :], Gb[:, :, :], ACT.Ln, bias=one_col[:, :]).then_inc(gate_act, 1)
            act.wait_ge(gate_dve, GATE_LOGF)
            act.activation(Gb[:, :, 0:H], Gb[:, :, 0:H], ACT.Exp, scale=-1.0).then_inc(gate_act, 1)
            act.wait_ge(gate_dve, GATE_LOGF)
            store(t["o_p_fox_logf"][0, 0].rearrange("(j p) h -> p j h", p=128), G[:, 0:TT, 2 * H:3 * H])
            store(t["o_s_fox_logf"][0, 0], G[0:NS, TT, 2 * H:3 * H])
            act.wait_ge(conv_dve, 2)
            act.preload_act_table_set("silu_and_others")
            act.activation(z[:, :, :], z[:, :, :], ACT.Silu).then_inc(conv_act, 2)
            p0, t0, _, _ = LIN["in_b"]
            for T in range(NCONV):
                if T % 2:
                    act.wait_ge(product_done, t0 + T + 1)
                    split(T // 2 % 2, 16 * ((p0 + T // 2) // 2 + 2))
                if T == 7:
                    for j, a, P in TOK:
                        row = k_out[:, j, :] if j < TT else k_out_s[:, :]
                        act.wait_ge(turn_pe, j + 1)
                        act.copy(row, MP[0:P, j % 4, :]).then_inc(turn_act, 1)
                    for j, a, P in TOK:
                        row = k_out[:, j, :] if j < TT else k_out_s[:, :]
                        act.wait_ge(turn_act, j + 1)
                        dst = t["o_p_fox_k"][0, 0, a:a + P] if j < TT else t["o_s_fox_k"][0, 0]
                        store(dst.rearrange("p h d -> p (h d)"), row)
                act.wait_ge(conv_dve, 2 + CW * (T + 1))
                act.activation(ua[:, T, 0:N], sq[:, T % 2, :], ACT.Silu).then_inc(conv_act, 1)
                if T == 4:
                    act.wait_ge(conv_turned, 1)
                    act.copy(conv_newT[:, :], MP[0:2 * NCONV * PAD, 3, 0:128]).then_inc(conv_out, 1)
                    act.wait_ge(conv_out, 1)
                    R = NCONV * PAD
                    for s, o in ((0, "o_p_gdn_conv"), (1, "o_s_gdn_conv")):
                        store(t[o][0, 0].rearrange("i (f p) -> (i f) p", p=128), conv_newT[R * s:R * s + R, :])
            act.wait_ge(conv_act, 2 + NCONV)
            act.preload_act_table_set("natural_log_exp_and_others")
            for j, a, P in TOK:
                act.wait_ge(turn_pe, NTOK + j + 1)
                act.copy(vb_n[0:P, j, :], MP[0:P, (NTOK + j) % 4, :]).then_inc(turn_act, 1)

            def forget_rows(sample):
                for h in range(H):
                    act.wait_ge(rows_pe, (H if sample else 0) + h + 1)
                    b = 2 * (h % 2)
                    inst = act.activation(nF[:, h, 0:512], LP[:, b, 0:512], ACT.Copy, scale=-1.0)
                    if sample:
                        inst = act.activation(nF[:, h, 512:N], LP[:, b + 1, 0:NS], ACT.Copy, scale=-1.0)
                    inst.then_inc(rows_act, 1)

            act.wait_ge(stored, 16 * STORES[0])
            forget_rows(False)
            for c in range(PAST // 128):
                act.wait_ge(turn_pe, 2 * NTOK + c + 1)
                act.copy(kpT[:, :, 128 * c:128 * c + 128],
                         MP[:, (2 * NTOK + c) % 4, :].rearrange("p (h n) -> p h n", h=H)).then_inc(turn_act, 1)
            act.wait_ge(turn_act, 2 * NTOK)
            for j, a, P in TOK:
                dst = t["o_p_fox_v"][0, 0, a:a + P] if j < TT else t["o_s_fox_v"][0, 0]
                store(dst.rearrange("p h d -> p (h d)"), vb_n[0:P, j, :])

            def delta_rstds(i):
                f = i // 2
                if i % 2 or f > 2 * H:
                    return
                if f:
                    act.wait_ge(head_sum, f)
                    if f >= 2:
                        act.wait_ge(head_mul, f - 1)
                    else:
                        act.wait_ge(drained, last_tile("in_b"))
                    act.activation(rstd[:, 0:HALF], LP[:, 1, 0:HALF], ACT.Ln, bias=eps_col[:, :])
                    act.activation(rstd[:, HALF:N], LP[:, 3, 0:HALF], ACT.Ln, bias=eps_col[:, :]
                                   ).then_inc(head_ln, 1)
                    act.wait_ge(head_ln, f)
                    act.activation(rstd[:, :], rstd[:, :], ACT.Exp, scale=-0.5).then_inc(head_exp, 1)
                if f < 2 * H:
                    act.activation(head_squares[:, :], ua[:, f, 0:N], ACT.Square).then_inc(head_sq, 1)

            attention("fox_p", delta_rstds)
            act.wait_ge(ol_ready, sum(GROUP["fox_p"]))
            forget_rows(True)
            attention("fox_s")

            def head_square(f, src):
                if f >= 2 * H + 2:
                    act.wait_ge(head_sum, f - 1)
                act.activation(sq[:, f % 2, :], src, ACT.Square).then_inc(head_sq, 1)

            def head_rstd(f, scale):
                act.wait_ge(head_sum, f + 1)
                act.wait_ge(head_mul, max(f - 1, 2 * H))
                buf = (rstd, acc)[f % 2]
                act.activation(buf[:, :].rearrange("p (a n) -> p a n", a=2),
                               MP[:, 2 * (f % 2):2 * (f % 2) + 2, 0:HALF], ACT.Ln, bias=eps_col[:, :], scale=scale
                               ).then_inc(head_ln, 1)
                act.wait_ge(head_ln, f + 1)
                act.activation(buf[:, :], buf[:, :], ACT.Exp, scale=-0.5).then_inc(head_exp, 1)

            act.wait_ge(ol_ready, sum(GROUP["fox_s"]))
            act.wait_ge(stored, 16 * STORES[0])
            act.dma_start(S[:, 2, :, :], t["state_gdn"][0, 0].rearrange("h k v -> k h v")).then_inc(s_loaded, 16)

            def rows(j):
                _, a, P = TOK[j]
                nch, par = (2 if P == 128 else 1), j % 2
                act.wait_ge(row_pe, j + 1)
                act.activation(qe[:, par, :, 0:P], MP[:, 0, 0:H * P].rearrange("p (h n) -> p h n", h=H), ACT.Exp)
                act.activation(gsm[0:P, par, 0:4], MP[0:P, 3, 0:4], ACT.Copy, scale=-1.0)
                act.activation(gsm[0:P, par, 4:12], MP[0:P, 3, 0:8], ACT.Exp)
                act.activation(eg[:, par, 0:nch, :].rearrange("p c h -> p (c h)"), MP[:, 3, 8:8 + 4 * nch], ACT.Exp
                               ).then_inc(row_act, 1)

            def inverse(half, name, j):
                _, a, P = TOK[j]
                b0, b1, par, h0 = 2 * half, 2 * half + 1, j % 2, 2 * half
                hs = slice(h0, h0 + 2)
                if name[:5] == "delta":
                    return
                act.wait_ge(inv_pe[half], count_of(INV["pe"], name, j))

                def two_heads(bank, at, n_, rows_=P):
                    return LP[0:rows_, bank, at:at + 2 * n_].rearrange("p (h n) -> p h n", h=2)

                if name == "gram":
                    act.wait_ge(row_act, j + 1)
                    for i in range(2):
                        inst = act.activation(dec[0:P, h0 + i, 0:P], LP[0:P, b0, i * P:i * P + P], ACT.Exp,
                                              bias=gsm[0:P, par, h0 + i:h0 + i + 1])
                elif name == "turns":
                    act.copy(kn[0:P, hs, :], two_heads(b0, 0, 128))
                    for i in range(2):
                        act.activation(vbt[0:P, h0 + i, :], LP[0:P, b0, 256 + 128 * i:384 + 128 * i], ACT.Copy,
                                       scale=Gb[0:P, j, h0 + i:h0 + i + 1])
                    inst = act.copy(Tm[0:P, hs, 0:P], two_heads(b1, 0, P))
                elif name[0] == "x":
                    inst = act.copy(Xm[0:P, hs, 0:P], two_heads(b0, 0, P))
                else:
                    act.copy(um[0:P, par, hs, :], two_heads(b0, 0, 128))
                    inst = act.copy(wT[:, par, hs, 0:P], two_heads(b0, 256, P, 128))
                inst.then_inc(inv_act[half], 1)

            def recurrence(name, j):
                _, a, P = TOK[j]
                if name == ("o1" if P == 128 else "o0"):
                    act.wait_ge(rec_pe, count_of(REC["pe"], name, j))
                    act.copy(o_a[:, :, a:a + P], MP[:, 2, 0:H * P].rearrange("p (h n) -> p h n", h=H)
                             ).then_inc(rec_act, 1)

            for j in range(NTOK + 1):
                for what in delta_order(j):
                    if what[0] == "rows":
                        rows(j)
                    elif what[0] == "rec":
                        recurrence(what[1], j - 1)
                    else:
                        inverse(*what, j)
            act.wait_ge(rec_dve, count_of(REC["dve"], "ds0", TT))
            store(t["o_p_gdn_state"][0, 0].rearrange("h k v -> k h v"), S[:, 0, :, :])
            store(t["o_s_gdn_state"][0, 0].rearrange("h k v -> k h v"), S[:, 1, :, :])
            act.wait_ge(rec_act, NTOK)
            act.wait_ge(stored, 16 * STORES[0])
            for h in range(H + 2):
                if h < H:
                    head_square(2 * H + h, o_a[:, h, :])
                if 1 <= h <= H:
                    head_rstd(2 * H + h - 1, 1.0 / HD)
                if h >= 2:
                    act.wait_ge(head_y, h - 1)
                    act.copy(xh[:, h - 2, :], o_a[:, h - 2, :]).then_inc(head_hi, 1)

            def layer_end(l):
                product(f"out{l}")
                act.wait_ge(stored, 16 * STORES[0])
                act.nop().then_inc(arena_free, 1)
                act.wait_ge(mem_loaded, 16 * (l + 1))
                for c in range(MEM // 128):
                    step(act.activation(kv_n[:, c, :], m_rows[:, c, :], ACT.Square, accum_out=mem_ss[:, c:c + 1]))
                settled()
                step(act.activation(mem_rs[:, :], mem_ss[:, :], ACT.Ln, bias=eps_col[:, :], scale=1.0 / D))
                settled()
                act.activation(mem_rs[:, :], mem_rs[:, :], ACT.Exp, scale=-0.5).then_inc(mem_act, 1)
                for k in range(KT):
                    act.wait_ge(mem_pe, KT * l + k + 1)
                    act.activation(mh[:, k, :], MP[:, k % 2, 0:MEM], ACT.Copy, scale=gain(7 + l, k)
                                   ).then_inc(mem_act, 1)
                norm(3 * l + 1)
                product(f"mem{l}")
                act.wait_ge(cx_pe, 2 * l + 1)
                for c in range(MEM // 128):
                    step(act.copy(kv_n[:, c, :].rearrange("p (b n) -> p b n", b=2), MP[:, 2 * c:2 * c + 2, :]))
                settled()
                for i, o in ((0, "o_p_mem_k"), (1, "o_p_mem_v")):
                    store(t[o][l, 0].rearrange("(c p) h d -> p c (h d)", p=128), kv_n[:, :, 512 * i:512 * i + 512])
                act.nop().then_inc(cx_act, 1)
                act.wait_ge(cx_pe, 2 * l + 2)
                act.copy(kxT[:, :, :].rearrange("p (b h) n -> p b (h n)", b=2), LP[:, 0:2, :]).then_inc(cx_act, 1)
                rstd_then_product(3 * l + 1, f"xq{l}")
                attention(f"cross{l}")
                product(f"xo{l}")
                norm(3 * l + 2)
                mlp(l)

            def rstd_then_product(n_, name):
                make_rstd(n_)
                product(name)

            def mlp_block(l, b, last):
                p0, t0, _, _ = LIN[f"mlp{l}"]
                for i in range(4):
                    for m in range(2):
                        k = 2 * i + m
                        T = t0 + 16 * b + k
                        hcount = KT * NB * l + KT * b + k
                        act.wait_ge(product_done, T + 1)
                        if not (isinstance(hcount, int) and hcount < 2):
                            act.wait_ge(hsq_ready, hcount - 1)
                            act.wait_ge(hh_ready, hcount - 1)
                        act.activation(rel[:, k % 2, :].rearrange("p (a n) -> p a n", a=2),
                                       LP[:, 2 * (k % 2):2 * (k % 2) + 2, 0:HALF], ACT.Relu).then_inc(relu_ready, 1)
                        act.wait_ge(relu_ready, hcount + 1)
                        act.activation(hh[:, k, :], rel[:, k % 2, :], ACT.Square).then_inc(hh_ready, 1)
                    split(i % 2, 16 * ((p0 + i) // 2 + 2) + 64 * b)
                for i in range(4):
                    act.wait_ge(product_done, t0 + 16 * b + 8 + 2 * (i + 1))
                    if not (last and i >= 2):
                        split(i % 2, 16 * ((p0 + 4 + i) // 2 + 2) + 64 * b)

            def mlp(l):
                act.wait_ge(stored, 16 * STORES[0])
                p0, t0, _, _ = LIN[f"mlp{l}"]
                make_rstd(3 * l + 2, squared=True)
                mlp_block(l, 0, False)
                end = NB if l == 0 else NB - 1
                with act.Fori(1, end) as b:
                    mlp_block(l, b, False)
                if l == 1:
                    mlp_block(l, NB - 1, True)

            layer_end(0)
            norm(3)
            make_rstd(3)
            product("in_c")
            act.wait_ge(cc_pe, 1)
            act.copy(kcT[:, :, :].rearrange("p c n -> p (c n)"), LP[:, 0, 0:256]).then_inc(cc_act, 1)
            for j, a, P in TOK:
                act.wait_ge(cc_pe, 1 + j + 1)
                if j >= TT - 1:
                    step(act.copy(kc_out[0:P, j % 2, :], MP[0:P, 2 * (j % 2), 0:256]))
                act.copy(v_cn[0:P, j, :], MP[0:P, 2 * (j % 2) + 1, 0:256]).then_inc(cc_act, 1)
                if j >= TT - 1:
                    act.wait_ge(cc_act, 1 + j + 1)
                    for nm_, src in (("k", kc_out[0:P, j % 2, :]), ("v", v_cn[0:P, j, :])):
                        dst = t[f"o_{'p' if j < TT else 's'}_swa_{nm_}"][0, 0]
                        store(dst.rearrange("p h d -> p (h d)"), src)
            attention("swa")
            layer_end(1)
            norm(6, last=True)
            make_rstd(6)
            for j, a, P in TOK:
                act.wait_ge(y_pe, j + 1)
                act.copy(y_rows[0:P, j, :].rearrange("p (b n) -> p b n", b=2), LP[0:P, 2 * (j % 2):2 * (j % 2) + 2, :]
                         ).then_inc(y_act, 1)
                act.wait_ge(y_act, j + 1)
                store(t["o_y_prompt"][0, a:a + P, :] if j < TT else t["o_y_sample"][0], y_rows[0:P, j, :])
            assert STORES[0] == STORES_TOTAL, STORES[0]

        @block.vector
        def _(dve):
            n = [0]

            def step(inst):
                inst.then_inc(dve_step, 1)
                n[0] += 1
                return n[0]

            def after(count):
                dve.wait_ge(dve_step, count)

            def settled():
                after(n[0])

            def norm(n_, last=False):
                g = n_
                for k in range(KT):
                    if not last:
                        dve.wait_ge(xh_ready, KT * n_ + k + 1)
                        dve.wait_ge(x_done, NORM_BASE[n_] + k + 1)
                        dve.scalar_tensor_tensor(out=xl[:, k, :], in0=x[:, k, :], scalar=gain(g, k),
                                                 in1=xh[:, k, :].bitcast(f32), op0=ALU.mult, op1=ALU.subtract
                                                 ).then_inc(xs_ready, 1)
                    dve.wait_ge(sq_ready, KT * n_ + k + 1)
                    if k:
                        dve.wait_ge(sq_used, KT * n_ + k)
                        dve.tensor_tensor(acc[:, :], acc[:, :], sq[:, k % 2, :], ALU.add).then_inc(sq_used, 1)
                    else:
                        dve.tensor_copy(acc[:, :], sq[:, 0, :]).then_inc(sq_used, 1)

            def banks(T):
                s = T % 2
                return LP[:, 2 * s:2 * s + 2, 0:HALF]

            def two(v):
                return v.rearrange("p (a n) -> p a n", a=2)

            def residual_product(name):
                _, t0, panels, tpp = LIN[name]
                with dve.Fori(0, KT // 4) as i:
                    for m in range(4):
                        dve.wait_ge(product_done, t0 + 4 * i + m + 1)
                        dst = x[:, bass.ds(4 * i + m, 1), :].rearrange("p o (a n) -> p (o a) n", a=2)
                        dve.tensor_tensor(dst, banks(m), dst, ALU.add).then_inc(x_done, 1)
                        dve.wait_ge(x_done, NORM_BASE[RES[name]] + 4 * i + m + 1)
                        dve.nop().then_inc(drained, 1)

            def attention(name, also=lambda i: None):
                u0, count = GROUP[name]

                def scored(u):
                    U = UNITS[u]
                    P, nk, s, G_, kind = U["P"], U["nk"], u % 2, U["G"], U["kind"]
                    buf = probs[0:P, u % 3, 0:G_ * nk]
                    rows = buf.rearrange("p (g n) -> p g n", g=G_)
                    dve.wait_ge(sc_ready, u + 1)
                    if u >= 3:
                        dve.wait_ge(tr_ready, u - 2)
                    if kind == "cross":
                        bank = LP[0:P, 2 * s, 0:G_ * nk].rearrange("p (g n) -> p g n", g=G_)
                        c = step(dve.tensor_reduce(nm[0:P, s, :], bank, AX.X, ALU.max, negate=True))
                        yield
                        after(c)
                        dve.tensor_scalar(nm[0:P, s, :], nm[0:P, s, :], U["scale"], None, ALU.mult
                                          ).then_inc(nm_ready, 1)
                        yield
                        return
                    if kind == "fox":
                        for lo_, hi_, b in [(0, min(nk, 512), 2 * s)] + ([(512, nk, 2 * s + 1)] if nk > 512 else []):
                            c = step(dve.scalar_tensor_tensor(
                                out=buf[:, lo_:hi_], in0=LP[0:P, b, 0:hi_ - lo_], scalar=U["scale"],
                                in1=nF[0:P, U["h"], lo_:hi_], op0=ALU.mult, op1=ALU.add))
                        yield
                        after(c)
                        c = step(dve.tensor_tensor(buf[:, nk - P:nk], buf[:, nk - P:nk], diag_mask[0:P, 0:P], ALU.add))
                        yield
                        after(c)
                        dve.tensor_reduce(nm[0:P, s, 0:1], buf, AX.X, ALU.max, negate=True).then_inc(nm_ready, 1)
                        return
                    for g in range(G_):
                        slope = 2.0 ** (-8.0 * (U["h"] + 2 * g + 1) / HQ)
                        c = step(dve.scalar_tensor_tensor(out=buf[:, g * nk:(g + 1) * nk], in0=U["dist"],
                                                          scalar=-slope, in1=LP[0:P, 2 * s, g * nk:(g + 1) * nk],
                                                          op0=ALU.mult, op1=ALU.add))
                    yield
                    after(c)
                    c = step(dve.tensor_reduce(nm[0:P, s, :], rows, AX.X, ALU.max, negate=True))
                    yield
                    after(c)
                    pair_ = slice(U["h"], U["h"] + 3, 2)
                    c = step(dve.tensor_tensor(nm[0:P, s, :], nm[0:P, s, :], neg_sinks[0:P, pair_], ALU.min))
                    after(c)
                    dve.tensor_tensor(es[0:P, s, :], nm[0:P, s, :], sinks[0:P, pair_], ALU.add).then_inc(nm_ready, 1)

                def normed(u):
                    U = UNITS[u]
                    P, nk, s, G_ = U["P"], U["nk"], u % 2, U["G"]
                    dve.wait_ge(ex_ready, u + 1)
                    if U["kind"] == "swa":
                        c = step(dve.tensor_tensor(rs[0:P, s, :], rs[0:P, s, :], es[0:P, s, :], ALU.add))
                        yield
                        after(c)
                    c = step(dve.reciprocal(rr[0:P, s, 0:G_], rs[0:P, s, 0:G_]))
                    yield
                    after(c)
                    for g in range(G_):
                        b = probs[0:P, u % 3, g * nk:(g + 1) * nk]
                        inst = dve.tensor_scalar(b, b, rr[0:P, s, g:g + 1], None, ALU.mult)
                    inst.then_inc(p_ready, 1)

                def low(u):
                    U = UNITS[u]
                    dve.wait_ge(oh_ready, u + 1)
                    dve.tensor_tensor(U["lo"], out_bank(U, u), U["hi"].bitcast(f32), ALU.subtract
                                      ).then_inc(ol_ready, 1)

                for i in range(count + 4):
                    turns = ([scored(u0 + i)] if i < count else []) + ([normed(u0 + i - 1)] if 1 <= i <= count else [])
                    while turns:
                        turns = [g for g in turns if next(g, "end") != "end"]
                    if i >= 4:
                        low(u0 + i - 4)
                    also(i)

            step(dve.memset(one_col[:, :], 1.0))
            dve.wait_ge(mask_done, MASKS)
            dve.wait_ge(par_loaded, 16 * 16)
            step(dve.tensor_scalar(neg_sinks[:, :], sinks[:, :], -1.0, None, ALU.mult))
            for m, w in ((dist_p, 256), (dist_s, WIN + NS)):
                P = m.shape[0]
                step(dve.tensor_scalar(sq[0:P, 0, 0:w], m[:, :], -1.0, None, ALU.mult))
                settled()
                step(dve.tensor_tensor(m[:, :], m[:, :], sq[0:P, 0, 0:w], ALU.max))
                settled()
            for k in range(KT):
                dve.wait_ge(x_turned, k + 1)
                dve.tensor_copy(x[:, k, 0:NPT], LP[:, 2 * (k % 2), 0:NPT])
                dve.tensor_copy(x[:, k, NPT:N], LP[:, 2 * (k % 2) + 1, 0:NS]).then_inc(x_done, 1)
            dve.wait_ge(param_turned, 1)
            dve.wait_ge(param_ready, 1)
            dve.wait_ge(x_turned, KT)
            step(dve.memset(ua[:, :, 0:PAD], 0.0))
            dve.tensor_copy(ua[:, :, PAD + NPT:PAD + NPT + PAD].rearrange("p f i -> p i f"),
                            MP[:, 1, 0:PAD * NCONV].rearrange("p (i f) -> p i f", i=PAD)).then_inc(param_ready, 1)
            norm(0)
            dve.wait_ge(gate_act, 1)
            dve.tensor_tensor(wgl[:, :, :], w_gate[:, :, :], wgh[:, :, :].bitcast(f32), ALU.subtract
                              ).then_inc(gate_dve, 1)
            dve.wait_ge(rstd_ready, 1)
            ta = LIN["in_a"][1]

            def four_conv_rows(i):
                for m in range(4):
                    dve.wait_ge(product_done, ta + 4 * i + m + 1)
                    b = 2 * (m % 2)
                    row = ua[:, bass.ds(4 * i + m, 1), :].rearrange("p o n -> p (o n)")
                    dve.tensor_tensor(row[:, PAD:PAD + HALF], LP[:, b, 0:HALF], rstd[:, 0:HALF], ALU.mult)
                    dve.tensor_tensor(row[:, PAD + HALF:PAD + NPT], LP[:, b + 1, 0:NPT - HALF], rstd[:, HALF:NPT],
                                      ALU.mult)
                    dve.tensor_tensor(row[:, 2 * PAD + NPT:UPAD], LP[:, b + 1, NPT - HALF:HALF], rstd[:, NPT:N],
                                      ALU.mult).then_inc(drained, 1)
            four_conv_rows(0)
            dve.wait_ge(gate_pe, 1)
            dve.tensor_tensor(two(gT[:, :]), MP[0:GATES, 0:2, 0:HALF], two(rstd[0:GATES, :]), ALU.mult
                              ).then_inc(gate_dve, 1)
            with dve.Fori(1, NCONV // 4) as i:
                four_conv_rows(i)
            for m in range(H):
                dve.wait_ge(product_done, ta + NCONV + m + 1)
                dve.tensor_tensor(two(z[:, m, :]), banks(m), two(rstd[:, :]), ALU.mult).then_inc(drained, 1)
            dve.wait_ge(gate_act, 3)
            dve.wait_ge(par_loaded, 16 * 16)

            def bc(i):
                return gate_par[:, i:i + 1, :].to_broadcast([128, NTOK, H])

            step(dve.tensor_tensor(G[:, :, H:2 * H], G[:, :, H:2 * H], bc(1), ALU.add))
            step(dve.tensor_tensor(G[:, :, 2 * H:3 * H], G[:, :, 2 * H:3 * H], bc(2), ALU.add))
            settled()
            step(dve.tensor_scalar(G[:, :, 0:H], G[:, :, 0:H], -1.0, None, ALU.mult))
            step(dve.tensor_scalar(G[:, :, 2 * H:3 * H], G[:, :, 2 * H:3 * H], -1.0, None, ALU.mult))
            settled()
            dve.tensor_scalar(Ga[:, :, :], G[:, :, :], -1.0, None, ALU.mult).then_inc(gate_dve, 1)
            dve.wait_ge(gate_dve, 3)
            dve.tensor_tensor(Gb[:, :, :], G[:, :, :], Ga[:, :, :], ALU.min).then_inc(gate_dve, 1)
            step(dve.tensor_scalar(G[:, :, :], G[:, :, :], 0.0, None, ALU.max))
            settled()
            dve.wait_ge(gate_act, 6)
            step(dve.tensor_tensor(Ga[:, :, :], G[:, :, :], Gb[:, :, :], ALU.add))
            settled()
            step(dve.tensor_scalar(G[:, :, 2 * H:3 * H], Ga[:, :, 2 * H:3 * H], -1.0, None, ALU.mult))
            step(dve.tensor_tensor(Gb[:, :, H:2 * H], Ga[:, :, H:2 * H], bc(0), ALU.mult))
            settled()
            step(dve.tensor_scalar(Gb[:, :, H:2 * H], Gb[:, :, H:2 * H], -1.0, None, ALU.mult))
            dve.tensor_copy(Gb[:, :, 0:H], Ga[:, :, 0:H]).then_inc(gate_dve, 2)
            dve.tensor_copy(conv_new[:, 0, :, :], ua[:, :, NPT:NPT + PAD].rearrange("p f i -> p i f"))
            dve.tensor_copy(conv_new[:, 1, :, :], ua[:, :, UPAD - PAD:UPAD].rearrange("p f i -> p i f")
                            ).then_inc(conv_dve, 2)
            tb = LIN["in_b"][1]
            for f in range(NCONV):
                dve.wait_ge(product_done, tb + f + 1)
                dve.tensor_tensor(two((kb_f, vb_f, qb_f)[f // H][:, f % H, :]), banks(f), two(rstd[:, :]), ALU.mult
                                  ).then_inc(drained, 1)
                if f >= 2:
                    dve.wait_ge(conv_act, 2 + f - 1)
                b, e = sq[:, f % 2, 0:NPT], sq[:, f % 2, NPT:N]
                for i in range(CW):
                    if i == 0:
                        dve.tensor_scalar(b, ua[:, f, 0:NPT], conv_w(0, f), None, ALU.mult)
                        inst = dve.tensor_scalar(e, ua[:, f, PAD + NPT:PAD + NPT + NS], conv_w(0, f), None, ALU.mult)
                    else:
                        dve.wait_ge(conv_dve, 2 + CW * f + i)
                        dve.scalar_tensor_tensor(out=b, in0=ua[:, f, i:i + NPT], scalar=conv_w(i, f), in1=b,
                                                 op0=ALU.mult, op1=ALU.add)
                        inst = dve.scalar_tensor_tensor(out=e, in0=ua[:, f, PAD + NPT + i:PAD + NPT + i + NS],
                                                        scalar=conv_w(i, f), in1=e, op0=ALU.mult, op1=ALU.add)
                    inst.then_inc(conv_dve, 1)

            def delta_scales(i):
                f = (i - 3) // 2
                if i % 2 and 0 <= f < 2 * H:
                    dve.wait_ge(head_exp, f + 1)
                    dve.scalar_tensor_tensor(out=ua[:, f, 0:N], in0=ua[:, f, 0:N], in1=rstd[:, :],
                                             scalar=HD ** -0.5 if f < H else 1.0, op0=ALU.mult, op1=ALU.mult
                                             ).then_inc(head_mul, 1)

            attention("fox_p", delta_scales)
            attention("fox_s")
            dve.wait_ge(gate_act, 7)
            dve.memset(S[:, 0, :, :], 0.0).then_inc(s_zero, 1)

            def rows(j):
                _, a, P = TOK[j]
                par = j % 2
                dve.wait_ge(row_act, j + 1)
                dve.tensor_tensor(gsm[0:P, par, 12:16], Gb[0:P, j, 0:H], gsm[0:P, par, 4:8], ALU.mult)
                dve.tensor_tensor(qe[:, par, :, 0:P], qe[:, par, :, 0:P], ua[:, 0:H, a:a + P], ALU.mult
                                  ).then_inc(row_dve, 1)

            def inverse(half, name, j):
                _, a, P = TOK[j]
                b0, b1, par, h0 = 2 * half, 2 * half + 1, j % 2, 2 * half
                hs = slice(h0, h0 + 2)

                def two_heads(bank, at):
                    return LP[0:P, bank, at:at + 2 * P].rearrange("p (h n) -> p h n", h=2)

                def over(m):
                    return m.rearrange("p (o n) -> p o n", o=1).to_broadcast([P, 2, P])

                def done(inst):
                    inst.then_inc(inv_dve[half], 1)

                def mask(s):
                    return dve.tensor_tensor(BT[0:P, hs, 0:P], LT[0:P, hs, 0:P],
                                             over(level[0:P, LEVELS.index(s), 0:P]), ALU.mult)

                if name == "gram":
                    dve.wait_ge(inv_act[half], count_of(INV["act"], "gram", j))
                    c = step(dve.tensor_tensor(LT[0:P, hs, 0:P], two_heads(b1, 0), dec[0:P, hs, 0:P], ALU.mult))
                    d_ = step(dve.tensor_tensor(AT[0:P, par, hs, 0:P], two_heads(b1, 2 * P), dec[0:P, hs, 0:P],
                                                ALU.mult))
                    after(c)
                    c = step(dve.tensor_tensor(LT[0:P, hs, 0:P], LT[0:P, hs, 0:P], two_heads(b0, 2 * P), ALU.mult))
                    after(c)
                    c = step(mask(1))
                    after(c)
                    done(dve.tensor_tensor(TmT[0:P, hs, 0:P], over(ident[0:P, 0:P]), BT[0:P, hs, 0:P], ALU.subtract))
                elif name == "turns":
                    dve.wait_ge(inv_dve[half], count_of(INV["dve"], "gram", j))
                    c = mask(2)
                    dve.wait_ge(row_dve, j + 1)
                    dve.wait_ge(inv_act[half], count_of(INV["act"], "turns", j))
                    for i in range(2):
                        dve.tensor_scalar(kbe[0:P, h0 + i, :], kn[0:P, h0 + i, :], gsm[0:P, par, 12 + h0 + i:13 + h0 + i],
                                          None, ALU.mult)
                        inst = dve.tensor_scalar(kd[0:P, par, h0 + i, :], kn[0:P, h0 + i, :],
                                                 gsm[0:P, par, 8 + h0 + i:9 + h0 + i], None, ALU.mult)
                    done(inst)
                elif name[:5] == "delta":
                    s = int(name[5:])
                    dve.wait_ge(inv_pe[half], count_of(INV["pe"], name, j))
                    dve.wait_ge(inv_dve[half], count_of(INV["dve"], "turns" if s == 2 else f"delta{s // 2}", j))
                    if s < SIZES[-1]:
                        dve.tensor_tensor(Tm[0:P, hs, 0:P], Tm[0:P, hs, 0:P], two_heads(b1, 0), ALU.subtract)
                        mask(2 * s)
                    done(dve.tensor_tensor(TmT[0:P, hs, 0:P], TmT[0:P, hs, 0:P], two_heads(b1, 2 * P), ALU.subtract))

            def recurrence(name, j):
                _, a, P = TOK[j]
                c, par = int(name[-1]), j % 2
                C = 64 if P == 128 else P
                r = slice(c * C, c * C + C)
                old, new = (2, 1) if j == TT else (c, 1 - c)
                if name[0] == "o":
                    return
                dve.wait_ge(rec_pe, count_of(REC["pe"], name, j))
                if name[:2] == "ws":
                    inst = dve.tensor_tensor(vnew[r, :, :], um[r, par, :, :],
                                             MP[r, 1, :].rearrange("p (h n) -> p h n", h=H), ALU.subtract)
                else:
                    if j or c:
                        dve.wait_ge(rec_dve, count_of(REC["dve"], f"ws{c}", j))
                    for h in range(H):
                        inst = dve.scalar_tensor_tensor(out=S[:, new, h, :], in0=S[:, old, h, :],
                                                        scalar=eg[:, par, c, h:h + 1],
                                                        in1=MP[:, 1, 128 * h:128 * h + 128], op0=ALU.mult, op1=ALU.add)
                inst.then_inc(rec_dve, 1)

            for j in range(NTOK + 1):
                if j == NTOK:
                    dve.wait_ge(s_loaded, 16)
                for what in delta_order(j):
                    if what[0] == "rows":
                        rows(j)
                    elif what[0] == "rec":
                        recurrence(what[1], j - 1)
                    else:
                        inverse(*what, j)
            for h in range(H + 1):
                if h < H:
                    f = 2 * H + h
                    dve.wait_ge(head_exp, f + 1)
                    dve.scalar_tensor_tensor(out=o_a[:, h, :], in0=o_a[:, h, :], scalar=column(ONORM),
                                             in1=(rstd, acc)[f % 2][:, :], op0=ALU.mult, op1=ALU.mult
                                             ).then_inc(head_mul, 1)
                    dve.wait_ge(head_mul, f + 1)
                    dve.tensor_tensor(o_a[:, h, :], o_a[:, h, :], z[:, h, :], ALU.mult).then_inc(head_y, 1)
                if h:
                    dve.wait_ge(head_hi, h)
                    dve.tensor_tensor(xl[:, h - 1, :], o_a[:, h - 1, :], xh[:, h - 1, :].bitcast(f32), ALU.subtract
                                      ).then_inc(low_done, 1)

            def layer_end(l):
                residual_product(f"out{l}")
                dve.wait_ge(mem_act, (KT + 1) * l + 1)
                for c in range(MEM // 128):
                    inst = dve.tensor_scalar(m_rows[:, c, :], m_rows[:, c, :], mem_rs[:, c:c + 1], None, ALU.mult)
                inst.then_inc(mem_dve, 1)
                for k in range(KT):
                    dve.wait_ge(mem_act, (KT + 1) * l + k + 2)
                    dve.scalar_tensor_tensor(out=ml[:, k, :], in0=MP[:, k % 2, 0:MEM], scalar=gain(7 + l, k),
                                             in1=mh[:, k, :].bitcast(f32), op0=ALU.mult, op1=ALU.subtract
                                             ).then_inc(mem_dve, 1)
                norm(3 * l + 1)
                _, t0, panels, tpp = LIN[f"mem{l}"]
                with dve.Fori(0, KT // 4) as i:
                    for m in range(4):
                        dve.wait_ge(product_done, t0 + 4 * i + m + 1)
                        dve.tensor_copy(kvT[:, bass.ds(4 * i + m, 1), :].rearrange("p o n -> p (o n)"),
                                        LP[:, 2 * (m % 2), 0:MEM]).then_inc(drained, 1)
                dve.wait_ge(rstd_ready, 3 * l + 2)
                t0 = LIN[f"xq{l}"][1]
                for m in range(H):
                    dve.wait_ge(product_done, t0 + m + 1)
                    dve.tensor_tensor(two(q_x[:, m, :]), banks(m), two(rstd[:, :]), ALU.mult).then_inc(drained, 1)
                attention(f"cross{l}")
                residual_product(f"xo{l}")
                norm(3 * l + 2)
                mlp(l)

            def mlp_block(l, b):
                t0, d0 = LIN[f"mlp{l}"][1], DRAINED[f"mlp{l}"]
                for k in range(KT):
                    hcount = KT * NB * l + KT * b + k
                    dve.wait_ge(relu_ready, hcount + 1)
                    if not (isinstance(hcount, int) and hcount < 2):
                        dve.wait_ge(h_ready, hcount - 1)
                    dve.tensor_tensor(hsq[:, k % 2, :], rel[:, k % 2, :], rel[:, k % 2, :], ALU.mult
                                      ).then_inc(hsq_ready, 1)
                    dve.wait_ge(hsq_ready, hcount + 1)
                    dve.wait_ge(hh_ready, hcount + 1)
                    dve.tensor_tensor(hl[:, k, :], hsq[:, k % 2, :], hh[:, k, :].bitcast(f32), ALU.subtract
                                      ).then_inc(h_ready, 1)
                base = NORM_BASE[3 * l + 2]
                for k in range(KT):
                    dve.wait_ge(product_done, t0 + 16 * b + KT + k + 1)
                    count = KT * NB * l + KT * b + k
                    if not (isinstance(count, int) and count < 2):
                        dve.wait_ge(x_done, base + KT + KT * b + k - 1)
                    dve.tensor_tensor(two(dtmp[:, k % 2, :]), banks(k), two(rstd[:, :]), ALU.mult
                                      ).then_inc(drained, 1)
                    dve.wait_ge(drained, d0 + KT * b + k + 1)
                    dve.tensor_tensor(x[:, k, :], x[:, k, :], dtmp[:, k % 2, :], ALU.add).then_inc(x_done, 1)

            def mlp(l):
                dve.wait_ge(rstd_ready, 3 * l + 3)
                mlp_block(l, 0)
                with dve.Fori(1, NB) as b:
                    mlp_block(l, b)

            layer_end(0)
            norm(3)
            dve.wait_ge(rstd_ready, 4)
            tc = LIN["in_c"][1]
            for m in range(12):
                dve.wait_ge(product_done, tc + m + 1)
                if m >= 8:
                    dst = (k_c, v_c)[(m - 8) // 2][:, m % 2, :]
                    dve.tensor_tensor(two(dst), banks(m), two(rstd[:, :]), ALU.mult).then_inc(drained, 1)
                    continue
                kv = m // 2
                o = (kv % 2) * 64
                for h in (2 * m, 2 * m + 1):
                    slot, ho = (h // 8) * 4 + h % 4, (h % 2) * 64
                    inst = dve.scalar_tensor_tensor(
                        out=two(q_c[o:o + 64, slot, :]), in0=LP[ho:ho + 64, 2 * (m % 2):2 * (m % 2) + 2, 0:HALF],
                        scalar=HDC ** -0.5, in1=two(rstd[ho:ho + 64, :]), op0=ALU.mult, op1=ALU.mult)
                inst.then_inc(drained, 1)
            attention("swa")
            layer_end(1)
            norm(6, last=True)
            dve.wait_ge(rstd_ready, 7)
            for k in range(KT):
                dve.scalar_tensor_tensor(out=yT[:, k, :], in0=x[:, k, :], scalar=gain(6, k), in1=rstd[:, :],
                                         op0=ALU.mult, op1=ALU.mult).then_inc(y_dve, 1)



def kernel(**inputs):
    import numpy as _np
    import concourse.bacc as _bacc
    from concourse import mybir as _mybir
    from concourse.bass_utils import run_bass_kernel_spmd as _run

    nc = _bacc.Bacc("TRN2", target_bir_lowering=False, num_devices=1)
    arrays, t = {}, {}
    for name, value in inputs.items():
        a = _np.ascontiguousarray(value)
        arrays[f"in_{name}"] = a
        t[name] = nc.dram_tensor(f"in_{name}", a.shape, _mybir.dt.from_np(a.dtype), kind="ExternalInput").ap()
    s = {k: tuple(v.shape) for k, v in inputs.items()}
    _, np_, d = s["x_prompt"]
    ns = s["x_sample"][1]
    _, _, h, dk, dv = s["state_gdn"]
    cw, cdim = s["state_gdn_conv"][2:]
    win, hkv, hdc = s["cache_swa_k"][2:]
    depth, _, mem, hx, hdx = s["cache_mem_k"]
    outs = [("y_prompt", (1, np_, d)), ("y_sample", (1, ns, d)),
            ("p_gdn_state", (1, 1, h, dk, dv)), ("p_gdn_conv", (1, 1, cw, cdim)),
            ("p_fox_k", (1, 1, np_, h, dk)), ("p_fox_v", (1, 1, np_, h, dk)), ("p_fox_logf", (1, 1, np_, h)),
            ("p_swa_k", (1, 1, win, hkv, hdc)), ("p_swa_v", (1, 1, win, hkv, hdc)),
            ("p_mem_k", (depth, 1, mem, hx, hdx)), ("p_mem_v", (depth, 1, mem, hx, hdx)),
            ("s_gdn_state", (1, 1, h, dk, dv)), ("s_gdn_conv", (1, 1, cw, cdim)),
            ("s_fox_k", (1, 1, ns, h, dk)), ("s_fox_v", (1, 1, ns, h, dk)), ("s_fox_logf", (1, 1, ns, h)),
            ("s_swa_k", (1, 1, ns, hkv, hdc)), ("s_swa_v", (1, 1, ns, hkv, hdc))]
    for name, shape in outs:
        t[f"o_{name}"] = nc.dram_tensor(f"o_{name}", shape, _mybir.dt.float32, kind="ExternalOutput").ap()
    build_program(nc, t)
    r = _run(nc, [arrays], core_ids=[0])
    return tuple(r.results[0][f"o_{name}"] for name, _ in outs)
```

```python
import concourse.bass as bass
from concourse import mybir
from contextlib import ExitStack


def build_program(nc, t):
    f32, f32r = mybir.dt.float32, mybir.dt.float32r
    ALU, ACT, AX = mybir.AluOpType, mybir.ActivationFunctionType, mybir.AxisListType

    D = t["x_prompt"].shape[2]
    NPT = t["x_prompt"].shape[1]
    NS = t["x_sample"].shape[1]
    N = NPT + NS
    HALF = N // 2
    KT = D // 128
    H = t["state_gdn"].shape[2]
    HD = 128
    NCONV = t["state_gdn_conv"].shape[3] // 128
    CW = t["conv_w_a"].shape[1]
    PAD = CW - 1
    PAST = t["cache_fox_k"].shape[2]
    WIN = t["cache_swa_k"].shape[2]
    HKV, HDC = t["cache_swa_k"].shape[3], t["cache_swa_k"].shape[4]
    HQ = t["sinks_c"].shape[1]
    MEM = t["mem_prompt"].shape[1]
    DFF = t["w_up"].shape[2]
    NB = DFF // D
    TT = NPT // 128
    NTOK = TT + 1
    EPS = 1e-6
    BIG = 1e30
    TOK = [(j, 128 * j, 128) for j in range(TT)] + [(TT, NPT, NS)]
    UPAD = PAD + NPT + PAD + NS
    GATES = 3 * H

    LIN = {}
    order = [("in_a", 8, 2), ("in_b", 6, 2)]
    for l in range(2):
        if l == 1:
            order += [("in_c", 6, 2)]
        order += [(f"out{l}", 4, 2), (f"mem{l}", 4, 2), (f"xq{l}", 2, 2), (f"xo{l}", 2, 4)]
        order += [(f"mlp{l}", 8 * NB, 2)]
    p = q = d = 0
    DRAINED = {}
    for name, panels, tpp in order:
        LIN[name] = (p, q, panels, tpp)
        DRAINED[name] = d
        p, q, d = p + panels, q + panels * tpp, d + panels * tpp // (2 if name[:3] == "mlp" else 1)
    PANELS = p

    def last_tile(name):
        return DRAINED[name] + LIN[name][2] * LIN[name][3]

    PER_LAYER = (2 + NB) * KT
    NORM_BASE = [0, KT, 2 * KT, PER_LAYER, PER_LAYER + KT, PER_LAYER + 2 * KT, 2 * PER_LAYER]
    LATE_FIRST = [4, 5, 6, 7, 0, 1, 2, 3]
    RES = {"out0": 1, "xo0": 2, "out1": 4, "xo1": 5}
    FIRST_MASKS = 4
    MASKS = 15 + 6 + 3 + 6 + 6 + 2 + 6 + 2
    GATE_LOGF = 6
    STORES_TOTAL = 2 + 2 * NTOK + 2 + 2 + 4 + 4

    ctx = ExitStack()
    with ctx:
        def sem(name):
            return ctx.enter_context(nc.semaphore(name))

        cursor = [(nc.sbuf_base + 31) // 32 * 32]

        def place(name, shape, dt=f32, at=None):
            size = 4
            for n in shape[1:]:
                size *= n
            size = (size + 31) // 32 * 32
            if at is None:
                at = cursor[0]
                cursor[0] += size
            return nc.alloc_sbuf_tensor_at(name, shape, dt, offset=at)

        x = place("x", [128, KT, N])
        xh_at = cursor[0]
        xh = place("xh", [128, KT, N], f32r)
        xl_at = cursor[0]
        xl = place("xl", [128, KT, N], f32r)
        stage = [place(f"stage{s}", [128, 2048]) for s in range(2)]
        wh = [place(f"wh{s}", [128, 2048], f32r) for s in range(2)]
        wl = [place(f"wl{s}", [128, 2048], f32r) for s in range(2)]
        rstd = place("rstd", [128, N])
        acc_at = cursor[0]
        acc = place("acc", [128, N])
        sq_at = cursor[0]
        sq = place("sq", [128, 2, N])
        probs3 = place("probs3", [128, 3, N], at=acc_at)
        probs4 = place("probs4", [128, 4, N], at=acc_at - 4 * N)
        ident = place("ident", [128, 128])
        ones = place("ones", [128, 128])
        upper = place("upper", [128, NPT])
        chunk_upper = place("chunk_upper", [128, 128])
        chunk_later = place("chunk_later", [128, 128])
        chunk_mask = place("chunk_mask", [128, 128])
        chunk_rows = place("chunk_rows", [128, 2, 128])
        LEVELS = [1, 2, 4, 8, 16, 32]
        level = place("level", [128, len(LEVELS), 128])
        diag_mask = place("diag_mask", [128, 128])
        dist_p = place("dist_p", [128, 256])
        dist_s = place("dist_s", [NS, WIN + NS])
        NROW = 9 * KT + CW * NCONV + 1
        cols = place("cols", [128, NROW])
        gate_par = place("gate_par", [128, 3, H])
        sinks = place("sinks", [128, HQ])
        eps_col = place("eps_col", [128, 1])
        one_col = place("one_col", [128, 1])
        nm = place("nm", [128, 3, 2])
        rs = place("rs", [128, 3, 2])
        rr = place("rr", [128, 3, 2])
        es = place("es", [128, 3, 2])
        neg_sinks = place("neg_sinks", [128, HQ])
        mem_ss = place("mem_ss", [128, 2])
        mem_rs = place("mem_rs", [128, 2])
        token_rstd = place("token_rstd", [128, NTOK])
        ARENA = cursor[0]
        peak = [ARENA]

        def arena(*parts):
            out, at = [], ARENA
            for part in parts:
                name, shape = part[0], part[1]
                dt = part[2] if len(part) > 2 else f32
                out.append(place(name, shape, dt, at=at))
                size = 4
                for n in shape[1:]:
                    size *= n
                at += (size + 31) // 32 * 32
            peak[0] = max(peak[0], at)
            return out

        x_rows, par_rows, conv_rows = arena(("x_rows", [128, NTOK, D]), ("par_rows", [NROW, 128]),
                                            ("conv_rows", [PAD * NCONV, 128]))
        (ua, z, vb_f, kb_f, qb_f, vb_n, nF, PT0) = arena(
            ("ua", [128, NCONV, UPAD]), ("z", [128, H, N]),
            ("vb_f", [128, H, N]), ("kb_f", [128, H, N]), ("qb_f", [128, H, N]),
            ("vb_n", [128, NTOK, H * HD]), ("nF", [128, H, N]),
            ("PT0", [128, 2, 5 * 128]))
        gates_at = peak[0] - 4 * 2 * 5 * 128
        size = 4 * KT * GATES
        w_gate = place("w_gate", [128, KT, GATES], at=gates_at)
        wgh = place("wgh", [128, KT, GATES], f32r, at=gates_at + size)
        wgl = place("wgl", [128, KT, GATES], f32r, at=gates_at + 2 * size)
        k_out = place("k_out", [128, TT, H * HD], at=peak[0] - 4 * (2 * 5 * 128 + H * N))
        conv_new = place("conv_new", [128, 2, PAD, NCONV], at=gates_at + 3 * size)
        conv_newT = place("conv_newT", [2 * NCONV * PAD, 128], at=gates_at + 3 * size + 512)
        gT = place("gT", [GATES, N], at=acc_at)
        delta_at = (ARENA + 4 * (NCONV * UPAD + H * N) + 31) // 32 * 32
        kpT = place("kpT", [128, H, PAST], at=xh_at)
        kp_rows = place("kp_rows", [128, PAST // 128, H * HD], at=xh_at + 4 * H * PAST)
        vp_n = place("vp_n", [128, PAST // 128, H * HD], at=xl_at)
        k_out_s = place("k_out_s", [NS, H * HD], at=gates_at + 3 * size + 1024)
        head_squares = place("head_squares", [128, 2, N], at=peak[0])
        gates_start = peak[0] + 4 * 2 * N

        def region(at):
            end = [at]

            def more(name, shape, dt=f32):
                b = place(name, shape, dt, at=end[0])
                size = 4
                for n in shape[1:]:
                    size *= n
                end[0] += (size + 31) // 32 * 32
                return b
            return more, end

        more, end = region(gates_start)
        gates_raw = more("gates_raw", [128, NTOK, GATES])
        gate_tmp = more("gate_tmp", [128, NTOK, GATES])
        gates = more("gates", [128, NTOK, GATES])
        lf_past = more("lf_past", [128, PAST // 128, H])
        peak[0] = max(peak[0], end[0])
        delta_buf, delta_end = region(delta_at)
        o_a = delta_buf("o_a", [128, H, N])
        LT, Tm, TmT, Xm, BT, kn, vbt, kbe, vnew = [
            delta_buf(n, [128, H, 128]) for n in ("LT", "Tm", "TmT", "Xm", "BT", "kn", "vbt", "kbe", "vnew")]
        dec = Xm
        AT, um, wT, qe, kd = [delta_buf(n, [128, 2, H, 128]) for n in ("AT", "um", "wT", "qe", "kd")]
        S = delta_buf("S", [128, 3, H, 128])
        gsm = delta_buf("gsm", [128, 2, 16])
        eg = delta_buf("eg", [128, 2, 2, H])
        assert delta_end[0] <= gates_start
        mem_buf, mem_end = region(delta_at + 4 * H * N)
        m_rows = mem_buf("m_rows", [128, 2, D])
        m_squares = place("m_squares", [128, D], at=mem_end[0])
        mh, ml = mem_buf("mh", [128, KT, MEM], f32r), mem_buf("ml", [128, KT, MEM], f32r)
        kx_rows, vx_rows = mem_buf("kx_rows", [128, 2, H * HD]), mem_buf("vx_rows", [128, 2, H * HD])
        peak[0] = max(peak[0], mem_end[0])
        (q_c, k_c, v_c, v_cn, kc_out, kc_rows, vc_rows, kcT, PTC) = arena(
            ("q_c", [128, 8, N]), ("k_c", [128, 2, N]), ("v_c", [128, 2, N]),
            ("v_cn", [128, NTOK, HKV * HDC]), ("kc_out", [128, 2, HKV * HDC]),
            ("kc_rows", [128, HKV * HDC]), ("vc_rows", [128, HKV * HDC]), ("kcT", [128, 2, WIN]),
            ("PTC", [128, 2, 5 * 128]))
        (kvT, kv_n, q_x, kxT, PTX) = arena(
            ("kvT", [128, KT, MEM]), ("kv_n", [128, 2, D]), ("q_x", [128, H, N]),
            ("kxT", [128, H, MEM]), ("PTX", [128, 2, 5 * 128]))
        hh, hl, rel, hsq, dtmp = arena(
            ("hh", [128, KT, N], f32r), ("hl", [128, KT, N], f32r), ("rel", [128, 2, N]),
            ("hsq", [128, 2, N]), ("dtmp", [128, 2, N]))
        y_rows, = arena(("y_rows", [128, NTOK, D]))
        yT = place("yT", [128, KT, N], at=xh_at)
        assert peak[0] <= nc.sbuf_usable_end, (peak[0], nc.sbuf_usable_end)

        LP = ctx.enter_context(nc.psum_tensor("LP", [128, 4, 512], f32))
        MP = ctx.enter_context(nc.psum_tensor("MP", [128, 4, 512], f32))

        def column(row):
            return cols[:, row:row + 1]

        def gain(norm, k):
            return column(norm * KT + k)

        def conv_w(i, f):
            return column(9 * KT + i * NCONV + f)

        ONORM = 9 * KT + CW * NCONV

        w_loaded = [sem(f"w_loaded{s}") for s in range(2)]
        w_hi = sem("w_hi")
        w_lo = sem("w_lo")
        product_done = sem("product_done")
        drained = sem("drained")
        x_loaded, par_loaded, mask_done = sem("x_loaded"), sem("par_loaded"), sem("mask_done")
        param_turned, param_ready = sem("param_turned"), sem("param_ready")
        x_turned, x_done = sem("x_turned"), sem("x_done")
        sq_ready, sq_used, xh_ready, xs_ready = sem("sq_ready"), sem("sq_used"), sem("xh_ready"), sem("xs_ready")
        stat_done, rstd_ready = sem("stat_done"), sem("rstd_ready")
        act_step, dve_step = sem("act_step"), sem("dve_step")
        stored = sem("stored")
        relu_ready, hh_ready, hsq_ready, h_ready = (sem("relu_ready"), sem("hh_ready"), sem("hsq_ready"),
                                                    sem("h_ready"))
        gate_pe, gate_act, gate_dve = sem("gate_pe"), sem("gate_act"), sem("gate_dve")
        conv_act, conv_dve = sem("conv_act"), sem("conv_dve")
        turn_pe, turn_act = sem("turn_pe"), sem("turn_act")
        sc_ready, nm_ready, ex_ready, rr_ready = sem("sc_ready"), sem("nm_ready"), sem("ex_ready"), sem("rr_ready")
        p_ready, second_ready, sink_ready = sem("p_ready"), sem("second_ready"), sem("sink_ready")
        tr_ready, pt_ready, o_ready, oh_ready, ol_ready = (sem("tr_ready"), sem("pt_ready"), sem("o_ready"),
                                                           sem("oh_ready"), sem("ol_ready"))
        inv_pe, inv_act, inv_dve = [[sem(f"inv_{e}{half}") for half in range(2)] for e in ("pe", "act", "dve")]
        rec_pe, rec_act, rec_dve = sem("rec_pe"), sem("rec_act"), sem("rec_dve")
        row_pe, row_act, row_dve = sem("row_pe"), sem("row_act"), sem("row_dve")
        s_loaded = sem("s_loaded")
        mem_loaded, mem_act, mem_dve, mem_pe = sem("mem_loaded"), sem("mem_act"), sem("mem_dve"), sem("mem_pe")
        cross_loaded, cross_turned, cross_copied = sem("cross_loaded"), sem("cross_turned"), sem("cross_copied")
        swa_loaded, swa_turned, swa_copied = sem("swa_loaded"), sem("swa_turned"), sem("swa_copied")
        y_scaled, y_turned, y_left, y_right, y_stored = (sem("y_scaled"), sem("y_turned"), sem("y_left"),
                                                         sem("y_right"), sem("y_stored"))
        arena_free = sem("arena_free")
        rows_pe, rows_act = sem("rows_pe"), sem("rows_act")
        head_sq, head_sum, head_ln, head_exp, head_mul = (sem("head_sq"), sem("head_sum"), sem("head_ln"),
                                                          sem("head_exp"), sem("head_mul"))
        head_y, head_hi = sem("head_y"), sem("head_hi")
        gate_in, vpast_in = sem("gate_in"), sem("vpast_in")
        kpast_in, conv_turned, conv_out = sem("kpast_in"), sem("conv_turned"), sem("conv_out")
        s_zero, low_done = sem("s_zero"), sem("low_done")

        UNITS, GROUP = [], {}

        def group(name, units):
            GROUP[name] = (len(UNITS), len(units))
            UNITS.extend(units)

        def probs_of(u, columns):
            U = UNITS[u]
            return (probs3[0:U["P"], u % 3, columns] if U["kind"] == "fox" else probs4[0:U["P"], u % 4, columns])

        def extra_lag(name):
            return 0 if name[:3] == "fox" else 1

        def unit(**kw):
            kw["G"], kw["nk"] = len(kw["q"]), sum(n for _, n in kw["keys"][0])
            return kw

        def fox_units(sample):
            out = []
            for h in range(H):
                hd = slice(h * HD, (h + 1) * HD)
                for j, a, P in (TOK[TT:] if sample else TOK[:TT]):
                    o = (slice(None), H + h, slice(a, a + P))
                    if sample:
                        keys = [(kpT[:, h, :], PAST), (kb_f[:, h, a:a + P], P)]
                        v = [(128, [vp_n[:, c, hd]]) for c in range(PAST // 128)] + [(P, [vb_n[0:P, j, hd]])]
                    else:
                        keys = [(kb_f[:, h, 0:a + P], a + P)]
                        v = [(128, [vb_n[:, c, hd]]) for c in range(j + 1)]
                    out.append(unit(kind="fox", h=h, P=P, q=[qb_f[:, h, a:a + P]], keys=[keys], scale=HD ** -0.5,
                                    PT=PT0, v=v, D=HD, hi=xh[o], lo=xl[o]))
            return out

        def cross_units():
            out = []
            for h in range(0, H, 2):
                for j, a, P in TOK:
                    kT = kvT if j < TT else kxT
                    vv = [(128, [(kv_n[:, c, (H + g) * HD:(H + g + 1) * HD] if j < TT else
                                  vx_rows[:, c, g * HD:(g + 1) * HD]) for g in (h, h + 1)])
                          for c in range(MEM // 128)]
                    o = (slice(None), slice(h, h + 2), slice(a, a + P))
                    out.append(unit(kind="cross", h=h, P=P, q=[q_x[:, g, a:a + P] for g in (h, h + 1)],
                                    keys=[[(kT[:, g, :], MEM)] for g in (h, h + 1)], scale=HD ** -0.5,
                                    PT=PTX, v=vv, D=HD, hi=xh[o], lo=xl[o]))
            return out

        def swa_units():
            out = []
            for h in [4 * g + e for g in range(HQ // 4) for e in range(2)]:
                kv = h // (HQ // HKV)
                o, kt_ = (kv % 2) * 64, kv // 2
                ho = (h % 2) * 64
                head_columns = slice(kv * HDC, (kv + 1) * HDC)
                for j, a, P in TOK:
                    first = max(j - 1, 0)
                    if j == TT:
                        keys = [(kcT[o:o + 64, kt_, :], WIN), (k_c[o:o + 64, kt_, a:a + P], P)]
                        vv = [(WIN, [vc_rows[:, head_columns]]), (P, [v_cn[0:P, j, head_columns]])]
                        dist = dist_s[:, :]
                    else:
                        n = a + 128 - 128 * first
                        keys = [(k_c[o:o + 64, kt_, 128 * first:a + 128], n)]
                        vv = [(128, [v_cn[:, c, head_columns]]) for c in range(first, j + 1)]
                        dist = dist_p[:, 256 - n:256]
                    oo = (slice(ho, ho + 64), slice(h // 2, h // 2 + 2), slice(a, a + P))
                    out.append(unit(kind="swa", h=h, P=P, dist=dist,
                                    q=[q_c[o:o + 64, (g // 8) * 4 + g % 4, a:a + P] for g in (h, h + 2)],
                                    keys=[keys, keys], scale=1.0, PT=PTC, v=vv, D=HDC, hi=xh[oo], lo=xl[oo]))
            return out

        group("fox_p", fox_units(False))
        group("fox_s", fox_units(True))
        group("cross0", cross_units())
        group("swa", swa_units())
        group("cross1", cross_units())

        def out_bank(U, u):
            bank = MP[0:U["D"], 2 + u % 2, 0:U["P"] * U["G"]]
            return bank.rearrange("p (g n) -> p g n", g=U["G"]) if U["G"] > 1 else bank

        SIZES = LEVELS[1:]
        INV = {"pe": ["gram", "turns"] + [f"{w}{s}" for s in SIZES for w in ("x", "delta")] + ["uw"],
               "act": ["gram", "turns"] + [f"x{s}" for s in SIZES] + ["uw"],
               "dve": ["gram", "lower1", "turns"] + [w for s in SIZES[:-1] for w in (f"lower{s}", f"delta{s}")] + [
                   f"delta{SIZES[-1]}"]}
        REC = {"pe": ["ws0", "ds0", "o0", "ws1", "ds1", "o1"], "dve": ["ws0", "ds0", "ws1", "ds1"]}

        def count_of(steps, name, j):
            return j * len(steps) + steps.index(name) + 1

        def delta_order(j):
            main = []
            if j < NTOK:
                main = [("rows",), (0, "gram"), (1, "gram"), (0, "turns"), (1, "turns"), (0, "x2"), (0, "delta2"),
                        (1, "x2")]
                for s in SIZES[1:]:
                    main += [(0, f"x{s}"), (1, f"delta{s // 2}"), (0, f"delta{s}"), (1, f"x{s}")]
                main += [(1, f"delta{SIZES[-1]}"), (0, "uw"), (1, "uw")]
            rec = []
            if j:
                nch = 2 if TOK[j - 1][2] == 128 else 1
                rec = [("rec", f"{w}{c}") for c in range(nch) for w in ("ws", "ds", "o")]
            out = []
            for i in range(max(len(main), 1)):
                out += main[i:i + 1]
                if i >= 3 and (i - 3) % 4 == 0 or not main:
                    out, rec = out + rec[:1], rec[1:]
            return out + rec

        MEM_PARTS = {4: (0, 1), 5: (2, 3, 4), 6: (5, 6, 7)}

        STORES = [0]

        block = ctx.enter_context(nc.Block())

        IN_B = (2, 3, 4, 5, 0, 1)

        def loads_of(name):
            l = int(name[-1]) if name[-1].isdigit() else 0
            if name in ("in_a", "in_b", "in_c", "mem0", "mem1", "xq0", "xq1", "out0", "out1"):
                w, c0 = {"in_a": (t["w_in_ab"][0], 0), "in_b": (t["w_in_ab"][0], 16 * 128 + 2 * H),
                         "in_c": (t["w_in_c"][0], 0), "mem": (t["w_xkv"][l], 0), "xq": (t["w_xq"][l], 0),
                         "out": (t["w_out_ab"][0] if l == 0 else t["w_out_c"][0], 0)}[
                             name if name in ("in_a", "in_b", "in_c") else name[:-1]]
                v = w.rearrange("(k p) n -> p k n", p=128)
                return lambda i: v[:, :, bass.ds(c0 + 256 * i, 256)]
            v = t["w_xo"][l].rearrange("(k p) n -> p k n", p=128)
            return lambda i: v[:, :, bass.ds(512 * i, 512)]

        @block.sync
        def _(sp):
            for j, a, P in TOK[:TT]:
                sp.dma_start(x_rows[:, j, :], t["x_prompt"][0, a:a + P, :]).then_inc(x_loaded, 16)
            sp.dma_start(x_rows[0:NS, TT, :], t["x_sample"][0]).then_inc(x_loaded, 16)
            row = 0
            for name, l in (("g_mix", 0), ("g_cross", 0), ("g_mlp", 0), ("g_mix", 1), ("g_cross", 1), ("g_mlp", 1),
                            ("g_final", None), ("g_mem", 0), ("g_mem", 1)):
                g = t[name] if l is None else t[name][l]
                sp.dma_start(par_rows[row:row + KT, :], g.rearrange("(k p) -> k p", p=128)).then_inc(par_loaded, 16)
                row += KT
            sp.dma_start(par_rows[row:row + CW * NCONV, :],
                         t["conv_w_a"][0].rearrange("i (f p) -> (i f) p", p=128)).then_inc(par_loaded, 16)
            row += CW * NCONV
            sp.dma_start(par_rows[row:row + 1, :], t["onorm_g_a"]).then_inc(par_loaded, 16)
            sp.dma_start(conv_rows[:, :], t["state_gdn_conv"][0, 0].rearrange("i (f p) -> (i f) p", p=128)
                         ).then_inc(par_loaded, 16)
            for i, name in enumerate(("a_log_a", "dt_bias_a", "f_bias_b")):
                sp.dma_start(gate_par[:, i, :], t[name][0].partition_broadcast(128)).then_inc(par_loaded, 16)
            sp.dma_start(sinks[:, :], t["sinks_c"][0].partition_broadcast(128)).then_inc(par_loaded, 16)

            def load(slot, source, kt, panel):
                if not (isinstance(panel, int) and panel < 2):
                    sp.wait_ge(w_lo, panel - 1)
                sp.dma_start(stage[slot][:, :].rearrange("p (k n) -> p k n", k=kt), source
                             ).then_inc(w_loaded[slot], 16)

            def first_pair(name, kt=KT):
                src = loads_of(name)
                load(0, src(0), kt, LIN[name][0])
                load(1, src(1), kt, LIN[name][0] + 1)

            def rest(name, kt=KT):
                p0, _, panels, _ = LIN[name]
                src = loads_of(name)
                if panels > 2:
                    with sp.Fori(1, panels // 2) as i:
                        load(0, src(2 * i), kt, p0 + 2 * i)
                        load(1, src(2 * i + 1), kt, p0 + 2 * i + 1)

            def product(name, kt=KT):
                first_pair(name, kt)
                rest(name, kt)

            def mlp(l):
                p0 = LIN[f"mlp{l}"][0]
                up_v = t["w_up"][l].rearrange("(k p) n -> p k n", p=128)
                dn_v = t["w_down"][l].rearrange("(k p) n -> p k n", p=128)
                with sp.Fori(0, NB) as b:
                    for i in range(4):
                        load(i % 2, up_v[:, :, bass.ds(b * D + 256 * i, 256)], KT, p0 + 8 * b + i)
                    for i in range(4):
                        load(i % 2, dn_v[:, bass.ds(b * KT, KT), 256 * i:256 * i + 256], KT, p0 + 8 * b + 4 + i)

            def memory_loads(l):
                sp.dma_start(m_rows[:, :, :], t["mem_prompt"][0].rearrange("(c p) d -> p c d", p=128)
                             ).then_inc(mem_loaded, 16)
                sp.dma_start(kx_rows[:, :, :], t["cache_mem_k"][l, 0].rearrange("(c p) h d -> p c (h d)", p=128)
                             ).then_inc(cross_loaded, 16)
                sp.dma_start(vx_rows[:, :, :], t["cache_mem_v"][l, 0].rearrange("(c p) h d -> p c (h d)", p=128)
                             ).then_inc(cross_loaded, 16)

            def layer_end(l):
                rest(f"out{l}")
                first_pair(f"mem{l}")
                rest(f"mem{l}")
                product(f"xq{l}")
                product(f"xo{l}", 4)
                mlp(l)

            load(1, loads_of("in_a")(1), KT, 1)
            sp.wait_ge(x_turned, KT)
            w = t["w_in_ab"][0].rearrange("(k p) n -> p k n", p=128)
            sp.dma_start(w_gate[:, :, 0:2 * H], w[:, :, 16 * 128:16 * 128 + 2 * H]).then_inc(gate_in, 16)
            sp.dma_start(w_gate[:, :, 2 * H:3 * H], w[:, :, w.shape[2] - H:w.shape[2]]).then_inc(gate_in, 16)
            sp.dma_start(lf_past[:, :, :], t["cache_fox_logf"][0, 0].rearrange("(c p) h -> p c h", p=128)
                         ).then_inc(gate_in, 16)
            rest("in_a")
            p0 = LIN["in_b"][0]
            src = loads_of("in_b")
            for i, panel in enumerate(IN_B):
                load(i % 2, src(panel), KT, p0 + i)
            first_pair("out0")
            sp.wait_ge(product_done, LIN["out0"][1])
            for dst, src_, signal in ((kp_rows, "cache_fox_k", kpast_in), (vp_n, "cache_fox_v", vpast_in)):
                sp.dma_start(dst[:, :, :], t[src_][0, 0].rearrange("(c p) h d -> p c (h d)", p=128)
                             ).then_inc(signal, 16)
            sp.wait_ge(arena_free, 1)
            memory_loads(0)
            layer_end(0)
            product("in_c")
            first_pair("out1")
            sp.wait_ge(drained, DRAINED["in_c"] + 4)
            sp.dma_start(kc_rows[:, :], t["cache_swa_k"][0, 0].rearrange("p h d -> p (h d)")).then_inc(swa_loaded, 16)
            sp.dma_start(vc_rows[:, :], t["cache_swa_v"][0, 0].rearrange("p h d -> p (h d)")).then_inc(swa_loaded, 16)
            memory_loads(1)
            layer_end(1)
            for j, a, P in TOK:
                sp.wait_ge(y_left, j + 1)
                sp.wait_ge(y_right, j + 1)
                sp.dma_start(t["o_y_prompt"][0, a:a + P, :] if j < TT else t["o_y_sample"][0], y_rows[0:P, j, :]
                             ).then_inc(y_stored, 16)
            sp.wait_ge(stored, 16 * STORES_TOTAL)
            sp.wait_ge(y_stored, 16 * NTOK)

        @block.gpsimd
        def _(pool):
            n = [0]

            def step(inst):
                inst.then_inc(mask_done, 1)
                n[0] += 1
                pool.wait_ge(mask_done, n[0])

            def low_parts(s, need):
                pool.wait_ge(w_hi, need)
                pool.tensor_tensor(wl[s][:, :], stage[s][:, :], wh[s][:, :].bitcast(f32), ALU.subtract
                                   ).then_inc(w_lo, 1)

            def select(m, pattern, base, mult, op, fill):
                step(pool.affine_select(out=m, in_=m, pattern=pattern, base=base, channel_multiplier=mult,
                                        compare_op=op, fill=fill))

            for m, v in ((ident, 0.0), (ones, 1.0), (eps_col, EPS)):
                step(pool.memset(m[:, :], v))
            select(ident[:, :], [[-1, 128]], 0, 1, ALU.not_equal, 1.0)
            assert n[0] == FIRST_MASKS, n[0]
            for s in range(2):
                low_parts(s, s + 1)
            for m, v in ((upper, 1.0), (chunk_upper, 1.0), (chunk_later, 1.0),
                         (chunk_mask, 0.0), (diag_mask, 0.0), (dist_p, 0.0), (dist_s, 0.0)):
                step(pool.memset(m[:, :], v))
            step(pool.memset(level[:, :, :], 0.0))
            step(pool.memset(gates_raw[:, :, :], 0.0))
            step(pool.memset(chunk_rows[:, :, :], 0.0))
            for c in range(2):
                step(pool.memset(chunk_rows[64 * c:64 * c + 64, c, :], 1.0))

            low_parts(0, 3)
            select(upper[:, :], [[1, NPT]], 0, -1, ALU.is_ge, 0.0)
            select(chunk_upper[:, :], [[1, 128]], 0, -1, ALU.is_ge, 0.0)
            select(chunk_mask[:, :], [[1, 128]], 0, -1, ALU.is_ge, -BIG)
            select(chunk_later[:, :], [[-1, 128]], -1, 1, ALU.is_ge, 0.0)
            select(diag_mask[:, :], [[-1, 128]], 0, 1, ALU.is_ge, -BIG)
            for m, v in ((chunk_upper, 0.0), (chunk_mask, -BIG)):
                select(m[0:64, 64:128], [[0, 64]], -1, 0, ALU.is_ge, v)
            select(chunk_later[64:128, 0:64], [[0, 64]], -1, 0, ALU.is_ge, 0.0)
            low_parts(1, 4)
            for n_, s in enumerate(LEVELS):
                part = level[:, n_, :].rearrange("p (b r c) -> p b r c", r=2, c=s)[:, :, 1, :]
                step(pool.memset(part, 1.0))
            for n_, s in enumerate(LEVELS):
                part = level[:, n_, :].rearrange("p (b r c) -> p b r c", r=2, c=s)[:, :, 1, :]
                select(part, [[-2 * s, 64 // s], [0, s]], 0, 1, ALU.is_ge, 0.0)
            step(pool.iota(dist_p[:, :], [[-1, 256]], base=128, channel_multiplier=1,
                           allow_small_or_imprecise_dtypes=True))
            step(pool.iota(dist_s[:, :], [[-1, WIN + NS]], base=WIN, channel_multiplier=1,
                           allow_small_or_imprecise_dtypes=True))
            for n_, s in enumerate(LEVELS):
                part = level[:, n_, :].rearrange("p (b r c) -> p b r c", r=2, c=s)[:, :, 1, :]
                select(part, [[2 * s, 64 // s], [0, s]], s - 1, -1, ALU.is_ge, 0.0)
            step(pool.memset(dist_p[0:64, 192:256], BIG))
            step(pool.memset(dist_p[64:128, 0:64], BIG))
            assert n[0] == MASKS, n[0]

            with pool.Fori(2, PANELS // 2) as i:
                for s in range(2):
                    low_parts(s, 2 * i + s + 1)

        @block.tensor
        def _(pe):
            TOKENS = ((0, HALF), (HALF, N))

            def block(slot, s, col, k, first, last, kt, halves, X):
                for n_, (w, part) in enumerate(((wh, 0), (wh, 1), (wl, 0))):
                    weights = w[s][:, :].rearrange("p (k n) -> p k n", k=kt)[:, k, col:col + 128]
                    for half, (a, b) in enumerate(halves):
                        mm = pe.matmul(LP[:, 2 * slot + half, 0:b - a], weights, X[part][:, k, a:b],
                                       start=(first and n_ == 0), stop=(last and n_ == 2), skip_group_check=True)
                if last:
                    mm.then_inc(product_done, 1)

            def pair(free, Pn, tpp, kt, halves, X, ready, after_first=None, order=None, between=None):
                order, LAG = order or list(range(kt)), 5

                def wait_free(tile_n):
                    if free(tile_n) is not None:
                        pe.wait_ge(*free(tile_n))

                for s in range(2):
                    if s and between is not None:
                        between()
                    pe.wait_ge(w_lo, Pn + s + 1)
                    if s == 0 and ready is not None:
                        wait_free(0)
                        for i in range(kt + LAG):
                            if i < kt:
                                ready(i)
                                block(0, s, 0, order[i], i == 0, i == kt - 1, kt, halves, X)
                            if i == kt and after_first is not None:
                                after_first()
                            if i == LAG:
                                wait_free(1)
                            if i >= LAG:
                                block(1, s, 128, order[i - LAG], i == LAG, i == kt + LAG - 1, kt, halves, X)
                    for i in range(2 if s == 0 and ready is not None else 0, tpp):
                        tile_n = s * tpp + i
                        wait_free(tile_n)
                        for k in range(kt):
                            block(tile_n % 2, s, 128 * i, k, k == 0, k == kt - 1, kt, halves, X)

            def reads(signal, base):
                return lambda i: pe.wait_ge(signal, base + i + 1)

            def one_pair(name, i, X, ready=None, kt=KT, halves=TOKENS, after_first=None, order=None,
                         between=None):
                p0, _, _, tpp = LIN[name]
                d0 = DRAINED[name] + 2 * tpp * i
                pair(lambda n_: (drained, d0 + n_ - 1) if not isinstance(d0, int) or d0 + n_ >= 2 else None,
                     p0 + 2 * i, tpp, kt, halves, X, ready, after_first, order, between)

            def rest(name, X, kt=KT, halves=TOKENS):
                panels = LIN[name][2]
                if panels > 2:
                    with pe.Fori(1, panels // 2) as i:
                        one_pair(name, i, X, None, kt, halves)

            def product(name, X, ready, kt=KT, halves=TOKENS, after_first=None):
                one_pair(name, 0, X, ready, kt, halves, after_first)
                rest(name, X, kt, halves)

            def stat(n):
                def go():
                    pe.wait_ge(sq_used, KT * (n + 1))
                    if n:
                        pe.wait_ge(rstd_ready, n)
                    for half, (a, b) in enumerate(TOKENS):
                        mm = pe.matmul(MP[:, half, 0:HALF], ones[:, :], acc[:, a:b], start=True, stop=True)
                    mm.then_inc(stat_done, 1)
                return go

            XS = (xh, xl)

            def attention(name, also=lambda i: None):
                u0, count = GROUP[name]

                def scores(u):
                    U = UNITS[u]
                    if u >= 2:
                        pe.wait_ge(ex_ready if UNITS[u - 2]["kind"] == "cross" else nm_ready, u - 1)
                    for g in range(U["G"]):
                        at = g * U["nk"]
                        for kT, n in U["keys"][g]:
                            mm = pe.matmul(LP[0:U["P"], 2 * (u % 2) + at // 512, at % 512:at % 512 + n], U["q"][g],
                                           kT, start=True, stop=True, skip_group_check=True)
                            at += n
                    mm.then_inc(sc_ready, 1)

                def turn(u):
                    U = UNITS[u]
                    P, G_ = U["P"], U["G"]
                    pe.wait_ge(p_ready, u + 1)
                    if U["kind"] == "swa":
                        pe.wait_ge(second_ready, u - GROUP["swa"][0] + 1)
                    if u >= 2:
                        pe.wait_ge(pt_ready, u - 1)
                    for g in range(G_):
                        at = g * U["nk"]
                        for c, (n, _) in enumerate(U["v"]):
                            to = (c * G_ + g) * P
                            mm = pe.transpose(MP[0:n, u % 2, to:to + P], probs_of(u, slice(at, at + n)),
                                              ident[0:P, 0:P])
                            at += n
                    mm.then_inc(tr_ready, 1)

                def values(u):
                    U = UNITS[u]
                    P, G_, last = U["P"], U["G"], len(U["v"]) - 1
                    pe.wait_ge(pt_ready, u + 1)
                    if u >= 2:
                        pe.wait_ge(ol_ready, u - 1)
                    shared = len(U["v"][0][1]) < G_
                    for g in range(1 if shared else G_):
                        w = (G_ if shared else 1) * P
                        for c, (n, v) in enumerate(U["v"]):
                            at = (c * G_ + g) * P
                            mm = pe.matmul(MP[0:U["D"], 2 + u % 2, g * P:g * P + w], v[g],
                                           U["PT"][0:n, u % 2, at:at + w], start=(c == 0), stop=(c == last),
                                           skip_group_check=True)
                    mm.then_inc(o_ready, 1)

                lag = 2 + extra_lag(name)
                for i in range(-1, count + lag + 1):
                    if lag <= i < count + lag:
                        turn(u0 + i - lag)
                    if i > lag:
                        values(u0 + i - lag - 1)
                    if i + 1 < count:
                        scores(u0 + i + 1)
                    also(i)

            pe.wait_ge(mask_done, FIRST_MASKS)
            pe.wait_ge(par_loaded, 16 * 16)
            pe.transpose(MP[:, 3, 256:256 + NROW], par_rows[:, :], ident[0:NROW, 0:NROW])
            pe.transpose(MP[:, 3, 384:384 + PAD * NCONV], conv_rows[:, :], ident[0:PAD * NCONV, 0:PAD * NCONV])
            pe.wait_ge(x_loaded, 16 * NTOK)
            for k in range(KT):
                mm = pe.transpose(MP[:, 3, NS * k:NS * k + NS], x_rows[0:NS, TT, 128 * k:128 * k + 128],
                                  ident[0:NS, 0:NS])
            mm.then_inc(param_turned, 1)

            def turn_x(k):
                if k >= 3:
                    pe.wait_ge(x_done, k - 2)
                for j, a, P in TOK[:TT]:
                    mm = pe.transpose(MP[:, k % 3, a:a + P], x_rows[0:P, j, 128 * k:128 * k + 128], ident[:, :])
                mm.then_inc(x_turned, 1)

            for k in range(3):
                turn_x(k)

            def first_stat():
                pe.wait_ge(x_done, KT)
                pe.wait_ge(param_ready, 2)
                stat(0)()

            def first_reads(i):
                if i + 3 < KT:
                    turn_x(i + 3)
                pe.wait_ge(xs_ready, i + 1)

            one_pair("in_a", 0, XS, first_reads, after_first=first_stat)
            pe.wait_ge(gate_act, 1)
            pe.wait_ge(gate_dve, 1)
            pe.wait_ge(rstd_ready, 1)
            for k in range(KT):
                for n_, (w, X) in enumerate(((wgh, xh), (wgh, xl), (wgl, xh))):
                    for half, (a, b) in enumerate(TOKENS):
                        mm = pe.matmul(MP[0:GATES, half, 0:HALF], w[:, k, :], X[:, k, a:b],
                                       start=(k == 0 and n_ == 0), stop=(k == KT - 1 and n_ == 2))
            mm.then_inc(gate_pe, 1)
            rest("in_a", XS)
            pe.wait_ge(mask_done, MASKS)
            pe.wait_ge(gate_dve, 2)
            for j, a, P in TOK:
                mm = pe.transpose(MP[0:P, 2, GATES * j:GATES * j + GATES], gT[:, a:a + P], ident[0:GATES, 0:GATES])
            mm.then_inc(gate_pe, 1)

            def turned(n_, P, source):
                if n_ >= 4:
                    pe.wait_ge(turn_act, n_ - 3)
                for h in range(H):
                    mm = pe.transpose(MP[0:P, n_ % 4, 128 * h:128 * h + 128], source(h), ident[:, :])
                mm.then_inc(turn_pe, 1)

            one_pair("in_b", 0, XS)
            pe.wait_ge(conv_dve, 1)
            pe.transpose(MP[0:2 * NCONV * PAD, 3, 0:128], conv_new[:, :, :, :].rearrange("p a i f -> p (a i f)"),
                         ident[:, :]).then_inc(conv_turned, 1)
            one_pair("in_b", 1, XS)
            pe.wait_ge(gate_act, 3)
            pe.wait_ge(conv_out, 1)
            for j, a, P in TOK:
                turned(j, P, lambda h: kb_f[:, h, a:a + P])

            def turn_values():
                for j, a, P in TOK:
                    turned(NTOK + j, P, lambda h: vb_f[:, h, a:a + P])

            one_pair("in_b", 2, XS, between=turn_values)

            def forget_rows(sample):
                pe.wait_ge(gate_dve, GATE_LOGF)
                if sample:
                    pe.wait_ge(ol_ready, GROUP["fox_p"][0] + GROUP["fox_p"][1])
                    pe.wait_ge(gate_in, 16 * 3)
                    pe.wait_ge(vpast_in, 16)
                for h in range(H):
                    if h >= 2:
                        pe.wait_ge(rows_act, (H if sample else 0) + h - 1)
                    b = 2 * (h % 2)
                    nt = NTOK if sample else TT
                    for j in range(nt):
                        if not sample:
                            lf, P = gates_raw[:, j, 2 * H + h:2 * H + h + 1], 128
                        elif j < TT:
                            lf, P = lf_past[:, j, h:h + 1], 128
                        else:
                            lf, P = gates_raw[0:NS, TT, 2 * H + h:2 * H + h + 1], NS
                        if j < TT:
                            mm = pe.matmul(LP[:, b, 128 * j:512], lf.to_broadcast([P, 128]),
                                           upper[0:P, 0:512 - 128 * j], start=(j == 0),
                                           stop=(j == TT - 1), skip_group_check=True)
                        if sample:
                            m = (ones[:, 0:NS] if j < TT else upper[0:NS, 0:NS])
                            mm = pe.matmul(LP[:, b + 1, 0:NS], lf.to_broadcast([P, 128]), m,
                                           start=(j == 0), stop=(j == TT), skip_group_check=True)
                    mm.then_inc(rows_pe, 1)

            pe.wait_ge(drained, last_tile("in_b"))
            forget_rows(False)
            pe.wait_ge(kpast_in, 16)
            for c in range(PAST // 128):
                turned(2 * NTOK + c, 128, lambda h: kp_rows[:, c, 128 * h:128 * h + 128])
            pe.wait_ge(turn_act, 2 * NTOK + PAST // 128)
            pe.wait_ge(rows_act, H)

            def delta_sums(i):
                f = (i - 2) // 2
                if i % 2 or not 0 <= f < 2 * H:
                    return
                pe.wait_ge(head_sq, f + 1)
                if f:
                    pe.wait_ge(head_ln, f)
                for half, (a, b) in enumerate(TOKENS):
                    mm = pe.matmul(LP[:, 1 + 2 * half, 0:HALF], ones[:, :], head_squares[:, f % 2, a:b],
                                   start=True, stop=True)
                mm.then_inc(head_sum, 1)

            attention("fox_p", delta_sums)
            pe.wait_ge(head_ln, 2 * H)
            forget_rows(True)
            pe.wait_ge(rows_act, 2 * H)
            attention("fox_s")
            pe.wait_ge(ol_ready, GROUP["fox_s"][0] + GROUP["fox_s"][1])
            pe.wait_ge(head_mul, 2 * H)
            pe.wait_ge(conv_act, 2 + NCONV)
            pe.wait_ge(gate_act, 7)

            def rows(j):
                _, a, P = TOK[j]
                nch = 2 if P == 128 else 1
                if j:
                    pe.wait_ge(row_act, j)
                if j >= 2:
                    pe.wait_ge(rec_dve, count_of(REC["dve"], "ds1", j - 2))
                    pe.wait_ge(rec_act, j - 1)
                for h in range(H):
                    pe.matmul(MP[:, 0, h * P:h * P + P], gates[0:P, j, H + h:H + h + 1].to_broadcast([P, 128]),
                              chunk_upper[0:P, 0:P], start=True, stop=True, skip_group_check=True)
                g4 = gates[0:P, j, H:2 * H]
                pe.matmul(MP[0:P, 3, 0:4], chunk_upper[0:P, 0:P], g4, start=True, stop=True, skip_group_check=True)
                pe.matmul(MP[0:P, 3, 4:8], chunk_later[0:P, 0:P], g4, start=True, stop=True, skip_group_check=True)
                for c in range(nch):
                    mm = pe.matmul(MP[:, 3, 8 + 4 * c:12 + 4 * c], chunk_rows[0:P, c, :], g4,
                                   start=True, stop=True, skip_group_check=True)
                mm.then_inc(row_pe, 1)

            def inverse(half, name, j):
                _, a, P = TOK[j]
                b0, b1 = 2 * half, 2 * half + 1
                heads = (2 * half, 2 * half + 1)

                def dve_at(step_, jj=j):
                    pe.wait_ge(inv_dve[half], count_of(INV["dve"], step_, jj))

                def act_at(step_, jj=j):
                    pe.wait_ge(inv_act[half], count_of(INV["act"], step_, jj))

                def mm_(out, lhsT, rhs, start=True, stop=True):
                    return pe.matmul(out, lhsT, rhs, start=start, stop=stop, skip_group_check=True)

                if name == "gram":
                    if j:
                        act_at("uw", j - 1)
                        dve_at("delta32", j - 1)
                    for i, h in enumerate(heads):
                        g = gates[0:P, j, H + h:H + h + 1].to_broadcast([P, P])
                        kT, qT = ua[:, H + h, a:a + P], ua[:, h, a:a + P]
                        mm_(LP[0:P, b0, i * P:i * P + P], g, chunk_upper[0:P, 0:P], stop=False)
                        mm_(LP[0:P, b0, i * P:i * P + P], ident[0:P, 0:P], chunk_mask[0:P, 0:P], start=False)
                        mm_(LP[0:P, b0, (2 + i) * P:(3 + i) * P], gates[0:P, j, h:h + 1].to_broadcast([P, P]),
                            ident[0:P, 0:P])
                        mm_(LP[0:P, b1, i * P:i * P + P], kT, kT)
                        mm = mm_(LP[0:P, b1, (2 + i) * P:(3 + i) * P], kT, qT)
                elif name == "turns":
                    dve_at("gram")
                    for i, h in enumerate(heads):
                        pe.transpose(LP[0:P, b0, 128 * i:128 * i + 128], ua[:, H + h, a:a + P], ident[:, :])
                        pe.transpose(LP[0:P, b0, 256 + 128 * i:384 + 128 * i], ua[:, 2 * H + h, a:a + P], ident[:, :])
                        mm = pe.transpose(LP[0:P, b1, P * i:P * i + P], TmT[0:P, h, 0:P], ident[0:P, 0:P])
                elif name[0] == "x":
                    s = int(name[1:])
                    if s == 2:
                        act_at("turns")
                    dve_at(f"lower{s // 2}")
                    for i, h in enumerate(heads):
                        mm = mm_(LP[0:P, b0, i * P:i * P + P], BT[0:P, h, 0:P], Tm[0:P, h, 0:P])
                elif name[:5] == "delta":
                    act_at("x" + name[5:])
                    dve_at("gram" if name == "delta2" else f"delta{int(name[5:]) // 2}")
                    for i, h in enumerate(heads):
                        if name != "delta32":
                            mm_(LP[0:P, b1, i * P:i * P + P], TmT[0:P, h, 0:P], Xm[0:P, h, 0:P])
                        mm = mm_(LP[0:P, b1, (2 + i) * P:(3 + i) * P], Xm[0:P, h, 0:P], TmT[0:P, h, 0:P])
                else:
                    dve_at("delta32")
                    for i, h in enumerate(heads):
                        mm_(LP[0:P, b0, 128 * i:128 * i + 128], TmT[0:P, h, 0:P], vbt[0:P, h, :])
                        mm = mm_(LP[:, b0, 256 + P * i:256 + P * i + P], kbe[0:P, h, :], TmT[0:P, h, 0:P])
                mm.then_inc(inv_pe[half], 1)

            def recurrence(name, j):
                _, a, P = TOK[j]
                c, par = int(name[-1]), j % 2
                C = 64 if P == 128 else P
                r = slice(c * C, c * C + C)
                old = 2 if j == TT else c
                if name[:2] == "ws":
                    if c == 0:
                        for half in range(2):
                            pe.wait_ge(inv_act[half], count_of(INV["act"], "uw", j))
                        pe.wait_ge(row_dve, j + 1)
                        if j:
                            pe.wait_ge(rec_dve, count_of(REC["dve"], "ds1", j - 1))
                        else:
                            pe.wait_ge(s_zero, 1)
                        if j == TT:
                            pe.wait_ge(s_loaded, 16)
                    else:
                        pe.wait_ge(rec_dve, count_of(REC["dve"], "ds0", j))
                    for h in range(H):
                        mm = pe.matmul(MP[0:P, 1, 128 * h:128 * h + 128], wT[:, par, h, 0:P], S[:, old, h, :],
                                       start=True, stop=True, skip_group_check=True)
                elif name[:2] == "ds":
                    pe.wait_ge(rec_dve, count_of(REC["dve"], f"ws{c}", j))
                    for h in range(H):
                        mm = pe.matmul(MP[:, 1, 128 * h:128 * h + 128], kd[r, par, h, :], vnew[r, h, :],
                                       start=True, stop=True, skip_group_check=True)
                else:
                    if j and c == 0:
                        pe.wait_ge(rec_act, j)
                    for h in range(H):
                        o = MP[:, 2, P * h + c * C:P * h + c * C + C]
                        pe.matmul(o, S[:, old, h, :], qe[:, par, h, r], start=True, stop=False, skip_group_check=True)
                        mm = pe.matmul(o, vnew[r, h, :], AT[r, par, h, r], start=False, stop=True,
                                       skip_group_check=True)
                mm.then_inc(rec_pe, 1)

            for j in range(NTOK + 1):
                for what in delta_order(j):
                    if what[0] == "rows":
                        rows(j)
                    elif what[0] == "rec":
                        recurrence(what[1], j - 1)
                    else:
                        inverse(*what, j)
            pe.wait_ge(rec_act, NTOK)
            def out0_reads(i):
                if i == H:
                    for f in range(2 * H, 3 * H):
                        pe.wait_ge(head_sq, f + 1)
                        if f >= 2 * H + 2:
                            pe.wait_ge(head_mul, f - 1)
                        for half, (a, b) in enumerate(TOKENS):
                            mm = pe.matmul(MP[:, 2 * (f % 2) + half, 0:HALF], ones[:, :], sq[:, f % 2, a:b],
                                           start=True, stop=True)
                        mm.then_inc(head_sum, 1)
                if i >= H:
                    pe.wait_ge(low_done, i - H + 1)

            def layer_end(l):
                if l == 0:
                    one_pair("out0", 0, XS, out0_reads, order=LATE_FIRST)
                    pe.wait_ge(head_ln, 3 * H)
                else:
                    one_pair("out1", 0, XS)
                pe.wait_ge(mem_dve, (KT + 1) * l + 1)
                for k in range(KT):
                    for c in range(MEM // 128):
                        at = MEM * (k // 4) + 128 * c
                        mm = pe.transpose(MP[:, k % 4, at:at + 128], m_rows[:, c, 128 * k:128 * k + 128], ident[:, :])
                mm.then_inc(mem_pe, 1)
                rest(f"out{l}", XS)
                pe.wait_ge(mem_dve, (KT + 1) * (l + 1))
                one_pair(f"mem{l}", 0, (mh, ml), halves=((0, MEM),))
                pe.wait_ge(cross_loaded, 32 * (l + 1))
                for h in range(H):
                    for c in range(MEM // 128):
                        mm = pe.transpose(MP[:, h // 2, 256 * (h % 2) + 128 * c:256 * (h % 2) + 128 * c + 128],
                                          kx_rows[:, c, 128 * h:128 * h + 128], ident[:, :])
                mm.then_inc(cross_turned, 1)
                rest(f"mem{l}", (mh, ml), halves=((0, MEM),))
                pe.wait_ge(drained, last_tile(f"mem{l}"))
                pe.wait_ge(cross_copied, 2 * l + 1)
                for c in range(MEM // 128):
                    for k in range(KT):
                        mm = pe.transpose(MP[:, 2 * c + k // 4, 128 * (k % 4):128 * (k % 4) + 128],
                                          kvT[:, k, 128 * c:128 * c + 128], ident[:, :])
                mm.then_inc(cross_turned, 1)

                def cross_stat():
                    pe.wait_ge(cross_copied, 2 * l + 2)
                    stat(3 * l + 1)()

                product(f"xq{l}", XS, reads(xs_ready, KT * (3 * l + 1)), after_first=cross_stat)
                pe.wait_ge(rstd_ready, 3 * l + 2)
                pe.wait_ge(drained, last_tile(f"xq{l}"))
                attention(f"cross{l}")
                pe.wait_ge(ol_ready, sum(GROUP[f"cross{l}"]))
                product(f"xo{l}", XS, None, kt=4)
                mlp(l)

            def mlp_block(l, b, after_first):
                P_ = LIN[f"mlp{l}"][0] + 8 * b
                relus, downs = KT * NB * l + KT * b, DRAINED[f"mlp{l}"] + KT * b

                def free(k):
                    if k < 2:
                        return drained, downs - 1 + k
                    if k < KT + 2:
                        return relu_ready, relus + k - 1
                    return drained, downs + k - KT - 1

                pair(free, P_, 2, KT, TOKENS, XS, reads(xs_ready, KT * (3 * l + 2)) if after_first else None,
                     after_first, LATE_FIRST)
                pair(lambda n_: free(4 + n_), P_ + 2, 2, KT, TOKENS, XS, None)
                pair(lambda n_: free(8 + n_), P_ + 4, 2, KT, TOKENS, (hh, hl), reads(h_ready, relus))
                pair(lambda n_: free(12 + n_), P_ + 6, 2, KT, TOKENS, (hh, hl), None)

            def mlp(l):
                mlp_block(l, 0, stat(3 * l + 2))
                with pe.Fori(1, NB) as b:
                    mlp_block(l, b, None)

            layer_end(0)
            product("in_c", XS, reads(xs_ready, KT * 3), after_first=stat(3))
            pe.wait_ge(drained, last_tile("in_c"))
            pe.wait_ge(swa_loaded, 32)
            for c in range(2):
                mm = pe.transpose(LP[:, 0, 128 * c:128 * c + 128], kc_rows[:, 128 * c:128 * c + 128], ident[:, :])
            mm.then_inc(swa_turned, 1)
            for j, a, P in TOK:
                if j >= 2:
                    pe.wait_ge(swa_copied, 1 + j - 1)
                for c in range(2):
                    pe.transpose(MP[0:P, 2 * (j % 2), 128 * c:128 * c + 128], k_c[:, c, a:a + P], ident[:, :])
                    mm = pe.transpose(MP[0:P, 2 * (j % 2) + 1, 128 * c:128 * c + 128], v_c[:, c, a:a + P],
                                      ident[:, :])
                mm.then_inc(swa_turned, 1)
            pe.wait_ge(swa_copied, 1 + NTOK)
            attention("swa")
            pe.wait_ge(ol_ready, sum(GROUP["swa"]))
            layer_end(1)
            for j, a, P in TOK:
                if j == 0:
                    pe.wait_ge(y_scaled, KT)
                if j >= 2:
                    pe.wait_ge(y_left, j - 1)
                    pe.wait_ge(y_right, j - 1)
                for k in range(KT):
                    mm = pe.transpose(LP[0:P, 2 * (j % 2) + k // 4, 128 * (k % 4):128 * (k % 4) + 128],
                                      yT[:, k, a:a + P], ident[:, :])
                mm.then_inc(y_turned, 1)
                if j == 0:
                    pe.wait_ge(sq_used, KT * 7)
                    pe.wait_ge(rstd_ready, 6)
                    for i, at, Q in TOK:
                        mm = pe.matmul(MP[0:Q, 0, i:i + 1], acc[:, at:at + Q], ones[:, 0:1], start=True, stop=True,
                                       skip_group_check=True)
                    mm.then_inc(stat_done, 1)

        @block.scalar
        def _(act):
            n = [0]

            def step(inst):
                inst.then_inc(act_step, 1)
                n[0] += 1

            def settled():
                act.wait_ge(act_step, n[0])

            def store(dst, src):
                act.dma_start(dst, src).then_inc(stored, 16)
                STORES[0] += 1

            def split(s, need):
                act.wait_ge(w_loaded[s], need)
                act.copy(wh[s][:, :], stage[s][:, :]).then_inc(w_hi, 1)

            def splits(p0, t0, tpp, i):
                for s in range(2):
                    act.wait_ge(product_done, t0 + 2 * tpp * i + tpp * (s + 1))
                    split(s, 16 * (p0 // 2 + 2) + 16 * i)

            def split_after(name, T):
                p0, t0, _, tpp = LIN[name]
                P_ = p0 + T // tpp
                act.wait_ge(product_done, t0 + T + 1)
                split(P_ % 2, 16 * (P_ // 2 + 2))

            def product(name):
                p0, t0, panels, tpp = LIN[name]
                with act.Fori(0, panels // 2) as i:
                    splits(p0, t0, tpp, i)

            def square(n_, k):
                act.wait_ge(x_done, NORM_BASE[n_] + k + 1)
                if k >= 2:
                    act.wait_ge(sq_used, KT * n_ + k - 1)
                act.activation(sq[:, k % 2, :], x[:, k, :], ACT.Square).then_inc(sq_ready, 1)

            def high_part(n_, k):
                act.wait_ge(x_done, NORM_BASE[n_] + k + 1)
                act.activation(xh[:, k, :], x[:, k, :], ACT.Copy, scale=gain(n_, k)).then_inc(xh_ready, 1)

            def make_rstd(n_, squared=False):
                act.wait_ge(stat_done, n_ + 1)
                src = MP[:, 0:2, 0:HALF]
                dst = rstd[:, :].rearrange("p (a n) -> p a n", a=2)
                step(act.activation(dst, src, ACT.Ln, bias=eps_col[:, :], scale=1.0 / D))
                settled()
                if squared:
                    act.activation(rstd[:, :], rstd[:, :], ACT.Exp, scale=-1.0).then_inc(rstd_ready, 1)
                else:
                    act.activation(rstd[:, :], rstd[:, :], ACT.Exp, scale=-0.5).then_inc(rstd_ready, 1)

            def attention(name, also=lambda i: None):
                u0, count = GROUP[name]

                def exps(u):
                    U = UNITS[u]
                    P, nk, s = U["P"], U["nk"], u % 2
                    act.wait_ge(nm_ready, u + 1)
                    for g in range(U["G"]):
                        at = slice(g * nk, (g + 1) * nk)
                        cross = U["kind"] == "cross"
                        inst = act.activation(probs_of(u, at), LP[0:P, 2 * s, at] if cross else probs_of(u, at),
                                              ACT.Exp, bias=nm[0:P, u % 3, g:g + 1], scale=U["scale"] if cross else 1.0,
                                              accum_out=rs[0:P, u % 3, g:g + 1])
                    if U["kind"] == "swa":
                        act.wait_ge(sink_ready, u - GROUP["swa"][0] + 1)
                        inst = act.activation(es[0:P, u % 3, :], es[0:P, u % 3, :], ACT.Exp)
                    inst.then_inc(ex_ready, 1)

                def scaled(u):
                    U = UNITS[u]
                    P, nk = U["P"], U["nk"]
                    act.wait_ge(rr_ready, u + 1)
                    b = probs_of(u, slice(nk, 2 * nk))
                    act.activation(b, b, ACT.Copy, scale=rr[0:P, u % 3, 1:2]).then_inc(second_ready, 1)

                def pt(u):
                    U = UNITS[u]
                    s, w = u % 2, U["P"] * U["G"]
                    act.wait_ge(tr_ready, u + 1)
                    if u >= 2:
                        act.wait_ge(o_ready, u - 1)
                    full = sum(n_ == 128 for n_, _ in U["v"])
                    inst = act.copy(U["PT"][:, s, 0:full * w], MP[:, s, 0:full * w])
                    if full < len(U["v"]):
                        rows = U["v"][-1][0]
                        inst = act.copy(U["PT"][0:rows, s, full * w:full * w + w], MP[0:rows, s, full * w:full * w + w])
                    inst.then_inc(pt_ready, 1)

                def high(u):
                    U = UNITS[u]
                    act.wait_ge(o_ready, u + 1)
                    act.copy(U["hi"], out_bank(U, u)).then_inc(oh_ready, 1)

                lag = 2 + extra_lag(name)
                for i in range(count + lag + 1):
                    if lag <= i < count + lag:
                        pt(u0 + i - lag)
                    if lag - 1 <= i < count + lag - 1 and name == "swa":
                        scaled(u0 + i - lag + 1)
                    if i < count:
                        exps(u0 + i)
                    if i > lag:
                        high(u0 + i - lag - 1)
                    also(i)

            act.preload_act_table_set("natural_log_exp_and_others")
            act.dma_start(stage[0][:, :].rearrange("p (k n) -> p k n", k=KT), loads_of("in_a")(0)
                          ).then_inc(w_loaded[0], 16)
            split(0, 16)
            act.wait_ge(param_ready, 1)
            for k in range(KT):
                square(0, k)
                high_part(0, k)
            split(1, 16)
            make_rstd(0)
            act.wait_ge(gate_in, 16 * 3)
            act.copy(wgh[:, :, :], w_gate[:, :, :]).then_inc(gate_act, 1)
            product("in_a")
            act.wait_ge(gate_pe, 2)
            act.copy(gates_raw[:, 0:TT, :].rearrange("p j c -> p (j c)"), MP[:, 2, 0:GATES * TT]).then_inc(gate_act, 1)
            act.copy(gates_raw[0:NS, TT, :], MP[0:NS, 2, GATES * TT:GATES * NTOK]).then_inc(gate_act, 1)
            act.wait_ge(gate_dve, 4)
            act.activation(gates[:, :, :], gates[:, :, :], ACT.Exp).then_inc(gate_act, 1)
            act.activation(gate_par[:, 0, :], gate_par[:, 0, :], ACT.Exp).then_inc(gate_act, 1)
            act.wait_ge(gate_act, 5)
            act.activation(gates[:, :, :], gates[:, :, :], ACT.Ln, bias=one_col[:, :]).then_inc(gate_act, 1)
            act.wait_ge(gate_dve, GATE_LOGF)
            act.activation(gates[:, :, 0:H], gates[:, :, 0:H], ACT.Exp, scale=-1.0).then_inc(gate_act, 1)
            act.wait_ge(gate_dve, GATE_LOGF)
            store(t["o_p_fox_logf"][0, 0].rearrange("(j p) h -> p j h", p=128), gates_raw[:, 0:TT, 2 * H:3 * H])
            store(t["o_s_fox_logf"][0, 0], gates_raw[0:NS, TT, 2 * H:3 * H])
            act.wait_ge(conv_dve, 2)
            act.preload_act_table_set("silu_and_others")
            act.activation(z[:, :, :], z[:, :, :], ACT.Silu).then_inc(conv_act, 2)
            for T in range(NCONV):
                if T % 2:
                    split_after("in_b", T)
                if T == 7:
                    for j, a, P in TOK:
                        row = k_out[:, j, :] if j < TT else k_out_s[:, :]
                        act.wait_ge(turn_pe, j + 1)
                        act.copy(row, MP[0:P, j % 4, :]).then_inc(turn_act, 1)
                    for j, a, P in TOK:
                        row = k_out[:, j, :] if j < TT else k_out_s[:, :]
                        act.wait_ge(turn_act, j + 1)
                        dst = t["o_p_fox_k"][0, 0, a:a + P] if j < TT else t["o_s_fox_k"][0, 0]
                        store(dst.rearrange("p h d -> p (h d)"), row)
                if T == 9:
                    for j, a, P in TOK:
                        act.wait_ge(turn_pe, NTOK + j + 1)
                        act.copy(vb_n[0:P, j, :], MP[0:P, (NTOK + j) % 4, :]).then_inc(turn_act, 1)
                act.wait_ge(conv_dve, 2 + CW * (T + 1))
                act.activation(ua[:, T, 0:N], sq[:, T % 2, :], ACT.Silu).then_inc(conv_act, 1)
                if T == 4:
                    act.wait_ge(conv_turned, 1)
                    act.copy(conv_newT[:, :], MP[0:2 * NCONV * PAD, 3, 0:128]).then_inc(conv_out, 1)
                    act.wait_ge(conv_out, 1)
                    R = NCONV * PAD
                    for s, o in ((0, "o_p_gdn_conv"), (1, "o_s_gdn_conv")):
                        store(t[o][0, 0].rearrange("i (f p) -> (i f) p", p=128), conv_newT[R * s:R * s + R, :])
            act.wait_ge(conv_act, 2 + NCONV)
            act.preload_act_table_set("natural_log_exp_and_others")
            def forget_rows(sample):
                for h in range(H):
                    act.wait_ge(rows_pe, (H if sample else 0) + h + 1)
                    b = 2 * (h % 2)
                    inst = act.activation(nF[:, h, 0:512], LP[:, b, 0:512], ACT.Copy, scale=-1.0)
                    if sample:
                        inst = act.activation(nF[:, h, 512:N], LP[:, b + 1, 0:NS], ACT.Copy, scale=-1.0)
                    inst.then_inc(rows_act, 1)

            act.wait_ge(stored, 16 * STORES[0])
            forget_rows(False)
            for c in range(PAST // 128):
                act.wait_ge(turn_pe, 2 * NTOK + c + 1)
                act.copy(kpT[:, :, 128 * c:128 * c + 128],
                         MP[:, (2 * NTOK + c) % 4, :].rearrange("p (h n) -> p h n", h=H)).then_inc(turn_act, 1)
            act.wait_ge(turn_act, 2 * NTOK)
            for j, a, P in TOK:
                dst = t["o_p_fox_v"][0, 0, a:a + P] if j < TT else t["o_s_fox_v"][0, 0]
                store(dst.rearrange("p h d -> p (h d)"), vb_n[0:P, j, :])

            def delta_rstds(i):
                f = (i - 3) // 2
                if i % 2 and 0 <= f < 2 * H:
                    act.wait_ge(head_sum, f + 1)
                    if f:
                        act.wait_ge(head_mul, f)
                    else:
                        act.wait_ge(drained, last_tile("in_b"))
                    act.activation(rstd[:, 0:HALF], LP[:, 1, 0:HALF], ACT.Ln, bias=eps_col[:, :])
                    act.activation(rstd[:, HALF:N], LP[:, 3, 0:HALF], ACT.Ln, bias=eps_col[:, :]
                                   ).then_inc(head_ln, 1)
                    act.wait_ge(head_ln, f + 1)
                    act.activation(rstd[:, :], rstd[:, :], ACT.Exp, scale=-0.5).then_inc(head_exp, 1)
                f = i // 2
                if i % 2 == 0 and f < 2 * H:
                    if f >= 2:
                        act.wait_ge(head_sum, f - 1)
                    act.activation(head_squares[:, f % 2, :], ua[:, f, 0:N], ACT.Square).then_inc(head_sq, 1)

            attention("fox_p", delta_rstds)
            act.wait_ge(ol_ready, sum(GROUP["fox_p"]))
            forget_rows(True)
            attention("fox_s")

            def head_square(f, src):
                if f >= 2 * H + 2:
                    act.wait_ge(head_sum, f - 1)
                act.activation(sq[:, f % 2, :], src, ACT.Square).then_inc(head_sq, 1)

            def head_rstd(f, scale):
                act.wait_ge(head_sum, f + 1)
                act.wait_ge(head_mul, max(f - 1, 2 * H))
                buf = (rstd, acc)[f % 2]
                act.activation(buf[:, :].rearrange("p (a n) -> p a n", a=2),
                               MP[:, 2 * (f % 2):2 * (f % 2) + 2, 0:HALF], ACT.Ln, bias=eps_col[:, :], scale=scale
                               ).then_inc(head_ln, 1)
                act.wait_ge(head_ln, f + 1)
                act.activation(buf[:, :], buf[:, :], ACT.Exp, scale=-0.5).then_inc(head_exp, 1)

            act.wait_ge(ol_ready, sum(GROUP["fox_s"]))
            act.wait_ge(stored, 16 * STORES[0])
            act.dma_start(S[:, 2, :, :], t["state_gdn"][0, 0].rearrange("h k v -> k h v")).then_inc(s_loaded, 16)

            def rows(j):
                _, a, P = TOK[j]
                nch, par = (2 if P == 128 else 1), j % 2
                act.wait_ge(row_pe, j + 1)
                act.activation(qe[:, par, :, 0:P], MP[:, 0, 0:H * P].rearrange("p (h n) -> p h n", h=H), ACT.Exp)
                act.activation(gsm[0:P, par, 0:4], MP[0:P, 3, 0:4], ACT.Copy, scale=-1.0)
                act.activation(gsm[0:P, par, 4:12], MP[0:P, 3, 0:8], ACT.Exp)
                act.activation(eg[:, par, 0:nch, :].rearrange("p c h -> p (c h)"), MP[:, 3, 8:8 + 4 * nch], ACT.Exp
                               ).then_inc(row_act, 1)

            def inverse(half, name, j):
                _, a, P = TOK[j]
                b0, b1, par, h0 = 2 * half, 2 * half + 1, j % 2, 2 * half
                hs = slice(h0, h0 + 2)
                if name[:5] == "delta":
                    return
                act.wait_ge(inv_pe[half], count_of(INV["pe"], name, j))

                def two_heads(bank, at, n_, rows_=P):
                    return LP[0:rows_, bank, at:at + 2 * n_].rearrange("p (h n) -> p h n", h=2)

                if name == "gram":
                    act.wait_ge(row_act, j + 1)
                    for i in range(2):
                        inst = act.activation(dec[0:P, h0 + i, 0:P], LP[0:P, b0, i * P:i * P + P], ACT.Exp,
                                              bias=gsm[0:P, par, h0 + i:h0 + i + 1])
                elif name == "turns":
                    act.copy(kn[0:P, hs, :], two_heads(b0, 0, 128))
                    for i in range(2):
                        act.activation(vbt[0:P, h0 + i, :], LP[0:P, b0, 256 + 128 * i:384 + 128 * i], ACT.Copy,
                                       scale=gates[0:P, j, h0 + i:h0 + i + 1])
                    inst = act.copy(Tm[0:P, hs, 0:P], two_heads(b1, 0, P))
                elif name[0] == "x":
                    inst = act.copy(Xm[0:P, hs, 0:P], two_heads(b0, 0, P))
                else:
                    act.copy(um[0:P, par, hs, :], two_heads(b0, 0, 128))
                    inst = act.copy(wT[:, par, hs, 0:P], two_heads(b0, 256, P, 128))
                inst.then_inc(inv_act[half], 1)

            def recurrence(name, j):
                _, a, P = TOK[j]
                if name == ("o1" if P == 128 else "o0"):
                    act.wait_ge(rec_pe, count_of(REC["pe"], name, j))
                    act.copy(o_a[:, :, a:a + P], MP[:, 2, 0:H * P].rearrange("p (h n) -> p h n", h=H)
                             ).then_inc(rec_act, 1)

            for j in range(NTOK + 1):
                for what in delta_order(j):
                    if what[0] == "rows":
                        rows(j)
                    elif what[0] == "rec":
                        recurrence(what[1], j - 1)
                    else:
                        inverse(*what, j)
            act.wait_ge(rec_dve, count_of(REC["dve"], "ds0", TT))
            store(t["o_p_gdn_state"][0, 0].rearrange("h k v -> k h v"), S[:, 0, :, :])
            store(t["o_s_gdn_state"][0, 0].rearrange("h k v -> k h v"), S[:, 1, :, :])
            act.wait_ge(rec_act, NTOK)
            act.wait_ge(stored, 16 * STORES[0])
            act.nop().then_inc(arena_free, 1)
            for h in range(H + 2):
                if h < H:
                    head_square(2 * H + h, o_a[:, h, :])
                if 1 <= h <= H:
                    head_rstd(2 * H + h - 1, 1.0 / HD)
                if h >= 2:
                    act.wait_ge(head_y, h - 1)
                    act.copy(xh[:, h - 2, :], o_a[:, h - 2, :]).then_inc(head_hi, 1)

            def layer_end(l):
                act.wait_ge(stored, 16 * STORES[0])
                for T in range(KT):
                    if T % 2:
                        split_after(f"out{l}", T)
                    square(3 * l + 1, T)
                    if T == 1:
                        act.wait_ge(mem_loaded, 16 * (l + 1))
                        for c in range(MEM // 128):
                            step(act.activation(m_squares[:, :], m_rows[:, c, :], ACT.Square,
                                                accum_out=mem_ss[:, c:c + 1]))
                            settled()
                        step(act.activation(mem_rs[:, :], mem_ss[:, :], ACT.Ln, bias=eps_col[:, :], scale=1.0 / D))
                        settled()
                        act.activation(mem_rs[:, :], mem_rs[:, :], ACT.Exp, scale=-0.5).then_inc(mem_act, 1)
                    for k in MEM_PARTS.get(T, ()):
                        act.wait_ge(mem_pe, l + 1)
                        if k >= 4:
                            act.wait_ge(mem_dve, (KT + 1) * l + k - 2)
                        at = MEM * (k // 4)
                        act.activation(mh[:, k, :], MP[:, k % 4, at:at + MEM], ACT.Copy, scale=gain(7 + l, k)
                                       ).then_inc(mem_act, 1)
                for T in range(KT):
                    if T % 2:
                        split_after(f"mem{l}", T)
                    high_part(3 * l + 1, T)
                    if T == 5:
                        act.wait_ge(cross_turned, 2 * l + 1)
                        act.copy(kxT[:, :, :].rearrange("p (b h) n -> p b (h n)", b=2), MP[:, 0:2, :]
                                 ).then_inc(cross_copied, 1)
                act.wait_ge(cross_turned, 2 * l + 2)
                for c in range(MEM // 128):
                    step(act.copy(kv_n[:, c, :].rearrange("p (b n) -> p b n", b=2), MP[:, 2 * c:2 * c + 2, :]))
                settled()
                act.nop().then_inc(cross_copied, 1)
                for i, o in ((0, "o_p_mem_k"), (1, "o_p_mem_v")):
                    store(t[o][l, 0].rearrange("(c p) h d -> p c (h d)", p=128), kv_n[:, :, 512 * i:512 * i + 512])
                make_rstd(3 * l + 1)
                product(f"xq{l}")
                attention(f"cross{l}")
                for T in range(KT):
                    if T == 3:
                        split_after(f"xo{l}", T)
                    square(3 * l + 2, T)
                    if T >= KT - 4:
                        high_part(3 * l + 2, T)
                for k in range(4):
                    high_part(3 * l + 2, k)
                split_after(f"xo{l}", KT - 1)
                mlp(l)

            def mlp_block(l, b, last):
                p0, t0, _, _ = LIN[f"mlp{l}"]
                for i in range(4):
                    for m in range(2):
                        k = 2 * i + m
                        T = t0 + 16 * b + k
                        hcount = KT * NB * l + KT * b + k
                        act.wait_ge(product_done, T + 1)
                        if not (isinstance(hcount, int) and hcount < 2):
                            act.wait_ge(hsq_ready, hcount - 1)
                            act.wait_ge(hh_ready, hcount - 1)
                        act.activation(rel[:, k % 2, :].rearrange("p (a n) -> p a n", a=2),
                                       LP[:, 2 * (k % 2):2 * (k % 2) + 2, 0:HALF], ACT.Relu).then_inc(relu_ready, 1)
                        act.wait_ge(relu_ready, hcount + 1)
                        act.activation(hh[:, k, :], rel[:, k % 2, :], ACT.Square).then_inc(hh_ready, 1)
                    split(i % 2, 16 * ((p0 + i) // 2 + 2) + 64 * b)
                for i in range(4):
                    if last:
                        square(3 * l + 3, 2 * i)
                        next_input(l, 2 * i)
                    if last and i == 3:
                        square(3 * l + 3, 2 * i + 1)
                        next_input(l, 2 * i + 1)
                    act.wait_ge(product_done, t0 + 16 * b + 8 + 2 * (i + 1))
                    if not (last and l == 1 and i >= 2):
                        split(i % 2, 16 * ((p0 + 4 + i) // 2 + 2) + 64 * b)
                    if last and i < 3:
                        square(3 * l + 3, 2 * i + 1)
                        next_input(l, 2 * i + 1)

            def next_input(l, k):
                if l == 0:
                    high_part(3, k)

            def mlp(l):
                act.wait_ge(stored, 16 * STORES[0])
                p0, t0, _, _ = LIN[f"mlp{l}"]
                make_rstd(3 * l + 2, squared=True)
                mlp_block(l, 0, False)
                with act.Fori(1, NB - 1) as b:
                    mlp_block(l, b, False)
                mlp_block(l, NB - 1, True)

            layer_end(0)
            make_rstd(3)
            product("in_c")
            act.wait_ge(swa_turned, 1)
            act.copy(kcT[:, :, :].rearrange("p c n -> p (c n)"), LP[:, 0, 0:256]).then_inc(swa_copied, 1)
            for j, a, P in TOK:
                act.wait_ge(swa_turned, 1 + j + 1)
                if j >= TT - 1:
                    step(act.copy(kc_out[0:P, j % 2, :], MP[0:P, 2 * (j % 2), 0:256]))
                act.copy(v_cn[0:P, j, :], MP[0:P, 2 * (j % 2) + 1, 0:256]).then_inc(swa_copied, 1)
                if j >= TT - 1:
                    act.wait_ge(swa_copied, 1 + j + 1)
                    for nm_, src in (("k", kc_out[0:P, j % 2, :]), ("v", v_cn[0:P, j, :])):
                        dst = t[f"o_{'p' if j < TT else 's'}_swa_{nm_}"][0, 0]
                        store(dst.rearrange("p h d -> p (h d)"), src)
            attention("swa")
            layer_end(1)
            act.wait_ge(stat_done, 7)
            for P, part in ((128, slice(0, TT)), (NS, slice(TT, NTOK))):
                step(act.activation(token_rstd[0:P, part], MP[0:P, 0, part], ACT.Ln, bias=eps_col[0:P, :],
                                    scale=1.0 / D))
            settled()
            for P, part in ((128, slice(0, TT)), (NS, slice(TT, NTOK))):
                inst = act.activation(token_rstd[0:P, part], token_rstd[0:P, part], ACT.Exp, scale=-0.5)
            inst.then_inc(rstd_ready, 1)
            act.wait_ge(rstd_ready, 7)
            for j, a, P in TOK:
                act.wait_ge(y_turned, j + 1)
                act.activation(y_rows[0:P, j, 0:512], LP[0:P, 2 * (j % 2), :], ACT.Copy,
                               scale=token_rstd[0:P, j:j + 1]).then_inc(y_left, 1)
            assert STORES[0] == STORES_TOTAL, STORES[0]

        @block.vector
        def _(dve):
            n = [0]

            def step(inst):
                inst.then_inc(dve_step, 1)
                n[0] += 1
                return n[0]

            def after(count):
                dve.wait_ge(dve_step, count)

            def settled():
                after(n[0])

            def accumulate(n_, k):
                dve.wait_ge(sq_ready, KT * n_ + k + 1)
                if k:
                    dve.wait_ge(sq_used, KT * n_ + k)
                    dve.tensor_tensor(acc[:, :], acc[:, :], sq[:, k % 2, :], ALU.add).then_inc(sq_used, 1)
                else:
                    dve.tensor_copy(acc[:, :], sq[:, 0, :]).then_inc(sq_used, 1)

            def low_part(n_, i, k):
                dve.wait_ge(xh_ready, KT * n_ + i + 1)
                dve.scalar_tensor_tensor(out=xl[:, k, :], in0=x[:, k, :], scalar=gain(n_, k),
                                         in1=xh[:, k, :].bitcast(f32), op0=ALU.mult, op1=ALU.subtract
                                         ).then_inc(xs_ready, 1)

            def banks(T):
                s = T % 2
                return LP[:, 2 * s:2 * s + 2, 0:HALF]

            def two(v):
                return v.rearrange("p (a n) -> p a n", a=2)

            def residual_tile(name, k):
                t0 = LIN[name][1]
                dve.wait_ge(product_done, t0 + k + 1)
                dve.tensor_tensor(two(x[:, k, :]), banks(k), two(x[:, k, :]), ALU.add).then_inc(x_done, 1)
                dve.wait_ge(x_done, NORM_BASE[RES[name]] + k + 1)
                dve.nop().then_inc(drained, 1)

            def attention(name, also=lambda i: None):
                u0, count = GROUP[name]

                def scored(u):
                    U = UNITS[u]
                    P, nk, s, G_, kind = U["P"], U["nk"], u % 2, U["G"], U["kind"]
                    buf = probs_of(u, slice(0, G_ * nk))
                    rows = buf.rearrange("p (g n) -> p g n", g=G_)
                    dve.wait_ge(sc_ready, u + 1)
                    if u >= 4:
                        dve.wait_ge(tr_ready, u - 2 - extra_lag(U["kind"]))
                    elif u == 3:
                        dve.wait_ge(tr_ready, 1)
                    if kind == "cross":
                        bank = LP[0:P, 2 * s, 0:G_ * nk].rearrange("p (g n) -> p g n", g=G_)
                        c = step(dve.tensor_reduce(nm[0:P, u % 3, :], bank, AX.X, ALU.max, negate=True))
                        yield
                        after(c)
                        dve.tensor_scalar(nm[0:P, u % 3, :], nm[0:P, u % 3, :], U["scale"], None, ALU.mult
                                          ).then_inc(nm_ready, 1)
                        yield
                        return
                    if kind == "fox":
                        for lo_, hi_, b in [(0, min(nk, 512), 2 * s)] + ([(512, nk, 2 * s + 1)] if nk > 512 else []):
                            c = step(dve.scalar_tensor_tensor(
                                out=buf[:, lo_:hi_], in0=LP[0:P, b, 0:hi_ - lo_], scalar=U["scale"],
                                in1=nF[0:P, U["h"], lo_:hi_], op0=ALU.mult, op1=ALU.add))
                        yield
                        after(c)
                        c = step(dve.tensor_tensor(buf[:, nk - P:nk], buf[:, nk - P:nk], diag_mask[0:P, 0:P], ALU.add))
                        yield
                        after(c)
                        dve.tensor_reduce(nm[0:P, u % 3, 0:1], buf, AX.X, ALU.max, negate=True).then_inc(nm_ready, 1)
                        return
                    for g in range(G_):
                        slope = 2.0 ** (-8.0 * (U["h"] + 2 * g + 1) / HQ)
                        c = step(dve.scalar_tensor_tensor(out=buf[:, g * nk:(g + 1) * nk], in0=U["dist"],
                                                          scalar=-slope, in1=LP[0:P, 2 * s, g * nk:(g + 1) * nk],
                                                          op0=ALU.mult, op1=ALU.add))
                    yield
                    after(c)
                    c = step(dve.tensor_reduce(nm[0:P, u % 3, :], rows, AX.X, ALU.max, negate=True))
                    yield
                    after(c)
                    pair_ = slice(U["h"], U["h"] + 3, 2)
                    dve.tensor_tensor(nm[0:P, u % 3, :], nm[0:P, u % 3, :], neg_sinks[0:P, pair_], ALU.min
                                      ).then_inc(nm_ready, 1)
                    yield
                    dve.wait_ge(nm_ready, u + 1)
                    dve.tensor_tensor(es[0:P, u % 3, :], nm[0:P, u % 3, :], sinks[0:P, pair_], ALU.add
                                      ).then_inc(sink_ready, 1)

                def normed(u):
                    U = UNITS[u]
                    P, nk, s, G_ = U["P"], U["nk"], u % 2, U["G"]
                    dve.wait_ge(ex_ready, u + 1)
                    if U["kind"] == "swa":
                        c = step(dve.tensor_tensor(rs[0:P, u % 3, :], rs[0:P, u % 3, :], es[0:P, u % 3, :], ALU.add))
                        yield
                        after(c)
                    dve.reciprocal(rr[0:P, u % 3, 0:G_], rs[0:P, u % 3, 0:G_]).then_inc(rr_ready, 1)
                    yield
                    dve.wait_ge(rr_ready, u + 1)
                    for g in range(1 if U["kind"] == "swa" else G_):
                        b = probs_of(u, slice(g * nk, (g + 1) * nk))
                        inst = dve.tensor_scalar(b, b, rr[0:P, u % 3, g:g + 1], None, ALU.mult)
                    inst.then_inc(p_ready, 1)

                def low(u):
                    U = UNITS[u]
                    dve.wait_ge(oh_ready, u + 1)
                    dve.tensor_tensor(U["lo"], out_bank(U, u), U["hi"].bitcast(f32), ALU.subtract
                                      ).then_inc(ol_ready, 1)

                lag = 2 + extra_lag(name)
                for i in range(count + lag + 2):
                    turns = ([scored(u0 + i)] if i < count else []) + (
                        [normed(u0 + i - lag + 1)] if lag - 1 <= i < count + lag - 1 else [])
                    while turns:
                        turns = [g for g in turns if next(g, "end") != "end"]
                    if i > lag + 1:
                        low(u0 + i - lag - 2)
                    also(i)

            step(dve.memset(one_col[:, :], 1.0))
            dve.wait_ge(param_turned, 1)
            dve.tensor_copy(cols[:, :], MP[:, 3, 256:256 + NROW]).then_inc(param_ready, 1)
            dve.tensor_copy(x[:, :, NPT:N], MP[:, 3, 0:NS * KT].rearrange("p (k n) -> p k n", k=KT))
            dve.wait_ge(param_ready, 1)
            for k in range(KT + 1):
                if k < KT:
                    dve.wait_ge(x_turned, k + 1)
                    dve.tensor_copy(x[:, k, 0:NPT], MP[:, k % 3, :]).then_inc(x_done, 1)
                if k:
                    dve.wait_ge(x_done, k)
                    low_part(0, k - 1, k - 1)
                    accumulate(0, k - 1)
            step(dve.memset(ua[:, :, 0:PAD], 0.0))
            dve.tensor_copy(ua[:, :, PAD + NPT:PAD + NPT + PAD].rearrange("p f i -> p i f"),
                            MP[:, 3, 384:384 + PAD * NCONV].rearrange("p (i f) -> p i f", i=PAD)
                            ).then_inc(param_ready, 1)
            dve.wait_ge(gate_act, 1)
            dve.tensor_tensor(wgl[:, :, :], w_gate[:, :, :], wgh[:, :, :].bitcast(f32), ALU.subtract
                              ).then_inc(gate_dve, 1)
            dve.wait_ge(rstd_ready, 1)
            ta = LIN["in_a"][1]

            def four_conv_rows(i):
                for m in range(4):
                    dve.wait_ge(product_done, ta + 4 * i + m + 1)
                    b = 2 * (m % 2)
                    row = ua[:, bass.ds(4 * i + m, 1), :].rearrange("p o n -> p (o n)")
                    dve.tensor_tensor(row[:, PAD:PAD + HALF], LP[:, b, 0:HALF], rstd[:, 0:HALF], ALU.mult)
                    dve.tensor_tensor(row[:, PAD + HALF:PAD + NPT], LP[:, b + 1, 0:NPT - HALF], rstd[:, HALF:NPT],
                                      ALU.mult)
                    dve.tensor_tensor(row[:, 2 * PAD + NPT:UPAD], LP[:, b + 1, NPT - HALF:HALF], rstd[:, NPT:N],
                                      ALU.mult).then_inc(drained, 1)
            four_conv_rows(0)
            dve.wait_ge(gate_pe, 1)
            dve.tensor_tensor(two(gT[:, :]), MP[0:GATES, 0:2, 0:HALF], two(rstd[0:GATES, :]), ALU.mult
                              ).then_inc(gate_dve, 1)
            with dve.Fori(1, NCONV // 4) as i:
                four_conv_rows(i)
            for m in range(H):
                dve.wait_ge(product_done, ta + NCONV + m + 1)
                dve.tensor_tensor(two(z[:, m, :]), banks(m), two(rstd[:, :]), ALU.mult).then_inc(drained, 1)
            dve.wait_ge(mask_done, MASKS)
            dve.wait_ge(par_loaded, 16 * 16)
            step(dve.tensor_scalar(neg_sinks[:, :], sinks[:, :], -1.0, None, ALU.mult))
            for m, w in ((dist_p, 256), (dist_s, WIN + NS)):
                P = m.shape[0]
                step(dve.tensor_scalar(sq[0:P, 0, 0:w], m[:, :], -1.0, None, ALU.mult))
                settled()
                step(dve.tensor_tensor(m[:, :], m[:, :], sq[0:P, 0, 0:w], ALU.max))
                settled()
            dve.wait_ge(gate_act, 3)

            def bc(i):
                return gate_par[:, i:i + 1, :].to_broadcast([128, NTOK, H])

            step(dve.tensor_tensor(gates_raw[:, :, H:2 * H], gates_raw[:, :, H:2 * H], bc(1), ALU.add))
            step(dve.tensor_tensor(gates_raw[:, :, 2 * H:3 * H], gates_raw[:, :, 2 * H:3 * H], bc(2), ALU.add))
            settled()
            step(dve.tensor_scalar(gates_raw[:, :, 0:H], gates_raw[:, :, 0:H], -1.0, None, ALU.mult))
            step(dve.tensor_scalar(gates_raw[:, :, 2 * H:3 * H], gates_raw[:, :, 2 * H:3 * H], -1.0, None, ALU.mult))
            settled()
            dve.tensor_scalar(gate_tmp[:, :, :], gates_raw[:, :, :], -1.0, None, ALU.mult).then_inc(gate_dve, 1)
            dve.wait_ge(gate_dve, 3)
            dve.tensor_tensor(gates[:, :, :], gates_raw[:, :, :], gate_tmp[:, :, :], ALU.min).then_inc(gate_dve, 1)
            step(dve.tensor_scalar(gates_raw[:, :, :], gates_raw[:, :, :], 0.0, None, ALU.max))
            settled()
            dve.wait_ge(gate_act, 6)
            step(dve.tensor_tensor(gate_tmp[:, :, :], gates_raw[:, :, :], gates[:, :, :], ALU.add))
            settled()
            step(dve.tensor_scalar(gates_raw[:, :, 2 * H:3 * H], gate_tmp[:, :, 2 * H:3 * H], -1.0, None, ALU.mult))
            step(dve.tensor_tensor(gates[:, :, H:2 * H], gate_tmp[:, :, H:2 * H], bc(0), ALU.mult))
            settled()
            step(dve.tensor_scalar(gates[:, :, H:2 * H], gates[:, :, H:2 * H], -1.0, None, ALU.mult))
            dve.tensor_copy(gates[:, :, 0:H], gate_tmp[:, :, 0:H]).then_inc(gate_dve, 2)
            dve.tensor_copy(conv_new[:, 0, :, :], ua[:, :, NPT:NPT + PAD].rearrange("p f i -> p i f"))
            dve.tensor_copy(conv_new[:, 1, :, :], ua[:, :, UPAD - PAD:UPAD].rearrange("p f i -> p i f")
                            ).then_inc(conv_dve, 2)
            tb = LIN["in_b"][1]
            for f in range(NCONV):
                dve.wait_ge(product_done, tb + f + 1)
                dve.tensor_tensor(two((kb_f, vb_f, qb_f)[f // H][:, f % H, :]), banks(f), two(rstd[:, :]), ALU.mult
                                  ).then_inc(drained, 1)
                if f >= 2:
                    dve.wait_ge(conv_act, 2 + f - 1)
                b, e = sq[:, f % 2, 0:NPT], sq[:, f % 2, NPT:N]
                for i in range(CW):
                    if i == 0:
                        dve.tensor_scalar(b, ua[:, f, 0:NPT], conv_w(0, f), None, ALU.mult)
                        inst = dve.tensor_scalar(e, ua[:, f, PAD + NPT:PAD + NPT + NS], conv_w(0, f), None, ALU.mult)
                    else:
                        dve.wait_ge(conv_dve, 2 + CW * f + i)
                        dve.scalar_tensor_tensor(out=b, in0=ua[:, f, i:i + NPT], scalar=conv_w(i, f), in1=b,
                                                 op0=ALU.mult, op1=ALU.add)
                        inst = dve.scalar_tensor_tensor(out=e, in0=ua[:, f, PAD + NPT + i:PAD + NPT + i + NS],
                                                        scalar=conv_w(i, f), in1=e, op0=ALU.mult, op1=ALU.add)
                    inst.then_inc(conv_dve, 1)

            def delta_scales(i):
                f = (i - 4) // 2
                if i % 2 == 0 and 0 <= f < 2 * H:
                    dve.wait_ge(head_exp, f + 1)
                    dve.scalar_tensor_tensor(out=ua[:, f, 0:N], in0=ua[:, f, 0:N], in1=rstd[:, :],
                                             scalar=HD ** -0.5 if f < H else 1.0, op0=ALU.mult, op1=ALU.mult
                                             ).then_inc(head_mul, 1)

            attention("fox_p", delta_scales)
            attention("fox_s")
            dve.wait_ge(gate_act, 7)
            dve.memset(S[:, 0, :, :], 0.0).then_inc(s_zero, 1)

            def rows(j):
                _, a, P = TOK[j]
                par = j % 2
                dve.wait_ge(row_act, j + 1)
                dve.tensor_tensor(gsm[0:P, par, 12:16], gates[0:P, j, 0:H], gsm[0:P, par, 4:8], ALU.mult)
                dve.tensor_tensor(qe[:, par, :, 0:P], qe[:, par, :, 0:P], ua[:, 0:H, a:a + P], ALU.mult
                                  ).then_inc(row_dve, 1)

            def inverse(half, name, j):
                _, a, P = TOK[j]
                b0, b1, par, h0 = 2 * half, 2 * half + 1, j % 2, 2 * half
                hs = slice(h0, h0 + 2)

                def two_heads(bank, at):
                    return LP[0:P, bank, at:at + 2 * P].rearrange("p (h n) -> p h n", h=2)

                def over(m):
                    return m.rearrange("p (o n) -> p o n", o=1).to_broadcast([P, 2, P])

                def done(inst):
                    inst.then_inc(inv_dve[half], 1)

                def mask(s):
                    return dve.tensor_tensor(BT[0:P, hs, 0:P], LT[0:P, hs, 0:P],
                                             over(level[0:P, LEVELS.index(s), 0:P]), ALU.mult)

                if name == "gram":
                    dve.wait_ge(inv_act[half], count_of(INV["act"], "gram", j))
                    c = step(dve.tensor_tensor(LT[0:P, hs, 0:P], two_heads(b1, 0), dec[0:P, hs, 0:P], ALU.mult))
                    d_ = step(dve.tensor_tensor(AT[0:P, par, hs, 0:P], two_heads(b1, 2 * P), dec[0:P, hs, 0:P],
                                                ALU.mult))
                    after(c)
                    c = step(dve.tensor_tensor(LT[0:P, hs, 0:P], LT[0:P, hs, 0:P], two_heads(b0, 2 * P), ALU.mult))
                    after(c)
                    c = step(mask(1))
                    after(c)
                    done(dve.tensor_tensor(TmT[0:P, hs, 0:P], over(ident[0:P, 0:P]), BT[0:P, hs, 0:P], ALU.subtract))
                elif name == "turns":
                    dve.wait_ge(inv_dve[half], count_of(INV["dve"], "gram", j))
                    done(mask(2))
                    dve.wait_ge(row_dve, j + 1)
                    dve.wait_ge(inv_act[half], count_of(INV["act"], "turns", j))
                    for i in range(2):
                        dve.tensor_scalar(kbe[0:P, h0 + i, :], kn[0:P, h0 + i, :], gsm[0:P, par, 12 + h0 + i:13 + h0 + i],
                                          None, ALU.mult)
                        inst = dve.tensor_scalar(kd[0:P, par, h0 + i, :], kn[0:P, h0 + i, :],
                                                 gsm[0:P, par, 8 + h0 + i:9 + h0 + i], None, ALU.mult)
                    done(inst)
                elif name[:5] == "delta":
                    s = int(name[5:])
                    dve.wait_ge(inv_pe[half], count_of(INV["pe"], name, j))
                    dve.wait_ge(inv_dve[half], count_of(INV["dve"], "turns" if s == 2 else f"delta{s // 2}", j))
                    if s < SIZES[-1]:
                        dve.tensor_tensor(Tm[0:P, hs, 0:P], Tm[0:P, hs, 0:P], two_heads(b1, 0), ALU.subtract)
                        done(mask(2 * s))
                    done(dve.tensor_tensor(TmT[0:P, hs, 0:P], TmT[0:P, hs, 0:P], two_heads(b1, 2 * P), ALU.subtract))

            def recurrence(name, j):
                _, a, P = TOK[j]
                c, par = int(name[-1]), j % 2
                C = 64 if P == 128 else P
                r = slice(c * C, c * C + C)
                old, new = (2, 1) if j == TT else (c, 1 - c)
                if name[0] == "o":
                    return
                dve.wait_ge(rec_pe, count_of(REC["pe"], name, j))
                if name[:2] == "ws":
                    inst = dve.tensor_tensor(vnew[r, :, :], um[r, par, :, :],
                                             MP[r, 1, :].rearrange("p (h n) -> p h n", h=H), ALU.subtract)
                else:
                    if j or c:
                        dve.wait_ge(rec_dve, count_of(REC["dve"], f"ws{c}", j))
                    for h in range(H):
                        inst = dve.scalar_tensor_tensor(out=S[:, new, h, :], in0=S[:, old, h, :],
                                                        scalar=eg[:, par, c, h:h + 1],
                                                        in1=MP[:, 1, 128 * h:128 * h + 128], op0=ALU.mult, op1=ALU.add)
                inst.then_inc(rec_dve, 1)

            for j in range(NTOK + 1):
                if j == NTOK:
                    dve.wait_ge(s_loaded, 16)
                for what in delta_order(j):
                    if what[0] == "rows":
                        rows(j)
                    elif what[0] == "rec":
                        recurrence(what[1], j - 1)
                    else:
                        inverse(*what, j)
            for h in range(H + 1):
                if h < H:
                    f = 2 * H + h
                    dve.wait_ge(head_exp, f + 1)
                    dve.scalar_tensor_tensor(out=o_a[:, h, :], in0=o_a[:, h, :], scalar=column(ONORM),
                                             in1=(rstd, acc)[f % 2][:, :], op0=ALU.mult, op1=ALU.mult
                                             ).then_inc(head_mul, 1)
                    dve.wait_ge(head_mul, f + 1)
                    dve.tensor_tensor(o_a[:, h, :], o_a[:, h, :], z[:, h, :], ALU.mult).then_inc(head_y, 1)
                if h:
                    dve.wait_ge(head_hi, h)
                    dve.tensor_tensor(xl[:, h - 1, :], o_a[:, h - 1, :], xh[:, h - 1, :].bitcast(f32), ALU.subtract
                                      ).then_inc(low_done, 1)

            def layer_end(l):
                for T in range(KT):
                    if T:
                        accumulate(3 * l + 1, T - 1)
                    residual_tile(f"out{l}", T)
                    if T == 2:
                        dve.wait_ge(mem_act, (KT + 1) * l + 1)
                        for c in range(MEM // 128):
                            inst = dve.tensor_scalar(m_rows[:, c, :], m_rows[:, c, :], mem_rs[:, c:c + 1], None,
                                                     ALU.mult)
                        inst.then_inc(mem_dve, 1)
                    for k in MEM_PARTS.get(T, ()):
                        dve.wait_ge(mem_act, (KT + 1) * l + k + 2)
                        at = MEM * (k // 4)
                        dve.scalar_tensor_tensor(out=ml[:, k, :], in0=MP[:, k % 4, at:at + MEM],
                                                 scalar=gain(7 + l, k), in1=mh[:, k, :].bitcast(f32),
                                                 op0=ALU.mult, op1=ALU.subtract).then_inc(mem_dve, 1)
                accumulate(3 * l + 1, KT - 1)
                t0 = LIN[f"mem{l}"][1]
                for T in range(KT):
                    dve.wait_ge(product_done, t0 + T + 1)
                    dve.tensor_copy(kvT[:, T, :], LP[:, 2 * (T % 2), 0:MEM]).then_inc(drained, 1)
                    low_part(3 * l + 1, T, T)
                dve.wait_ge(rstd_ready, 3 * l + 2)
                t0 = LIN[f"xq{l}"][1]
                for m in range(H):
                    dve.wait_ge(product_done, t0 + m + 1)
                    dve.tensor_tensor(two(q_x[:, m, :]), banks(m), two(rstd[:, :]), ALU.mult).then_inc(drained, 1)
                attention(f"cross{l}")
                for T in range(KT):
                    if T:
                        accumulate(3 * l + 2, T - 1)
                    if T > KT - 4:
                        low_part(3 * l + 2, T - 5, T - 1)
                    residual_tile(f"xo{l}", T)
                low_part(3 * l + 2, 3, KT - 1)
                accumulate(3 * l + 2, KT - 1)
                for k in range(4):
                    low_part(3 * l + 2, 4 + k, k)
                mlp(l)

            def mlp_block(l, b, last=False):
                t0, d0 = LIN[f"mlp{l}"][1], DRAINED[f"mlp{l}"]
                for k in range(KT):
                    hcount = KT * NB * l + KT * b + k
                    dve.wait_ge(relu_ready, hcount + 1)
                    if not (isinstance(hcount, int) and hcount < 2):
                        dve.wait_ge(h_ready, hcount - 1)
                    dve.tensor_tensor(hsq[:, k % 2, :], rel[:, k % 2, :], rel[:, k % 2, :], ALU.mult
                                      ).then_inc(hsq_ready, 1)
                    dve.wait_ge(hsq_ready, hcount + 1)
                    dve.wait_ge(hh_ready, hcount + 1)
                    dve.tensor_tensor(hl[:, k, :], hsq[:, k % 2, :], hh[:, k, :].bitcast(f32), ALU.subtract
                                      ).then_inc(h_ready, 1)
                base = NORM_BASE[3 * l + 2]
                for k in range(KT):
                    if last and k:
                        next_norm(l, k - 1)
                    dve.wait_ge(product_done, t0 + 16 * b + KT + k + 1)
                    count = KT * NB * l + KT * b + k
                    if not (isinstance(count, int) and count < 2):
                        dve.wait_ge(x_done, base + KT + KT * b + k - 1)
                    dve.tensor_tensor(two(dtmp[:, k % 2, :]), banks(k), two(rstd[:, :]), ALU.mult
                                      ).then_inc(drained, 1)
                    dve.wait_ge(drained, d0 + KT * b + k + 1)
                    dve.tensor_tensor(x[:, k, :], x[:, k, :], dtmp[:, k % 2, :], ALU.add).then_inc(x_done, 1)
                if last:
                    next_norm(l, KT - 1)

            def next_norm(l, k):
                if l == 0:
                    low_part(3, k, k)
                else:
                    dve.wait_ge(x_done, NORM_BASE[6] + k + 1)
                    dve.tensor_scalar(yT[:, k, :], x[:, k, :], gain(6, k), None, ALU.mult).then_inc(y_scaled, 1)
                accumulate(3 * l + 3, k)

            def mlp(l):
                dve.wait_ge(rstd_ready, 3 * l + 3)
                mlp_block(l, 0)
                with dve.Fori(1, NB - 1) as b:
                    mlp_block(l, b)
                mlp_block(l, NB - 1, True)

            layer_end(0)
            dve.wait_ge(rstd_ready, 4)
            tc = LIN["in_c"][1]
            for m in range(12):
                dve.wait_ge(product_done, tc + m + 1)
                if m >= 8:
                    dst = (k_c, v_c)[(m - 8) // 2][:, m % 2, :]
                    dve.tensor_tensor(two(dst), banks(m), two(rstd[:, :]), ALU.mult).then_inc(drained, 1)
                    continue
                kv = m // 2
                o = (kv % 2) * 64
                for h in (2 * m, 2 * m + 1):
                    slot, ho = (h // 8) * 4 + h % 4, (h % 2) * 64
                    inst = dve.scalar_tensor_tensor(
                        out=two(q_c[o:o + 64, slot, :]), in0=LP[ho:ho + 64, 2 * (m % 2):2 * (m % 2) + 2, 0:HALF],
                        scalar=HDC ** -0.5, in1=two(rstd[ho:ho + 64, :]), op0=ALU.mult, op1=ALU.mult)
                inst.then_inc(drained, 1)
            attention("swa")
            layer_end(1)
            dve.wait_ge(rstd_ready, 7)
            for j, a, P in TOK:
                dve.wait_ge(y_turned, j + 1)
                dve.tensor_scalar(y_rows[0:P, j, 512:D], LP[0:P, 2 * (j % 2) + 1, :], token_rstd[0:P, j:j + 1],
                                  None, ALU.mult).then_inc(y_right, 1)



def kernel(**inputs):
    import numpy as _np
    import concourse.bacc as _bacc
    from concourse import mybir as _mybir
    from concourse.bass_utils import run_bass_kernel_spmd as _run

    nc = _bacc.Bacc("TRN2", target_bir_lowering=False, num_devices=1)
    arrays, t = {}, {}
    for name, value in inputs.items():
        a = _np.ascontiguousarray(value)
        arrays[f"in_{name}"] = a
        t[name] = nc.dram_tensor(f"in_{name}", a.shape, _mybir.dt.from_np(a.dtype), kind="ExternalInput").ap()
    s = {k: tuple(v.shape) for k, v in inputs.items()}
    _, np_, d = s["x_prompt"]
    ns = s["x_sample"][1]
    _, _, h, dk, dv = s["state_gdn"]
    cw, cdim = s["state_gdn_conv"][2:]
    win, hkv, hdc = s["cache_swa_k"][2:]
    depth, _, mem, hx, hdx = s["cache_mem_k"]
    outs = [("y_prompt", (1, np_, d)), ("y_sample", (1, ns, d)),
            ("p_gdn_state", (1, 1, h, dk, dv)), ("p_gdn_conv", (1, 1, cw, cdim)),
            ("p_fox_k", (1, 1, np_, h, dk)), ("p_fox_v", (1, 1, np_, h, dk)), ("p_fox_logf", (1, 1, np_, h)),
            ("p_swa_k", (1, 1, win, hkv, hdc)), ("p_swa_v", (1, 1, win, hkv, hdc)),
            ("p_mem_k", (depth, 1, mem, hx, hdx)), ("p_mem_v", (depth, 1, mem, hx, hdx)),
            ("s_gdn_state", (1, 1, h, dk, dv)), ("s_gdn_conv", (1, 1, cw, cdim)),
            ("s_fox_k", (1, 1, ns, h, dk)), ("s_fox_v", (1, 1, ns, h, dk)), ("s_fox_logf", (1, 1, ns, h)),
            ("s_swa_k", (1, 1, ns, hkv, hdc)), ("s_swa_v", (1, 1, ns, hkv, hdc))]
    for name, shape in outs:
        t[f"o_{name}"] = nc.dram_tensor(f"o_{name}", shape, _mybir.dt.float32, kind="ExternalOutput").ap()
    build_program(nc, t)
    r = _run(nc, [arrays], core_ids=[0])
    return tuple(r.results[0][f"o_{name}"] for name, _ in outs)
```
